# Optimizing a Trainium2 kernel written in Bass

```python
import jax, jax.numpy as jnp
from jax import lax
import numpy as np
import math

D_MODEL = 1024
BATCH = 1
SEQ = 512
DEPTH = 2

HEAD_DIM = 64
NSA_HEADS = 8
NSA_KV_GROUPS = 2
NSA_HPG = NSA_HEADS // NSA_KV_GROUPS
CMP_LEN = 32
CMP_STRIDE = 16
CMP_HIDDEN = 256
SEL_BLOCK = 64
SEL_TOPK = 16
WINDOW = 512
NSA_QBLOCK = 64
FORCE_BONUS = 1e4
GLA_HEADS = 4
GLA_DK = 32
GLA_DV = 64
GLA_RANK = 16
GLA_TAU = 16.0
GLA_CHUNK = 64
SG_GROUPS = 4
SG_CH = 64
SG_CHUNK = 128
NSA_W = NSA_HEADS * HEAD_DIM
GLA_W = GLA_HEADS * GLA_DV
SG_W = SG_GROUPS * SG_CH
D_MIX = NSA_W + GLA_W + SG_W
KV_W = NSA_KV_GROUPS * HEAD_DIM
IN_SIZES = (NSA_W, KV_W, KV_W, KV_W, KV_W, KV_W, KV_W, NSA_HEADS * 3,
            GLA_HEADS * GLA_DK, GLA_HEADS * GLA_DK, GLA_W, GLA_RANK, GLA_W, 2 * SG_W)
D_IN = sum(IN_SIZES)
D_FF = -(-8 * D_MODEL // (3 * 256)) * 256
ROPE_THETA = 10000.0
NORM_EPS = 1e-6


def rmsnorm(x, g):
    xf = x.astype(jnp.float32)
    y = xf * lax.rsqrt(jnp.mean(xf * xf, axis=-1, keepdims=True) + NORM_EPS)
    return (y * g.astype(jnp.float32)).astype(x.dtype)

def layernorm(x, g, b):
    xf = x.astype(jnp.float32)
    mu = jnp.mean(xf, axis=-1, keepdims=True)
    var = jnp.mean(jnp.square(xf - mu), axis=-1, keepdims=True)
    y = (xf - mu) * lax.rsqrt(var + NORM_EPS)
    return (y * g.astype(jnp.float32) + b.astype(jnp.float32)).astype(x.dtype)

def rope(x, pos):
    half = x.shape[-1] // 2
    inv = 1.0 / (ROPE_THETA ** (jnp.arange(half, dtype=jnp.float32) / half))
    ang = pos[:, None] * inv[None, :]
    cos = jnp.cos(ang)[None, :, None, :]
    sin = jnp.sin(ang)[None, :, None, :]
    xf = x.astype(jnp.float32)
    x1, x2 = xf[..., :half], xf[..., half:]
    return jnp.concatenate([x1 * cos - x2 * sin, x2 * cos + x1 * sin], axis=-1).astype(x.dtype)

def masked_softmax(s, mask):
    s = jnp.where(mask, s.astype(jnp.float32), -jnp.inf)
    m = jnp.max(s, axis=-1, keepdims=True)
    m = jnp.where(jnp.isfinite(m), m, 0.0)
    e = jnp.exp(s - m)
    d = jnp.sum(e, axis=-1, keepdims=True)
    return e / jnp.where(d > 0, d, 1.0)

def compress_blocks(k_raw, pos_emb, w1, w2):
    B, S, G, hd = k_raw.shape
    nc = (S - CMP_LEN) // CMP_STRIDE + 1
    idx = np.arange(nc)[:, None] * CMP_STRIDE + np.arange(CMP_LEN)[None, :]
    blk = k_raw[:, idx] + pos_emb[None, None, :, None, :]
    blk = blk.transpose(0, 1, 3, 2, 4).reshape(B, nc, G, CMP_LEN * hd)
    return jax.nn.gelu(blk @ w1) @ w2

def importance_map(nc, nsb):
    cs = np.arange(nc) * CMP_STRIDE
    ce = cs + CMP_LEN
    bs = np.arange(nsb) * SEL_BLOCK
    be = bs + SEL_BLOCK
    ov = np.clip(np.minimum(ce[:, None], be[None, :]) - np.maximum(cs[:, None], bs[None, :]), 0, None)
    return jnp.asarray(ov / CMP_LEN, jnp.float32)

def nsa_mixer(q, k_cmp_raw, v_cmp_raw, k_slc, v_slc, k_win, v_win, gates,
              cmp_pos_k, cmp_w1_k, cmp_w2_k, cmp_pos_v, cmp_w1_v, cmp_w2_v):
    B, S, _ = q.shape
    G, HPG, hd, QB = NSA_KV_GROUPS, NSA_HPG, HEAD_DIM, NSA_QBLOCK
    pos = jnp.arange(S, dtype=jnp.float32)
    q = rope(q.reshape(B, S, NSA_HEADS, hd), pos).reshape(B, S, G, HPG, hd) * (hd ** -0.5)
    nc = (S - CMP_LEN) // CMP_STRIDE + 1
    cmp_end_np = np.arange(nc) * CMP_STRIDE + CMP_LEN - 1
    kc = compress_blocks(k_cmp_raw.reshape(B, S, G, hd), cmp_pos_k, cmp_w1_k, cmp_w2_k)
    kc = rope(kc, jnp.asarray(cmp_end_np, jnp.float32))
    vc = compress_blocks(v_cmp_raw.reshape(B, S, G, hd), cmp_pos_v, cmp_w1_v, cmp_w2_v)
    cmp_end = jnp.asarray(cmp_end_np, jnp.int32)
    nsb = S // SEL_BLOCK
    topk = min(SEL_TOPK, nsb)
    ks = rope(k_slc.reshape(B, S, G, hd), pos)
    kb = ks.reshape(B, nsb, SEL_BLOCK, G, hd).transpose(0, 3, 1, 2, 4)
    vb = v_slc.reshape(B, nsb, SEL_BLOCK, G, hd).transpose(0, 3, 1, 2, 4)
    imp_map = importance_map(nc, nsb)
    blk_id = jnp.arange(nsb)
    bi = jnp.arange(B)[:, None, None, None]
    gi = jnp.arange(G)[None, :, None, None]
    kw = jnp.pad(rope(k_win.reshape(B, S, G, hd), pos), ((0, 0), (WINDOW, 0), (0, 0), (0, 0)))
    vw = jnp.pad(v_win.reshape(B, S, G, hd), ((0, 0), (WINDOW, 0), (0, 0), (0, 0)))
    gates = jax.nn.sigmoid(gates).reshape(B, S, G, HPG, 3)

    def query_block(i):
        s0 = i * QB
        t = s0 + jnp.arange(QB)
        qb = lax.dynamic_slice_in_dim(q, s0, QB, axis=1)
        gb = lax.dynamic_slice_in_dim(gates, s0, QB, axis=1)
        s = jnp.einsum('bqghd,bcgd->bghqc', qb, kc)
        p_cmp = masked_softmax(s, (cmp_end[None, :] <= t[:, None])[None, None, None])
        o_cmp = jnp.einsum('bghqc,bcgd->bqghd', p_cmp.astype(vc.dtype), vc)
        imp = jnp.einsum('bghqc,cn->bgqn', p_cmp, imp_map)
        tb = t // SEL_BLOCK
        valid = blk_id[None, :] * SEL_BLOCK <= t[:, None]
        forced = (blk_id[None, :] == 0) | (blk_id[None, :] == tb[:, None]) | (blk_id[None, :] == tb[:, None] - 1)
        score = jnp.where(valid, imp + jnp.where(forced, FORCE_BONUS, 0.0), -jnp.inf)
        _, idx = lax.top_k(score, topk)
        ksel = kb[bi, gi, idx].reshape(B, G, QB, topk * SEL_BLOCK, hd)
        vsel = vb[bi, gi, idx].reshape(B, G, QB, topk * SEL_BLOCK, hd)
        tok = (idx[..., None] * SEL_BLOCK + jnp.arange(SEL_BLOCK)).reshape(B, G, 1, QB, topk * SEL_BLOCK)
        s = jnp.einsum('bqghd,bgqmd->bghqm', qb, ksel)
        p = masked_softmax(s, tok <= t[None, None, None, :, None])
        o_slc = jnp.einsum('bghqm,bgqmd->bqghd', p.astype(vsel.dtype), vsel)
        kwb = lax.dynamic_slice_in_dim(kw, s0, WINDOW + QB, axis=1)
        vwb = lax.dynamic_slice_in_dim(vw, s0, WINDOW + QB, axis=1)
        kpos = s0 - WINDOW + jnp.arange(WINDOW + QB)
        wmask = (kpos[None, :] <= t[:, None]) & (kpos[None, :] > t[:, None] - WINDOW) & (kpos[None, :] >= 0)
        s = jnp.einsum('bqghd,bkgd->bghqk', qb, kwb)
        p = masked_softmax(s, wmask[None, None, None])
        o_win = jnp.einsum('bghqk,bkgd->bqghd', p.astype(vwb.dtype), vwb)
        return gb[..., 0:1] * o_cmp + gb[..., 1:2] * o_slc + gb[..., 2:3] * o_win

    out = lax.map(query_block, jnp.arange(S // QB))
    return out.transpose(1, 0, 2, 3, 4, 5).reshape(B, S, NSA_W)

def gla_mixer(q, k, v, a_lr, r, w_up, b_up, norm_g):
    B, S, _ = q.shape
    H, DK, DV, C = GLA_HEADS, GLA_DK, GLA_DV, GLA_CHUNK
    f32 = jnp.float32
    q = q.reshape(B, S, H, DK).astype(f32) * (DK ** -0.5)
    k = k.reshape(B, S, H, DK).astype(f32)
    v = v.reshape(B, S, H, DV).astype(f32)
    g = jax.nn.log_sigmoid((a_lr @ w_up + b_up).astype(f32)).reshape(B, S, H, DK) / GLA_TAU
    n = S // C

    def to_chunks(a):
        return a.reshape(B, n, C, H, a.shape[-1]).transpose(1, 0, 3, 2, 4)

    causal = jnp.tril(jnp.ones((C, C), dtype=bool))

    def step(state, inp):
        qc, kc, vc, gc = inp
        bcum = jnp.cumsum(gc, axis=2)
        o_inter = jnp.einsum('bhck,bhkv->bhcv', qc * jnp.exp(bcum), state)
        diff = bcum[:, :, :, None, :] - bcum[:, :, None, :, :]
        decay = jnp.exp(jnp.where(causal[None, None, :, :, None], diff, -jnp.inf))
        attn = jnp.einsum('bhik,bhjk,bhijk->bhij', qc, kc, decay)
        o_intra = jnp.einsum('bhij,bhjv->bhiv', attn, vc)
        blast = bcum[:, :, -1:, :]
        state = jnp.exp(blast[:, :, 0, :])[..., None] * state + jnp.einsum(
            'bhjk,bhjv->bhkv', kc * jnp.exp(blast - bcum), vc)
        return state, o_inter + o_intra

    state0 = jnp.zeros((B, H, DK, DV), f32)
    _, o = lax.scan(step, state0, (to_chunks(q), to_chunks(k), to_chunks(v), to_chunks(g)))
    o = o.transpose(1, 0, 3, 2, 4).reshape(B, S, H, DV)
    o = rmsnorm(o, norm_g) * jax.nn.silu(r.astype(f32)).reshape(B, S, H, DV)
    return o.reshape(B, S, GLA_W).astype(r.dtype)

def spatial_gating(uv, ln_g, ln_b, w_s, b_s):
    B, S, _ = uv.shape
    nch = S // SG_CHUNK
    u, v = jnp.split(jax.nn.gelu(uv), 2, axis=-1)
    v = layernorm(v, ln_g, ln_b).reshape(B, nch, SG_CHUNK, SG_GROUPS, SG_CH)
    w = jnp.tril(w_s)
    s = jnp.einsum('gij,bnjgc->bnigc', w, v) + b_s.T[None, None, :, :, None]
    out = u.reshape(B, nch, SG_CHUNK, SG_GROUPS, SG_CH) * s
    return out.reshape(B, S, SG_W)

def split_columns(z):
    offs = np.cumsum(IN_SIZES)[:-1]
    return jnp.split(z, [int(o) for o in offs], axis=-1)

def first_inputs(seed: int = 0) -> dict:
    key = jax.random.key(seed)
    ks = jax.random.split(key, 32)
    L = DEPTH
    res = (2.0 * DEPTH) ** -0.5

    def nrm(k, shape, scale):
        return jax.random.normal(k, shape, jnp.float32) * scale

    def gain(k, shape):
        return 1.0 + nrm(k, shape, 0.02)

    return {
        "x": nrm(ks[0], (BATCH, SEQ, D_MODEL), 1.0),
        "attn_norm": gain(ks[1], (L, D_MODEL)),
        "w_in": nrm(ks[2], (L, D_MODEL, D_IN), D_MODEL ** -0.5),
        "cmp_pos_k": nrm(ks[3], (L, CMP_LEN, HEAD_DIM), 0.1),
        "cmp_w1_k": nrm(ks[4], (L, CMP_LEN * HEAD_DIM, CMP_HIDDEN), (CMP_LEN * HEAD_DIM) ** -0.5),
        "cmp_w2_k": nrm(ks[5], (L, CMP_HIDDEN, HEAD_DIM), CMP_HIDDEN ** -0.5),
        "cmp_pos_v": nrm(ks[6], (L, CMP_LEN, HEAD_DIM), 0.1),
        "cmp_w1_v": nrm(ks[7], (L, CMP_LEN * HEAD_DIM, CMP_HIDDEN), (CMP_LEN * HEAD_DIM) ** -0.5),
        "cmp_w2_v": nrm(ks[8], (L, CMP_HIDDEN, HEAD_DIM), CMP_HIDDEN ** -0.5),
        "gla_w_up": nrm(ks[9], (L, GLA_RANK, GLA_HEADS * GLA_DK), GLA_RANK ** -0.5),
        "gla_b_up": nrm(ks[10], (L, GLA_HEADS * GLA_DK), 0.1),
        "gla_norm": gain(ks[11], (L, GLA_DV)),
        "sg_ln_g": gain(ks[12], (L, SG_W)),
        "sg_ln_b": nrm(ks[13], (L, SG_W), 0.02),
        "sg_w": nrm(ks[14], (L, SG_GROUPS, SG_CHUNK, SG_CHUNK), SG_CHUNK ** -0.5),
        "sg_b": 1.0 + nrm(ks[15], (L, SG_GROUPS, SG_CHUNK), 0.1),
        "w_out": nrm(ks[16], (L, D_MIX, D_MODEL), D_MIX ** -0.5 * res),
        "ffn_norm": gain(ks[17], (L, D_MODEL)),
        "w_gate": nrm(ks[18], (L, D_MODEL, D_FF), D_MODEL ** -0.5),
        "w_up": nrm(ks[19], (L, D_MODEL, D_FF), D_MODEL ** -0.5),
        "w_down": nrm(ks[20], (L, D_FF, D_MODEL), D_FF ** -0.5 * res),
        "final_norm": gain(ks[21], (D_MODEL,)),
    }

def first_block(x, attn_norm, w_in, cmp_pos_k, cmp_w1_k, cmp_w2_k, cmp_pos_v, cmp_w1_v, cmp_w2_v,
              gla_w_up, gla_b_up, gla_norm, sg_ln_g, sg_ln_b, sg_w, sg_b, w_out,
              ffn_norm, w_gate, w_up, w_down, final_norm):
    for l in range(DEPTH):
        h = rmsnorm(x, attn_norm[l])
        (q, kc, vc, ksl, vsl, kwn, vwn, gts, gq, gk, gv, ga, gr, uv) = split_columns(h @ w_in[l])
        o_nsa = nsa_mixer(q, kc, vc, ksl, vsl, kwn, vwn, gts,
                          cmp_pos_k[l], cmp_w1_k[l], cmp_w2_k[l], cmp_pos_v[l], cmp_w1_v[l], cmp_w2_v[l])
        o_gla = gla_mixer(gq, gk, gv, ga, gr, gla_w_up[l], gla_b_up[l], gla_norm[l])
        o_sg = spatial_gating(uv, sg_ln_g[l], sg_ln_b[l], sg_w[l], sg_b[l])
        x = x + jnp.concatenate([o_nsa, o_gla.astype(x.dtype), o_sg], axis=-1) @ w_out[l]
        h = rmsnorm(x, ffn_norm[l])
        x = x + (jax.nn.silu(h @ w_gate[l]) * (h @ w_up[l])) @ w_down[l]
    return rmsnorm(x, final_norm)


DEPTH_2 = 1

GRID_W = 64
D_A = D_MODEL
A_BLOCKS = 16
A_BW = D_A // A_BLOCKS
CONV_W = 4
RG_C = 8.0
N_HEADS = 16
D_B = N_HEADS * HEAD_DIM
WIN_R = 8
WIN_C = 16
IN_SPLITS = (D_A, D_A, D_B, D_B, D_B, D_B, D_MODEL, D_MODEL)
IN_COLS = sum(IN_SPLITS)
EPS = 1e-6


def rms_norm(x, g):
    x32 = x.astype(jnp.float32)
    y = x32 * lax.rsqrt(jnp.mean(x32 * x32, axis=-1, keepdims=True) + EPS)
    return (y * g.astype(jnp.float32)).astype(x.dtype)

def block_diag(x, w, b):
    B, S, C = x.shape
    xr = x.reshape(B, S, A_BLOCKS, A_BW)
    return jnp.einsum('bshi,hij->bshj', xr, w).reshape(B, S, C) + b

def centred_dwconv(x, w, b):
    C = x.shape[-1]
    y = lax.conv_general_dilated(
        x, w[:, None, :].astype(x.dtype), window_strides=(1,),
        padding=[(CONV_W // 2, CONV_W - 1 - CONV_W // 2)],
        dimension_numbers=('NWC', 'WIO', 'NWC'), feature_group_count=C)
    return y + b

def _lin_combine(e1, e2):
    a1, b1 = e1
    a2, b2 = e2
    return a1 * a2, a2 * b1 + b2

def rg_lru(x, w_r, b_r, w_i, b_i, lam, reverse):
    x32 = x.astype(jnp.float32)
    r = jax.nn.sigmoid(block_diag(x, w_r, b_r).astype(jnp.float32))
    i = jax.nn.sigmoid(block_diag(x, w_i, b_i).astype(jnp.float32))
    log_a = -RG_C * r * jax.nn.softplus(-lam.astype(jnp.float32))
    a = jnp.exp(log_a)
    u = jnp.sqrt(-jnp.expm1(2.0 * log_a)) * (i * x32)
    _, h = lax.associative_scan(_lin_combine, (a, u), axis=1, reverse=reverse)
    return h

def neighbourhood_attention(q, k, v, rpb):
    B, S, H, dh = q.shape
    rows = S // GRID_W
    win_r = min(WIN_R, rows)
    qg = q.reshape(B, rows, GRID_W, H, dh)
    kg = k.reshape(B, rows, GRID_W, H, dh)
    vg = v.reshape(B, rows, GRID_W, H, dh)
    cols = jnp.arange(GRID_W)
    c0 = jnp.clip(cols - WIN_C // 2, 0, GRID_W - WIN_C)
    cidx = c0[:, None] + jnp.arange(WIN_C)[None, :]
    dcol = cidx - cols[:, None] + (WIN_C - 1)
    scale = dh ** -0.5

    def row_fn(r):
        r0 = jnp.clip(r - win_r // 2, 0, rows - win_r)
        q_r = lax.dynamic_index_in_dim(qg, r, axis=1, keepdims=False)
        k_rows = lax.dynamic_slice_in_dim(kg, r0, win_r, axis=1)
        v_rows = lax.dynamic_slice_in_dim(vg, r0, win_r, axis=1)
        k_win = k_rows[:, :, cidx]
        v_win = v_rows[:, :, cidx]
        s = jnp.einsum('bqhd,bwqkhd->bhqwk', q_r, k_win).astype(jnp.float32) * scale
        drow = r0 + jnp.arange(win_r) - r + (WIN_R - 1)
        bias = rpb[:, drow][:, :, dcol]
        s = s + jnp.transpose(bias, (0, 2, 1, 3)).astype(jnp.float32)[None]
        p = jax.nn.softmax(s.reshape(B, H, GRID_W, win_r * WIN_C), axis=-1)
        p = p.reshape(B, H, GRID_W, win_r, WIN_C).astype(v.dtype)
        return jnp.einsum('bhqwk,bwqkhd->bqhd', p, v_win)

    out = lax.map(row_fn, jnp.arange(rows))
    return jnp.transpose(out, (1, 0, 2, 3, 4)).reshape(B, S, H * dh)

def second_inputs(seed: int = 0) -> dict:
    key = jax.random.key(seed)
    ks = jax.random.split(key, 26)
    n = lambda k, shp, s: jax.random.normal(k, shp, jnp.float32) * s

    def lam_init(k):
        a0 = jax.random.uniform(k, (DEPTH_2, D_A), jnp.float32, 0.9, 0.999)
        u = a0 ** (1.0 / RG_C)
        return jnp.log(u) - jnp.log1p(-u)

    return {
        "x": n(ks[0], (BATCH, SEQ, D_MODEL), 1.0),
        "c": n(ks[1], (BATCH, D_MODEL), 1.0),
        "g_pre": 1.0 + n(ks[2], (DEPTH_2, D_MODEL), 0.02),
        "w_c": n(ks[3], (DEPTH_2, D_MODEL, 3 * D_MODEL), D_MODEL ** -0.5),
        "b_c": n(ks[4], (DEPTH_2, 3 * D_MODEL), 0.02),
        "w_in": n(ks[5], (DEPTH_2, D_MODEL, IN_COLS), D_MODEL ** -0.5),
        "conv_w": n(ks[6], (DEPTH_2, CONV_W, D_A), CONV_W ** -0.5),
        "conv_b": n(ks[7], (DEPTH_2, D_A), 0.02),
        "w_r_f": n(ks[8], (DEPTH_2, A_BLOCKS, A_BW, A_BW), A_BW ** -0.5),
        "b_r_f": n(ks[9], (DEPTH_2, D_A), 0.02),
        "w_i_f": n(ks[10], (DEPTH_2, A_BLOCKS, A_BW, A_BW), A_BW ** -0.5),
        "b_i_f": n(ks[11], (DEPTH_2, D_A), 0.02),
        "lam_f": lam_init(ks[12]),
        "w_r_b": n(ks[13], (DEPTH_2, A_BLOCKS, A_BW, A_BW), A_BW ** -0.5),
        "b_r_b": n(ks[14], (DEPTH_2, D_A), 0.02),
        "w_i_b": n(ks[15], (DEPTH_2, A_BLOCKS, A_BW, A_BW), A_BW ** -0.5),
        "b_i_b": n(ks[16], (DEPTH_2, D_A), 0.02),
        "lam_b": lam_init(ks[17]),
        "rpb": n(ks[18], (DEPTH_2, N_HEADS, 2 * WIN_R - 1, 2 * WIN_C - 1), 0.1),
        "w_pa": n(ks[19], (DEPTH_2, D_A, D_MODEL), D_A ** -0.5),
        "w_pb": n(ks[20], (DEPTH_2, D_B, D_MODEL), D_B ** -0.5),
        "w_o": n(ks[21], (DEPTH_2, D_MODEL, D_MODEL), D_MODEL ** -0.5),
        "g_final": 1.0 + n(ks[22], (D_MODEL,), 0.02),
    }

def second_block(x, c, g_pre, w_c, b_c, w_in, conv_w, conv_b, w_r_f, b_r_f, w_i_f, b_i_f, lam_f,
              w_r_b, b_r_b, w_i_b, b_i_b, lam_b, rpb, w_pa, w_pb, w_o, g_final):
    B, S, D = x.shape
    split_pts = list(np.cumsum(IN_SPLITS)[:-1])
    for l in range(DEPTH_2):
        mod = jax.nn.silu(c) @ w_c[l] + b_c[l]
        shift, scl, gate = jnp.split(mod, 3, axis=-1)
        h = rms_norm(x, g_pre[l]) * (1.0 + scl[:, None, :]) + shift[:, None, :]

        proj = h @ w_in[l]
        xa, za, q, k, v, zb, ga, gb = jnp.split(proj, split_pts, axis=-1)

        xa = centred_dwconv(xa, conv_w[l], conv_b[l])
        h_fwd = rg_lru(xa, w_r_f[l], b_r_f[l], w_i_f[l], b_i_f[l], lam_f[l], reverse=False)
        h_bwd = rg_lru(xa, w_r_b[l], b_r_b[l], w_i_b[l], b_i_b[l], lam_b[l], reverse=True)
        y_a = (h_fwd + h_bwd).astype(x.dtype) * jax.nn.silu(za)
        y_a = y_a @ w_pa[l]

        qh = q.reshape(B, S, N_HEADS, HEAD_DIM)
        kh = k.reshape(B, S, N_HEADS, HEAD_DIM)
        vh = v.reshape(B, S, N_HEADS, HEAD_DIM)
        y_b = neighbourhood_attention(qh, kh, vh, rpb[l]) * jax.nn.silu(zb)
        y_b = y_b @ w_pb[l]

        merged = jax.nn.sigmoid(ga) * y_a + jax.nn.sigmoid(gb) * y_b
        x = x + gate[:, None, :] * (merged @ w_o[l])
    return rms_norm(x, g_final)


def setup_inputs(seed=0):
    out = dict(first_inputs(seed))
    for name, value in second_inputs(seed + 1).items():
        if name != "x":
            out[name + "_2"] = value
    return out


def reference(
    x, attn_norm, w_in, cmp_pos_k, cmp_w1_k, cmp_w2_k, cmp_pos_v, cmp_w1_v, cmp_w2_v, gla_w_up,
    gla_b_up, gla_norm, sg_ln_g, sg_ln_b, sg_w, sg_b, w_out, ffn_norm, w_gate, w_up, w_down,
    final_norm, c_2, g_pre_2, w_c_2, b_c_2, w_in_2, conv_w_2, conv_b_2, w_r_f_2, b_r_f_2,
    w_i_f_2, b_i_f_2, lam_f_2, w_r_b_2, b_r_b_2, w_i_b_2, b_i_b_2, lam_b_2, rpb_2, w_pa_2,
    w_pb_2, w_o_2, g_final_2,
):
    x = first_block(
        x, attn_norm, w_in, cmp_pos_k, cmp_w1_k, cmp_w2_k, cmp_pos_v, cmp_w1_v, cmp_w2_v,
        gla_w_up, gla_b_up, gla_norm, sg_ln_g, sg_ln_b, sg_w, sg_b, w_out, ffn_norm, w_gate,
        w_up, w_down, final_norm,
    )
    return second_block(
        x, c_2, g_pre_2, w_c_2, b_c_2, w_in_2, conv_w_2, conv_b_2, w_r_f_2, b_r_f_2, w_i_f_2,
        b_i_f_2, lam_f_2, w_r_b_2, b_r_b_2, w_i_b_2, b_i_b_2, lam_b_2, rpb_2, w_pa_2, w_pb_2,
        w_o_2, g_final_2,
    )


_drawn_inputs = setup_inputs


def setup_inputs(seed=0):
    import zlib

    import numpy as np

    out = dict(_drawn_inputs(seed))
    spreads = {}
    factors = {'attn_norm': 4.469,
     'cmp_pos_k': 8.0,
     'gla_b_up': 5.706,
     'gla_norm': 8.0,
     'sg_ln_g': 8.0,
     'sg_ln_b': 8.0,
     'ffn_norm': 4.712,
     'g_pre_2': 3.258,
     'b_r_f_2': 38.778,
     'b_i_f_2': 27.379,
     'b_r_b_2': 44.263,
     'b_i_b_2': 29.013,
     'rpb_2': 8.0,
     'g_final_2': 8.497,
     'cmp_pos_v': 4.108}
    for name, (base, spread) in spreads.items():
        noise = np.random.default_rng([zlib.crc32(name.encode()), seed]).standard_normal(out[name].shape)
        drawn = base * np.exp(spread * noise) if base else spread * noise
        out[name] = __import__('jax').numpy.asarray(drawn.astype(out[name].dtype))
    for name, factor in factors.items():
        out[name] = (out[name] * factor).astype(out[name].dtype)
    return out
```

```python
import concourse.bass as bass
from concourse import mybir
from contextlib import ExitStack

S, D, P = 512, 1024, 128
DEPTH = 2
KT = D // P
NT = S // P
HD = 64
HEADS, GROUPS, BR = 8, 2, 3
CMP_LEN, CMP_STRIDE = 32, 16
NC = (S - CMP_LEN) // CMP_STRIDE + 1
GH, GDK, GDV = 4, 32, 64
TAU = 16.0
DFF = 2816
FCH = 2
FT = DFF // P // FCH
EPS = 1e-6
NH2, GRID, ROWS = 16, 64, 8
QC, KC = 16, 32
RW = QC + KC
LOW = [0, 8, 24, 32]
RG_C = 8.0

T = {"q0": 0, "q1": 1, "q2": 2, "q3": 3, "ksl": 4, "vsl": 5, "kwn": 6, "vwn": 7, "kc": 8, "vc": 9,
     "gk": 10, "gq": 11, "gv0": 12, "gv1": 13, "gr0": 14, "gr1": 15, "sv0": 16, "sv1": 17,
     "su0": 18, "su1": 19, "gate": 20}
ORDER = ["kc", "gate", "ksl", "vsl", "CK", "vc", "kwn", "vwn", "q0", "q1", "CV", "q2", "q3",
         "gk", "gq", "gv0", "gv1", "gr0", "gr1", "sv0", "sv1", "su0", "su1"]
LAG = 2
MOD_SLOTS = 3 * KT
MOD_PER_LAYER = MOD_SLOTS // DEPTH


def mod_tiles(h):
    return 2 if h < MOD_PER_LAYER - HEADS else 1


CMP_SLOTS = 2 * (CMP_LEN * HD // P) // 8

def columns(fields):
    at, out = 0, {}
    for name, n in fields:
        out[name] = (at, at + n)
        at += n
    return out, at


CONST, CONST_N = columns([
    ("ident", P), ("ones", P), ("nmask", NT * KC), ("cos", S), ("sin", S), ("cosc", 2 * NC), ("sinc", 2 * NC),
    ("causal", P), ("cmask", NT * NC), ("rowok", 1), ("rot", P), ("dup", 2 * P), ("rotdup", 2 * P),
    ("headones", P), ("triu", P), ("levels", 8 * P)])
MISC, MISC_N = columns([
    ("g_attn", KT), ("g_ffn", KT), ("pos_k", 16), ("pos_v", 16), ("b_up", 1), ("gnorm", 1),
    ("w2k", 2 * P), ("w2v", 2 * HD), ("w_up", P), ("swt", 4 * P), ("lng", 2 * P), ("lnb", 2 * P),
    ("sgb", 2 * P)])
VEC, VEC_N = columns([
    ("g_fin1", KT), ("c", 2 * KT), ("b_c", MOD_SLOTS), ("g_pre", KT), ("conv_w", 4 * KT),
    ("conv_b", KT), ("b_gate", 4 * KT), ("lam", 2 * KT), ("g_fin2", KT)])
RPB_PAD = QC
RPB_LEN = NH2 * 15 * 31


def stream_plan():
    out = []
    for l in range(DEPTH):
        for name in ORDER:
            out += [("cmp", l, name, i) for i in range(CMP_SLOTS)] if name in ("CK", "CV") else [("in", l, name)]
        out += [("mod", l * MOD_PER_LAYER + m) for m in range(MOD_PER_LAYER)]
        out += [("out", l, m) for m in range(KT)]
        for c in range(FCH):
            for f in range(FT):
                out += [("gate", l, c * FT + f), ("up", l, c * FT + f)]
            out += [("down", l, c, i) for i in range(FT)]
    out += [("in2", m) for m in range(8)]
    for g in range(4):
        out += [("in2", 8 + 2 * g + j) for j in range(2)]
        out += [("in2", part * 8 + 2 * g + j) for part in (2, 3, 4, 5) for j in range(2)]
    for m in range(8):
        out += [("in2", 48 + m), ("pa", m)]
    for m in range(8):
        out += [("pb", m), ("in2", 56 + m)]
    out += [("wo", m) for m in range(8)]
    return out


def build(nc, a_x, a_w, a_const, a_misc, a_vec, a_rgw, a_rpb, a_out, dbg=None):
    F32, F32R, U32 = mybir.dt.float32, mybir.dt.float32r, mybir.dt.uint32
    ALU, ACT, AX = mybir.AluOpType, mybir.ActivationFunctionType, mybir.AxisListType
    PLAN = stream_plan()
    SLOTS = len(PLAN)
    RING = 4
    assert SLOTS % RING == 2
    ctx = ExitStack()
    with ctx:
        place = [0]

        def at(name, shape, dt, offset):
            return nc.alloc_sbuf_tensor_at(name, shape, dt, offset=offset)

        base = nc.sbuf_base if not callable(nc.sbuf_base) else nc.sbuf_base()
        place[0] = (int(base) + 63) // 64 * 64

        def sb(name, shape, dt=F32):
            n = 4
            for k in shape[1:]:
                n *= k
            t = at(name, shape, dt, place[0])
            place[0] += (n + 31) // 32 * 32
            return t

        def sem(name):
            return ctx.enter_context(nc.semaphore(name))

        x = sb("x", [P, KT, S])
        a_hi = sb("a_hi", [P, KT, S], F32R)
        a_lo = sb("a_lo", [P, KT, S], F32R)
        raw = sb("raw", [P, RING, 8, P])
        w_hi = sb("w_hi", [P, RING, 8, P], F32R)
        w_lo = sb("w_lo", [P, RING, 8, P], F32R)
        const = sb("const", [P, CONST_N])
        tail = place[0] - (CONST_N - CONST["cos"][0]) * 4
        vec = sb("vec", [P, VEC_N])
        rstd = sb("rstd", [P, S])
        tmp = sb("tmp", [P, S])
        sq = sb("sq", [P, 2, S])
        modv = sb("modv", [P, MOD_SLOTS])
        csil = sb("csil", [P, 2 * KT])
        c_hi = sb("c_hi", [P, 2 * KT], F32R)
        c_lo = sb("c_lo", [P, 2 * KT], F32R)
        lam_z = sb("lam_z", [P, 2 * KT])
        lam_s = sb("lam_s", [P, 2 * KT])
        lam_q = sb("lam_q", [P, 2 * KT])
        lam_p = sb("lam_p", [P, 2 * KT])
        lam_n = sb("lam_n", [P, 2 * KT])
        epst = sb("epst", [P, 1])
        gainm = sb("gainm", [P, KT])
        arena = place[0]
        proj = sb("proj", [P, 21, S])
        after = place[0]
        place[0] = arena
        f_hi = sb("f_hi", [P, FT, S], F32R)
        f_lo = sb("f_lo", [P, FT, S], F32R)
        place[0] = max(after, place[0])
        misc = sb("misc", [P, MISC_N])
        keys = sb("keys", [P, 2, GROUPS, S])
        work = sb("work", [P, 8, S])
        X_hi = at("X_hi", [P, 16, 2 * NC], F32R, place[0] - 4 * S * 4)
        X_lo = at("X_lo", [P, 16, 2 * NC], F32R, place[0] - 2 * S * 4)
        hid = sb("hid", [P, 2, 2, 2 * NC])
        kcr = sb("kcr", [P, 2 * NC])
        kc0 = sb("kc0", [P, 2 * NC])
        vcn = sb("vcn", [32, GROUPS * HD])
        gN = sb("gN", [P, NT, 24])
        Pc = sb("Pc", [P, 2, NT, 32])
        PTc = sb("PTc", [32, 2, S])
        diag = sb("diag", [P, 2, 2, P])
        diagc = sb("diagc", [P, NT, P])
        nmaxc = sb("nmaxc", [P, 2, NT])
        sumsc = sb("sumsc", [P, 2, NT])
        nmax = sb("nmax", [P, 2, 4])
        sums = sb("sums", [P, 2, 4])
        r3 = sb("r3", [P, 4])
        small = sb("small", [P, 64])
        end1 = place[0]
        place[0] = arena
        y_hi = sb("y_hi", [P, KT, S], F32R)
        y_lo = sb("y_lo", [P, KT, S], F32R)
        yb = sb("yb", [P, KT, S])
        xc = sb("xc", [P, KT, S])
        qkv = sb("qkv", [P, 6, S])
        shared = place[0]
        rg = sb("rg", [P, 6, S])
        end2 = place[0]
        place[0] = shared
        P2 = sb("P2", [P, 4, 256])
        PT2 = sb("PT2", [P, 4, 256])
        vW = sb("vW", [P, 8, P])
        end2 = max(end2, place[0])
        place[0] = (tail + 31) // 32 * 32
        xpad = sb("xpad", [P, S + 3])
        rgw = sb("rgw", [P, 4, P])
        bias = sb("bias", [P, 4, ROWS, RW])
        dg2 = sb("dg2", [P, 4, P])
        sm2 = sb("sm2", [P, 12])
        assert place[0] <= tail + (CONST_N - CONST["cos"][0]) * 4
        assert max(end1, end2) <= nc.sbuf_usable_end
        PS = ctx.enter_context(nc.psum_tensor("PS", [P, 8, S], F32))
        rpb_dram = a_rpb

        def c_(name):
            return const[:, CONST[name][0]:CONST[name][1]]

        def m_(name):
            return misc[:, MISC[name][0]:MISC[name][1]]

        def v_(name):
            return vec[:, VEC[name][0]:VEC[name][1]]

        ident = c_("ident")
        Ad = proj[:, 0:4, :].rearrange("p h (n c) -> p h n c", c=P)
        Ax = proj[:, 4:10, :].rearrange("p a b -> p (a b)").rearrange("p (h c) -> p h c", h=GH)
        X = work[:, 0:2, :].rearrange("p a b -> p (a b)")[:, 0:16 * 2 * NC].rearrange("p (k c) -> p k c", c=2 * NC)

        full = [sem(f"full{b}") for b in range(8)]
        free = [sem(f"free{b}") for b in range(8)]
        fills = [0] * 8
        uses = {}

        class Signal:

            def __init__(self, name):
                self.sem, self.n, self.seen = sem(name), 0, {}

            def raised(self):
                self.n += 1
                return self.n

            def seen_by(self, who, k=1):
                self.seen[who] = self.seen.get(who, 0) + k
                return self.seen[who]

        raw_in = [sem(f"raw_in{r}") for r in range(RING)]
        split_done = sem("split_done")
        slot_used = sem("slot_used")
        const_in = sem("const_in")
        misc_in = sem("misc_in")
        rgw_in = sem("rgw_in")
        bias_in = [sem("bias_in0"), sem("bias_in1")]
        x_in = sem("x_in")
        out_done = sem("out_done")
        pool_chain = sem("pool_chain")
        dve_chain = Signal("dve_chain")
        act_chain = Signal("act_chain")
        h_hi = Signal("h_hi")
        h_lo = Signal("h_lo")
        squares = Signal("squares")
        sq_used = Signal("sq_used")
        rstd_ok = Signal("rstd_ok")
        x_ok = Signal("x_ok")
        roped = Signal("roped")
        to_act = Signal("to_act")
        to_dve = Signal("to_dve")
        to_pe = Signal("to_pe")
        maxc_ok = Signal("maxc_ok")
        max_ok = Signal("max_ok")
        exp_ok = Signal("exp_ok")
        diagc_ok = Signal("diagc_ok")
        diag_ok = Signal("diag_ok")
        pv_done = Signal("pv_done")
        misc_free = Signal("misc_free")
        rgw_free = Signal("rgw_free")
        bias_free = Signal("bias_free")
        eps_ok = Signal("eps_ok")
        c_ready = Signal("c_ready")
        out_ok = Signal("out_ok")

        def filling(name):
            b, k = uses[name]
            return full[b], k + 1

        def emptying(name):
            b, k = uses[name]
            return free[b], k + 1

        def room(name):
            b, k = uses[name]
            return free[b], k

        def emptied(name):
            return free[uses[name][0]]

        block = ctx.enter_context(nc.Block())
        w_rows = a_w.rearrange("n p c -> (n p) c")
        w_sl = a_w.rearrange("n p (k c) -> n p k c", c=P)

        @block.tensor
        def _(pe):
            st = {"n": 0, "sub": 0}

            def claim(name, b):
                uses[name] = (b, fills[b])
                fills[b] += 1
                return fills[b] > 1

            def weights():
                if st["sub"] == 0:
                    pe.wait_ge(split_done, st["n"] + 1)
                first = st["sub"] == 0 and st["n"] > 0
                r, k = st["n"] % RING, st["sub"]
                st["sub"] += 1
                if st["sub"] == 8:
                    st["sub"], st["n"] = 0, st["n"] + 1
                return w_hi[:, r, k, :], w_lo[:, r, k, :], first

            def product(out, hi, lo, start, stop):
                wh, wl, first = weights()
                ins = nc.tensor.matmul(out, wh, hi, start=start, stop=False)
                if first:
                    ins.then_inc(slot_used, 1)
                nc.tensor.matmul(out, wh, lo, start=False, stop=False)
                return nc.tensor.matmul(out, wl, hi, start=False, stop=stop)

            def gemm(name, b, hi, lo, n=KT):
                if claim(name, b):
                    pe.wait_ge(*room(name))
                out = PS[:, b, :]
                for k in range(n):
                    ins = product(out, hi[:, k, :], lo[:, k, :], k == 0, k == n - 1)
                ins.then_inc(filling(name)[0], 1)

            def stats_step(key, k):
                if k == 0:
                    if claim(key, 7):
                        pe.wait_ge(*room(key))
                pe.wait_ge(squares.sem, squares.seen_by("pe"))
                ins = nc.tensor.matmul(PS[:, 7, :], c_("ones"), sq[:, k % 2, :], start=k == 0, stop=k == KT - 1)
                if k < KT - 1:
                    ins.then_inc(sq_used.sem, 1)
                    sq_used.raised()
                else:
                    ins.then_inc(filling(key)[0], 1)

            def normed_gemm(key, name, b):
                if claim(name, b):
                    pe.wait_ge(*room(name))
                for k in range(KT):
                    pe.wait_ge(h_lo.sem, h_lo.seen_by("pe"))
                    ins = product(PS[:, b, :], a_hi[:, k, :], a_lo[:, k, :], k == 0, k == KT - 1)
                    if k == KT - 1:
                        ins.then_inc(filling(name)[0], 1)
                    stats_step(key, k)

            aux = [0]

            def aux_bank():
                aux[0] += 1
                return 4 + aux[0] % 3

            def one(name, lhsT, rhs, cols=S, rows=P):
                b = aux_bank()
                if claim(name, b):
                    pe.wait_ge(*room(name))
                nc.tensor.matmul(PS[0:rows, b, 0:cols], lhsT, rhs, start=True, stop=True)\
                    .then_inc(filling(name)[0], 1)

            pe.wait_ge(const_in, 32)
            for l in range(DEPTH):
                gb = 0

                def further(name):
                    t = T.get(name)
                    if name in ("kc", "vc"):
                        pe.wait_ge(*emptying((l, name)))
                        for g in range(GROUPS):
                            one((l, name, "dup", g), c_("dup")[:, g * P:(g + 1) * P], proj[:, t, :])
                    elif name in ("ksl", "kwn"):
                        pe.wait_ge(*emptying((l, name)))
                        for g in range(GROUPS):
                            one((l, name, "dup", g), c_("dup")[:, g * P:(g + 1) * P], proj[:, t, :])
                            one((l, name, "rot", g), c_("rotdup")[:, g * P:(g + 1) * P], proj[:, t, :])
                    elif name[0] == "q":
                        pe.wait_ge(*emptying((l, name)))
                        one((l, name, "rot"), c_("rot"), proj[:, t, :])
                    elif name in ("vsl", "vwn", "gv0", "gv1", "sv0", "sv1", "gate"):
                        pe.wait_ge(*emptying((l, name)))
                        w = 24 if name == "gate" else P
                        b = aux_bank()
                        if claim((l, name, "T"), b):
                            pe.wait_ge(*room((l, name, "T")))
                        for i in range(NT):
                            ins = nc.tensor.transpose(PS[:, b, i * w:(i + 1) * w], proj[0:w, t, i * P:(i + 1) * P],
                                                      ident[0:w, 0:w])
                        ins.then_inc(filling((l, name, "T"))[0], 1)
                    elif name == "CK":
                        pe.wait_ge(*emptying((l, "CK", 1)))
                        b = aux_bank()
                        if claim((l, "kc2"), b):
                            pe.wait_ge(*room((l, "kc2")))
                        for m in range(2):
                            ins = nc.tensor.matmul(PS[:, b, 0:2 * NC], m_("w2k")[:, m * P:(m + 1) * P], hid[:, 0, m, :],
                                                   start=m == 0, stop=m == 1)
                        ins.then_inc(filling((l, "kc2"))[0], 1)
                        pe.wait_ge(*emptying((l, "kc2")))
                        one((l, "kc2rot"), c_("rot"), kc0[:, :], cols=2 * NC)
                    elif name == "CV":
                        pe.wait_ge(*emptying((l, "CV", 1)))
                        b = aux_bank()
                        if claim((l, "vc2"), b):
                            pe.wait_ge(*room((l, "vc2")))
                        for g in range(GROUPS):
                            for m in range(2):
                                ins = nc.tensor.matmul(PS[0:NC, b, g * HD:(g + 1) * HD], hid[:, 1, m, g * NC:(g + 1) * NC],
                                                       m_("w2v")[:, m * HD:(m + 1) * HD], start=m == 0, stop=m == 1)
                        ins.then_inc(filling((l, "vc2"))[0], 1)

                for idx, name in enumerate(ORDER):
                    if idx == 0:
                        normed_gemm((l, "ss"), (l, name), 0)
                        gb = 1
                        pe.wait_ge(misc_in, 16 * (l + 1))
                    elif name in ("CK", "CV"):
                        for m in range(2):
                            key, b = (l, name, m), gb % 4
                            gb += 1
                            if claim(key, b):
                                pe.wait_ge(*room(key))
                            if m == 0:
                                pe.wait_ge(to_pe.sem, to_pe.seen_by("pe"))
                            for k in range(16):
                                ins = product(PS[:, b, 0:2 * NC], X_hi[:, k, :], X_lo[:, k, :], k == 0, k == 15)
                            ins.then_inc(filling(key)[0], 1)
                    else:
                        gemm((l, name), gb % 4, a_hi, a_lo)
                        gb += 1
                    if idx >= LAG:
                        further(ORDER[idx - LAG])
                for name in ORDER[-LAG:]:
                    further(name)

                U = HEADS * NT

                def scores(u):
                    h, i, par = u // NT, u % NT, u % 2
                    p0, g = HD * (h % 2), h // (HEADS // GROUPS)
                    q = proj[p0:p0 + HD, h // 2, i * P:(i + 1) * P]
                    w = (i + 1) * P
                    for br in range(2):
                        key = (l, "S", br, u)
                        if claim(key, 2 * par + br):
                            pe.wait_ge(*room(key))
                        nc.tensor.matmul(PS[:, 2 * par + br, 0:w], q, keys[p0:p0 + HD, br, g, 0:w],
                                                start=True, stop=True).then_inc(filling(key)[0], 1)

                def turn(u):
                    i, par = u % NT, u % 2
                    pe.wait_ge(diag_ok.sem, diag_ok.seen_by("pe"))
                    for br in range(2):
                        key = (l, "PT", br, u)
                        if claim(key, 4 + br):
                            pe.wait_ge(*room(key))
                        for j in range(i + 1):
                            ins = nc.tensor.matmul(PS[:, 4 + br, j * P:(j + 1) * P],
                                                   work[:, 2 * par + br, j * P:(j + 1) * P], diag[:, par, br, :],
                                                   start=True, stop=True)
                        ins.then_inc(filling(key)[0], 1)

                def compressed_scores(h):
                    p0, g = HD * (h % 2), h // (HEADS // GROUPS)
                    key = (l, "Sc", h)
                    if claim(key, 7):
                        pe.wait_ge(*room(key))
                    for i in range(NT):
                        ins = nc.tensor.matmul(PS[:, 7, i * 32:i * 32 + NC], proj[p0:p0 + HD, h // 2, i * P:(i + 1) * P],
                                               kcr[p0:p0 + HD, g * NC:(g + 1) * NC], start=True, stop=True)
                    ins.then_inc(filling(key)[0], 1)

                def turn_compressed(h):
                    pe.wait_ge(diagc_ok.sem, diagc_ok.seen_by("pe"))
                    key = (l, "PTc", h)
                    if claim(key, 7):
                        pe.wait_ge(*room(key))
                    for i in range(NT):
                        ins = nc.tensor.matmul(PS[0:NC, 7, i * P:(i + 1) * P], Pc[:, h % 2, i, 0:NC], diagc[:, i, :],
                                               start=True, stop=True)
                    ins.then_inc(filling(key)[0], 1)

                def values(u):
                    h, i, par = u // NT, u % NT, u % 2
                    p0, g = HD * (h % 2), h // (HEADS // GROUPS)
                    key = (l, "O", h // 2)
                    if u % (2 * NT) == 0:
                        if claim(key, 6):
                            pe.wait_ge(*room(key))
                    out = PS[p0:p0 + HD, 6, i * P:(i + 1) * P]
                    pe.wait_ge(*emptying((l, "PTc", h)))
                    nc.tensor.matmul(out, vcn[0:NC, g * HD:(g + 1) * HD], PTc[0:NC, h % 2, i * P:(i + 1) * P],
                                     start=True, stop=False)
                    for br in range(2):
                        pe.wait_ge(*emptying((l, "PT", br, u)))
                        v = proj[:, T["vsl"] + 2 * br, :].rearrange("p (n c) -> p n c", c=P)
                        for j in range(i + 1):
                            ins = nc.tensor.matmul(out, v[:, j, g * HD:(g + 1) * HD],
                                                   work[:, 4 + 2 * par + br, j * P:(j + 1) * P],
                                                   start=False, stop=br == 1 and j == i)
                    if u % (2 * NT) == 2 * NT - 1:
                        ins.then_inc(filling(key)[0], 1)
                    else:
                        ins.then_inc(pv_done.sem, 1)
                        pv_done.raised()

                def modulation(h):
                    if l == 0 and h == 0:
                        pe.wait_ge(c_ready.sem, 1)
                    if claim((l, "mod", h), 7):
                        pe.wait_ge(*room((l, "mod", h)))
                    for n in range(mod_tiles(h)):
                        for k in range(KT):
                            ins = product(PS[:, 7, 2 * n:2 * n + 2], c_hi[:, 2 * k:2 * k + 2], c_lo[:, 2 * k:2 * k + 2],
                                          k == 0, k == KT - 1)
                    ins.then_inc(filling((l, "mod", h))[0], 1)

                pe.wait_ge(roped.sem, roped.seen_by("pe", 2 * GROUPS + 4 + 1))
                pe.wait_ge(*emptying((l, "vc2")))
                pe.wait_ge(*emptying((l, "vwn", "T")))
                compressed_scores(0)
                scores(0)
                scores(1)
                turn_compressed(0)
                for u in range(U):
                    h, i = u // NT, u % NT
                    turn(u)
                    if u + 2 < U:
                        scores(u + 2)
                    if i == 0 and h + 1 < HEADS:
                        compressed_scores(h + 1)
                    if i == 2:
                        modulation(h)
                    if i == 3 and h + 1 < HEADS:
                        turn_compressed(h + 1)
                    if u >= 1:
                        values(u - 1)
                values(U - 1)

                one((l, "z"), m_("w_up")[32:48, :], proj[32:48, T["gate"], :])
                for lv in range(8):
                    pe.wait_ge(to_pe.sem, to_pe.seen_by("pe"))
                    for h in range(GH):
                        key = (l, "lv", lv, h)
                        if claim(key, h):
                            pe.wait_ge(*room(key))
                        for i in range(NT):
                            r = slice(GDK * h, GDK * h + GDK)
                            ins = nc.tensor.matmul(PS[:, h, i * P:(i + 1) * P], work[r, 6 + lv % 2, i * P:(i + 1) * P],
                                                   work[r, 4 + lv % 2, i * P:(i + 1) * P], start=True, stop=True,
                                                   tile_position=(GDK * h, 0))
                        ins.then_inc(filling(key)[0], 1)
                for j in range(NT - 1):
                    pe.wait_ge(to_pe.sem, to_pe.seen_by("pe"))
                    w = (NT - 1 - j) * P
                    for h in range(GH):
                        key = (l, "cross", j, h)
                        if claim(key, h):
                            pe.wait_ge(*room(key))
                        r = slice(GDK * h, GDK * h + GDK)
                        nc.tensor.matmul(PS[:, h, 0:w], work[r, 6 + j % 2, 0:P], work[r, 4 + j % 2, 0:w],
                                                start=True, stop=True, tile_position=(GDK * h, 0))\
                            .then_inc(filling(key)[0], 1)
                for h in range(GH):
                    pe.wait_ge(*emptying((l, "cross", NT - 2, h)))
                for t in range(2):
                    key = (l, "og", t)
                    if claim(key, 4 + t):
                        pe.wait_ge(*room(key))
                    for hh in range(2):
                        h = 2 * t + hh
                        v = proj[:, T["gv0"] + t, :].rearrange("p (n c) -> p n c", c=P)
                        rows = slice(HD * hh, HD * hh + HD)
                        for j in range(NT):
                            vj = v[:, j, hh * HD:(hh + 1) * HD]
                            if j < NT - 1:
                                off = [0, 384, 640][j]
                                w = (NT - 1 - j) * P
                                nc.tensor.matmul(PS[rows, 4 + t, (j + 1) * P:S], vj,
                                                 Ax[:, h, off:off + w], start=j == 0, stop=False)
                            ins = nc.tensor.matmul(PS[rows, 4 + t, j * P:(j + 1) * P], vj,
                                                   Ad[:, h, j, :], start=False, stop=j == NT - 1)
                    ins.then_inc(filling(key)[0], 1)
                for t in range(2):
                    pe.wait_ge(squares.sem, squares.seen_by("pe"))
                    if claim((l, "hn", t), 6):
                        pe.wait_ge(*room((l, "hn", t)))
                    nc.tensor.matmul(PS[:, 6, :], c_("headones"), sq[:, t, :], start=True, stop=True)\
                        .then_inc(filling((l, "hn", t))[0], 1)

                pe.wait_ge(to_pe.sem, to_pe.seen_by("pe"))
                for t in range(2):
                    key = (l, "sg", t)
                    if claim(key, t):
                        pe.wait_ge(*room(key))
                    v = proj[:, T["sv0"] + t, :].rearrange("p (n c) -> p n c", c=P)
                    for hh in range(2):
                        for n in range(NT):
                            ins = nc.tensor.matmul(PS[HD * hh:HD * hh + HD, t, n * P:(n + 1) * P], v[:, n, hh * HD:(hh + 1) * HD],
                                                   m_("swt")[:, (2 * t + hh) * P:(2 * t + hh + 1) * P], start=True, stop=True)
                    ins.then_inc(filling(key)[0], 1)

                pe.wait_ge(h_lo.sem, h_lo.seen_by("pe", 4))
                pe.wait_ge(*emptying((l, "O", HEADS // 2 - 1)))
                for m in range(KT):
                    gemm((l, "out", m), m % 4, a_hi, a_lo)

                for c in range(FCH):
                    for f in range(FT):
                        if c == 0 and f == 0:
                            normed_gemm((l, "ss2"), (l, "g", c, f), f % 2)
                        else:
                            gemm((l, "g", c, f), f % 2, a_hi, a_lo)
                        gemm((l, "u", c, f), 2 + f % 2, a_hi, a_lo)
                    pe.wait_ge(h_lo.sem, h_lo.seen_by("pe", FT))
                    for m in range(KT):
                        gemm((l, "d", c, m), 4 + m % 3, f_hi, f_lo, n=FT)

            for key in ("n1", "n2"):
                for k in range(KT):
                    stats_step((key,), k)
            pe.wait_ge(h_lo.sem, h_lo.seen_by("pe", KT))
            for m in range(KT):
                gemm(("xa", m), m % 4, a_hi, a_lo)
            gb = 0
            for g in range(4):
                for j in range(2):
                    gemm(("za", 2 * g + j), gb % 4, a_hi, a_lo)
                    gb += 1
                for part in "qkvz":
                    for j in range(2):
                        gemm((part, 2 * g + j), gb % 4, a_hi, a_lo)
                        gb += 1
                for j in range(2):
                    t = 2 * g + j
                    pe.wait_ge(rgw_in, 16 * (t + 1))
                    if t == 0:
                        pe.wait_ge(to_pe.sem, to_pe.seen_by("pe"))
                    for m in range(4):
                        if claim(("rg", t, m), m):
                            pe.wait_ge(*room(("rg", t, m)))
                        ins = nc.tensor.matmul(PS[:, m, :], rgw[:, m, :], xc[:, t, :], start=True, stop=True)
                        ins.then_inc(filling(("rg", t, m))[0], 1)
                for j in range(2):
                    t = 2 * g + j
                    pe.wait_ge(*emptying(("v", t)))
                    pe.wait_ge(*emptying(("k", t)))
                    pe.wait_ge(*emptying(("q", t)))
                    for half in range(2):
                        if claim(("vT", t, half), 4 + half):
                            pe.wait_ge(*room(("vT", t, half)))
                        for n in range(4):
                            i, c = 2 * half + n // 2, n % 2
                            k0 = LOW[i] * ROWS + c * P
                            src = qkv[:, 4 + j, k0:k0 + P]
                            ins = nc.tensor.transpose(PS[:, 4 + half, n * P:(n + 1) * P], src, ident)
                        ins.then_inc(filling(("vT", t, half))[0], 1)
                    for hh in range(2):
                        h = 2 * t + hh
                        p0 = HD * hh
                        for half in range(2):
                            if claim(("S2", h, half), half):
                                pe.wait_ge(*room(("S2", h, half)))
                            for n in range(2):
                                i = 2 * half + n
                                ins = nc.tensor.matmul(PS[:, half, n * 256:(n + 1) * 256], qkv[p0:p0 + HD, j, i * P:(i + 1) * P],
                                                       qkv[p0:p0 + HD, 2 + j, LOW[i] * ROWS:(LOW[i] + KC) * ROWS], start=True, stop=True)
                            ins.then_inc(filling(("S2", h, half))[0], 1)
                        pe.wait_ge(diag_ok.sem, diag_ok.seen_by("pe"))
                        for half in range(2):
                            if claim(("PT2", h, half), 2 + half):
                                pe.wait_ge(*room(("PT2", h, half)))
                            for n in range(4):
                                i, c = 2 * half + n // 2, n % 2
                                ins = nc.tensor.matmul(PS[:, 2 + half, n * P:(n + 1) * P], P2[:, i, c * P:(c + 1) * P],
                                                       dg2[:, i, :], start=True, stop=True)
                            ins.then_inc(filling(("PT2", h, half))[0], 1)
                        if hh == 0:
                            if claim(("O2", t), 6):
                                pe.wait_ge(*room(("O2", t)))
                            for half in range(2):
                                pe.wait_ge(*emptying(("vT", t, half)))
                        for half in range(2):
                            pe.wait_ge(*emptying(("PT2", h, half)))
                            for n in range(4):
                                i, c = 2 * half + n // 2, n % 2
                                ins = nc.tensor.matmul(PS[p0:p0 + HD, 6, i * P:(i + 1) * P], vW[:, 2 * i + c, p0:p0 + HD],
                                                       PT2[:, i, c * P:(c + 1) * P], start=c == 0, stop=c == 1)
                        if hh == 1:
                            ins.then_inc(filling(("O2", t))[0], 1)
                        else:
                            ins.then_inc(pv_done.sem, 1)
                            pv_done.raised()
            for m in range(KT):
                gemm(("ga", m), m % 4, a_hi, a_lo)
                if m == 0:
                    pe.wait_ge(h_lo.sem, h_lo.seen_by("pe", KT))
                gemm(("pa", m), 4 + m % 2, y_hi, y_lo)
            pe.wait_ge(h_lo.sem, h_lo.seen_by("pe", KT))
            for m in range(KT):
                gemm(("pb", m), 4 + m % 2, y_hi, y_lo)
                gemm(("gb", m), m % 4, a_hi, a_lo)
            pe.wait_ge(h_lo.sem, h_lo.seen_by("pe", KT))
            for m in range(KT):
                gemm(("wo", m), m % 4, a_hi, a_lo)
            for k in range(KT):
                stats_step(("n3",), k)

        def pv_finished(eng, l, u):
            if u % (2 * NT) == 2 * NT - 1:
                eng.wait_ge(*filling((l, "O", u // (2 * NT))))
            else:
                eng.wait_ge(pv_done.sem, l * 28 + u // 8 * 7 + u % 8 + 1)

        A_ID = ACT.Identity

        def by_row(ap):
            return ap.rearrange("p (r c) -> p r c", c=GRID)

        def by_column(ap):
            return ap.rearrange("p (c r) -> p r c", r=ROWS)

        def load_bias(eng, t):
            for hh in range(2):
                for c in range(QC):
                    first = RPB_PAD + (2 * t + hh) * 15 * 31 - c - 1
                    src = bass.AP(a_rpb.tensor, first, [[31, ROWS], [31, ROWS], [1, RW]])
                    eng.dma_start(bias[c * ROWS:(c + 1) * ROWS, 2 * (t % 2) + hh, :, :], src)\
                       .then_inc(bias_in[t % 2], 16)

        GDK_SCALE = GDK ** -0.5
        OFF = [0, 384, 640]

        @block.scalar
        def _(act):
            A = nc.scalar.activation

            def inverse_rms(key, n, dst=None, src=None):
                act.wait_ge(*filling(key))
                d = rstd[:, :] if dst is None else dst
                A(d, PS[:, 7, :] if src is None else src, ACT.Ln, scale=1.0 / n, bias=epst[:, 0:1])\
                    .then_inc(emptied(key), 1)
                act.wait_ge(*emptying(key))

            def norm(key, gain, made_by):
                for k in range(KT):
                    if made_by:
                        act.wait_ge(*emptying(made_by(k)))
                    A(a_hi[:, k, :], x[:, k, :], ACT.Copy, scale=gain[:, k:k + 1]).then_inc(h_hi.sem, 1)
                    act.wait_ge(h_hi.sem, h_hi.raised())
                    square(k)
                inverse_rms(key, D)
                A(rstd[:, :], rstd[:, :], ACT.Exp, scale=-0.5).then_inc(rstd_ok.sem, 1)
                act.wait_ge(rstd_ok.sem, rstd_ok.raised())

            def square(k):
                if k >= 2:
                    act.wait_ge(sq_used.sem, sq_used.seen_by("act"))
                A(sq[:, k % 2, :], x[:, k, :], ACT.Square).then_inc(squares.sem, 1)
                act.wait_ge(squares.sem, squares.raised())
                if k == KT - 1:
                    act.wait_ge(sq_used.sem, sq_used.seen_by("act"))

            act.dma_start(const[:, :], a_const).then_inc(const_in, 16)
            act.dma_start(vec[:, :], a_vec).then_inc(const_in, 16)
            act.dma_start(misc[:, :], a_misc[0]).then_inc(misc_in, 16)
            act.wait_ge(const_in, 32)
            act.wait_ge(eps_ok.sem, eps_ok.seen_by("act"))
            A(csil[:, :], v_("c"), ACT.Silu).then_inc(act_chain.sem, 1)
            act.wait_ge(act_chain.sem, act_chain.raised())
            A(c_hi[:, :], csil[:, :], ACT.Copy).then_inc(to_dve.sem, 1)
            act.wait_ge(to_dve.sem, to_dve.raised())
            A(lam_z[:, :], v_("lam"), ACT.Abs).then_inc(act_chain.sem, 1)
            act.wait_ge(act_chain.sem, act_chain.raised())
            A(lam_z[:, :], lam_z[:, :], ACT.Exp, scale=-1.0).then_inc(to_dve.sem, 1)
            act.wait_ge(to_dve.sem, to_dve.raised())

            for l in range(DEPTH):
                if l == 0:
                    act.wait_ge(x_in, 16 * KT)
                act.wait_ge(misc_in, 16 * (l + 1))
                norm((l, "ss"), m_("g_attn"),
                     (lambda k: (l - 1, "d", FCH - 1, k)) if l else None)

                def further(name):
                    t = T.get(name)
                    if name in ("vsl", "vwn", "gv0", "gv1"):
                        act.wait_ge(*filling((l, name, "T")))
                        A(proj[:, t, :], PS[:, uses[(l, name, "T")][0], :], ACT.Copy)\
                            .then_inc(emptied((l, name, "T")), 1)
                        act.wait_ge(*emptying((l, name, "T")))
                    elif name in ("sv0", "sv1"):
                        act.wait_ge(*filling((l, name, "T")))
                        A(proj[:, t, :], PS[:, uses[(l, name, "T")][0], :], ACT.Gelu_apprx_tanh)\
                            .then_inc(emptied((l, name, "T")), 1)
                        act.wait_ge(*emptying((l, name, "T")))
                    elif name == "gate":
                        act.wait_ge(*filling((l, name, "T")))
                        A(gN[:, :, :], PS[:, uses[(l, name, "T")][0], 0:NT * 24].rearrange("p (n c) -> p n c", c=24), ACT.Sigmoid)\
                            .then_inc(emptied((l, name, "T")), 1)
                        act.wait_ge(*emptying((l, name, "T")))
                    elif name in ("kc", "vc"):
                        act.wait_ge(to_act.sem, to_act.seen_by("act"))
                        A(X_hi[:, :, :], X, ACT.Copy).then_inc(to_dve.sem, 1)
                        act.wait_ge(to_dve.sem, to_dve.raised())
                    elif name == "CV":
                        act.wait_ge(*filling((l, "vc2")))
                        A(vcn[0:NC, :], PS[0:NC, uses[(l, "vc2")][0], 0:GROUPS * HD], ACT.Copy)\
                            .then_inc(emptied((l, "vc2")), 1)
                        act.wait_ge(*emptying((l, "vc2")))

                for idx, name in enumerate(ORDER):
                    if name in ("CK", "CV"):
                        for m in range(2):
                            act.wait_ge(*filling((l, name, m)))
                            A(hid[:, int(name == "CV"), m, :], PS[:, uses[(l, name, m)][0], 0:2 * NC], ACT.Gelu_apprx_tanh)\
                                .then_inc(emptied((l, name, m)), 1)
                            act.wait_ge(*emptying((l, name, m)))
                    if idx >= LAG:
                        further(ORDER[idx - LAG])
                for name in ORDER[-LAG:]:
                    further(name)

                U = HEADS * NT

                def exps(u):
                    i, par = u % NT, u % 2
                    w = (i + 1) * P
                    act.wait_ge(max_ok.sem, max_ok.seen_by("act"))
                    for br in range(2):
                        A(work[:, 2 * par + br, 0:w], PS[:, 2 * par + br, 0:w], ACT.Exp,
                                       bias=nmax[:, par, br:br + 1], accum_out=sums[:, par, br:br + 1])\
                            .then_inc(emptied((l, "S", br, u)), 1)
                        act.wait_ge(*emptying((l, "S", br, u)))

                def compressed_exps(h):
                    act.wait_ge(maxc_ok.sem, maxc_ok.seen_by("act"))
                    for i in range(NT):
                        ins = A(Pc[:, h % 2, i, 0:NC], PS[:, 7, i * 32:i * 32 + NC], ACT.Exp,
                                bias=nmaxc[:, h % 2, i:i + 1], accum_out=sumsc[:, h % 2, i:i + 1])
                        if i < NT - 1:
                            ins.then_inc(act_chain.sem, 1)
                            act.wait_ge(act_chain.sem, act_chain.raised())
                        else:
                            ins.then_inc(emptied((l, "Sc", h)), 1)
                            act.wait_ge(*emptying((l, "Sc", h)))

                compressed_exps(0)
                exps(0)
                exps(1)
                for u in range(U):
                    i, par = u % NT, u % 2
                    if u >= 2:
                        pv_finished(act, l, u - 2)
                    act.wait_ge(*filling((l, "PT", 0, u)))
                    A(work[:, 4 + 2 * par, 0:(i + 1) * P], PS[:, 4, 0:(i + 1) * P], ACT.Copy)\
                        .then_inc(emptied((l, "PT", 0, u)), 1)
                    act.wait_ge(*emptying((l, "PT", 0, u)))
                    if u + 2 < U:
                        exps(u + 2)
                    if i == 0 and u // NT + 1 < HEADS:
                        compressed_exps(u // NT + 1)
                    if u % 8 == 0 and u:
                        t = u // 8 - 1
                        act.wait_ge(*filling((l, "O", t)))
                        A(a_hi[:, t, :], PS[:, 6, :], ACT.Copy).then_inc(h_hi.sem, 1)
                        act.wait_ge(h_hi.sem, h_hi.raised())
                act.wait_ge(*filling((l, "O", HEADS // 2 - 1)))
                A(a_hi[:, HEADS // 2 - 1, :], PS[:, 6, :], ACT.Copy).then_inc(h_hi.sem, 1)
                act.wait_ge(h_hi.sem, h_hi.raised())

                act.wait_ge(to_act.sem, to_act.seen_by("act"))
                A(work[:, 1, :], work[:, 0, :], ACT.Abs).then_inc(act_chain.sem, 1)
                act.wait_ge(act_chain.sem, act_chain.raised())
                A(work[:, 1, :], work[:, 1, :], ACT.Exp, scale=-1.0).then_inc(act_chain.sem, 1)
                act.wait_ge(act_chain.sem, act_chain.raised())
                A(work[:, 1, :], work[:, 1, :], ACT.Ln, bias=1.0).then_inc(to_dve.sem, 1)
                act.wait_ge(to_dve.sem, to_dve.raised())
                for lv in range(7):
                    act.wait_ge(to_act.sem, to_act.seen_by("act"))
                    e = work[:, 2 + lv % 2, :]
                    A(e, e, ACT.Abs).then_inc(act_chain.sem, 1)
                    act.wait_ge(act_chain.sem, act_chain.raised())
                    A(e, e, ACT.Exp, scale=-1.0 / TAU).then_inc(to_dve.sem, 1)
                    act.wait_ge(to_dve.sem, to_dve.raised())
                act.wait_ge(to_act.sem, to_act.seen_by("act"))
                for j in range(NT - 1):
                    w = (NT - 1 - j) * P
                    eq = work[:, 2 + j, 0:w] if j < 2 else work[:, 1, 3 * P:4 * P]
                    A(eq, work[:, 0, (j + 1) * P:S], ACT.Exp, scale=1.0 / TAU, bias=small[:, j:j + 1])\
                        .then_inc(act_chain.sem, 1)
                    act.wait_ge(act_chain.sem, act_chain.raised())
                    A(work[:, 1, j * P:(j + 1) * P], work[:, 0, j * P:(j + 1) * P], ACT.Exp,
                                     scale=-1.0 / TAU, bias=small[:, 4 + j:5 + j]).then_inc(to_dve.sem, 1)
                    act.wait_ge(to_dve.sem, to_dve.raised())
                for j in range(NT - 1):
                    w = (NT - 1 - j) * P
                    for h in range(GH):
                        act.wait_ge(*filling((l, "cross", j, h)))
                        A(Ax[:, h, OFF[j]:OFF[j] + w], PS[:, h, 0:w], ACT.Copy)\
                            .then_inc(emptied((l, "cross", j, h)), 1)
                        act.wait_ge(*emptying((l, "cross", j, h)))
                for t in range(2):
                    act.wait_ge(*filling((l, "og", t)))
                    A(sq[:, t, :], PS[:, 4 + t, :], ACT.Square).then_inc(squares.sem, 1)
                    act.wait_ge(squares.sem, squares.raised())
                for t in range(2):
                    act.wait_ge(*filling((l, "hn", t)))
                    A(work[:, 2 + t, :], PS[:, 6, :], ACT.Ln, scale=1.0 / GDV, bias=epst[:, 0:1])\
                        .then_inc(emptied((l, "hn", t)), 1)
                    act.wait_ge(*emptying((l, "hn", t)))
                    A(work[:, 2 + t, :], work[:, 2 + t, :], ACT.Exp, scale=-0.5).then_inc(to_dve.sem, 1)
                    act.wait_ge(to_dve.sem, to_dve.raised())
                for t in range(2):
                    g = proj[:, T["gr0"] + t, :]
                    A(g, g, ACT.Silu).then_inc(to_dve.sem, 1)
                    act.wait_ge(to_dve.sem, to_dve.raised())
                for t in range(2):
                    act.wait_ge(to_act.sem, to_act.seen_by("act"))
                    A(a_hi[:, 4 + t, :], work[:, 4 + t, :], ACT.Copy).then_inc(h_hi.sem, 1)
                    act.wait_ge(h_hi.sem, h_hi.raised())
                act.wait_ge(to_act.sem, to_act.seen_by("act"))
                A(small[:, 48:52], small[:, 33:40:2], ACT.Ln, bias=epst[:, 0:1]).then_inc(act_chain.sem, 1)
                act.wait_ge(act_chain.sem, act_chain.raised())
                A(small[:, 48:52], small[:, 48:52], ACT.Exp, scale=-0.5).then_inc(to_dve.sem, 1)
                act.wait_ge(to_dve.sem, to_dve.raised())
                for t in range(2):
                    u_ = proj[:, T["su0"] + t, :]
                    A(u_, u_, ACT.Gelu_apprx_tanh).then_inc(to_dve.sem, 1)
                    act.wait_ge(to_dve.sem, to_dve.raised())
                for t in range(2):
                    act.wait_ge(to_act.sem, to_act.seen_by("act"))
                    A(a_hi[:, 6 + t, :], work[:, 6 + t, :], ACT.Copy).then_inc(h_hi.sem, 1)
                    act.wait_ge(h_hi.sem, h_hi.raised())

                for k in range(KT):
                    act.wait_ge(*filling((l, "out", k)))
                norm((l, "ss2"), m_("g_ffn"), lambda k: (l, "out", k))
                if l + 1 < DEPTH:
                    act.wait_ge(misc_free.sem, misc_free.seen_by("act"))
                    act.dma_start(misc[:, :], a_misc[l + 1]).then_inc(misc_in, 16)
                for c in range(FCH):
                    for f in range(FT + 1):
                        if f < FT:
                            act.wait_ge(to_act.sem, to_act.seen_by("act"))
                            A(work[:, f % 2, :], work[:, f % 2, :], ACT.Silu).then_inc(to_dve.sem, 1)
                            act.wait_ge(to_dve.sem, to_dve.raised())
                        if f > 0:
                            act.wait_ge(to_act.sem, to_act.seen_by("act"))
                            A(f_hi[:, f - 1, :], work[:, 4 + (f - 1) % 2, :], ACT.Copy).then_inc(h_hi.sem, 1)
                            act.wait_ge(h_hi.sem, h_hi.raised())

            for k in range(KT):
                act.wait_ge(*emptying((DEPTH - 1, "d", FCH - 1, k)))
                square(k)
            inverse_rms(("n1",), D)
            A(rstd[:, :], rstd[:, :], ACT.Exp, scale=-0.5).then_inc(rstd_ok.sem, 1)
            act.wait_ge(rstd_ok.sem, rstd_ok.raised())
            for k in range(KT):
                act.wait_ge(x_ok.sem, x_ok.seen_by("act"))
                square(k)
            inverse_rms(("n2",), D)
            A(rstd[:, :], rstd[:, :], ACT.Exp, scale=-0.5).then_inc(rstd_ok.sem, 1)
            act.wait_ge(rstd_ok.sem, rstd_ok.raised())
            act.dma_start(rgw[:, :, :], a_rgw[0]).then_inc(rgw_in, 16)
            for t in range(2):
                load_bias(act, t)
            for k in range(KT):
                act.wait_ge(to_act.sem, to_act.seen_by("act"))
                A(a_hi[:, k, :], xc[:, k, :], A_ID, bias=modv[:, k:k + 1]).then_inc(h_hi.sem, 1)
                act.wait_ge(h_hi.sem, h_hi.raised())

            for g in range(4):
                for j in range(2):
                    t = 2 * g + j
                    if g:
                        pass
                    act.wait_ge(*filling(("za", t)))
                    A(sq[:, j, :], PS[:, uses[("za", t)][0], :], ACT.Silu)\
                        .then_inc(emptied(("za", t)), 1)
                    act.wait_ge(*emptying(("za", t)))
                for j in range(2):
                    t = 2 * g + j
                    act.wait_ge(*filling(("k", t)))
                    A(by_column(qkv[:, 2 + j, :]), by_row(PS[:, uses[("k", t)][0], :]), ACT.Copy)\
                        .then_inc(emptied(("k", t)), 1)
                    act.wait_ge(*emptying(("k", t)))
                for j in range(2):
                    t = 2 * g + j
                    act.wait_ge(*filling(("v", t)))
                    A(by_column(qkv[:, 4 + j, :]), by_row(PS[:, uses[("v", t)][0], :]), ACT.Copy)\
                        .then_inc(emptied(("v", t)), 1)
                    act.wait_ge(*emptying(("v", t)))
                for j in range(2):
                    t = 2 * g + j
                    act.wait_ge(*filling(("z", t)))
                    A(yb[:, t, :], PS[:, uses[("z", t)][0], :], ACT.Silu)\
                        .then_inc(emptied(("z", t)), 1)
                    act.wait_ge(*emptying(("z", t)))
                for j in range(2):
                    t = 2 * g + j
                    for m in range(4):
                        col = VEC["b_gate"][0] + m * KT + t
                        act.wait_ge(*filling(("rg", t, m)))
                        A(rg[:, m, :], PS[:, m, :], ACT.Sigmoid, bias=vec[:, col:col + 1])\
                            .then_inc(emptied(("rg", t, m)), 1)
                        act.wait_ge(*emptying(("rg", t, m)))
                    if t + 1 < KT:
                        act.dma_start(rgw[:, :, :], a_rgw[t + 1]).then_inc(rgw_in, 16)
                    for d in range(2):
                        lc = d * KT + t
                        A(rg[:, 4 + d, :], rg[:, 2 * d, :], ACT.Tanh, scale=lam_p[:, lc:lc + 1])\
                            .then_inc(act_chain.sem, 1)
                        act.wait_ge(act_chain.sem, act_chain.raised())
                    for d in range(2):
                        lc = d * KT + t
                        A(rg[:, 2 * d, :], rg[:, 2 * d, :], ACT.Exp, scale=lam_n[:, lc:lc + 1])\
                            .then_inc(to_dve.sem, 1)
                        act.wait_ge(to_dve.sem, to_dve.raised())
                    for d in range(2):
                        act.wait_ge(to_act.sem, to_act.seen_by("act"))
                        A(rg[:, 4 + d, :], rg[:, 4 + d, :], ACT.Sqrt, scale=2.0).then_inc(to_dve.sem, 1)
                        act.wait_ge(to_dve.sem, to_dve.raised())
                    act.wait_ge(to_act.sem, to_act.seen_by("act"))
                    A(y_hi[:, t, :], tmp[:, :], ACT.Copy).then_inc(h_hi.sem, 1)
                    act.wait_ge(h_hi.sem, h_hi.raised())
                for j in range(2):
                    t = 2 * g + j
                    if t:
                        act.wait_ge(*filling(("O2", t - 1)))
                    act.wait_ge(*filling(("vT", t, 0)))
                    A(vW[:, 0:4, :], PS[:, 4, :].rearrange("p (n c) -> p n c", c=P), ACT.Copy)\
                        .then_inc(emptied(("vT", t, 0)), 1)
                    act.wait_ge(*emptying(("vT", t, 0)))
                    for hh in range(2):
                        h = 2 * t + hh
                        act.wait_ge(max_ok.sem, max_ok.seen_by("act"))
                        for i in range(4):
                            ins = A(P2[:, i, :], P2[:, i, :], ACT.Exp, bias=sm2[:, i:i + 1], accum_out=sm2[:, 4 + i:5 + i])
                            ins.then_inc(exp_ok.sem, 1)
                            act.wait_ge(exp_ok.sem, exp_ok.raised())
                        if hh == 0 and t:
                            pass
                        if hh == 1:
                            act.wait_ge(pv_done.sem, 56 + t + 1)
                        act.wait_ge(*filling(("PT2", h, 0)))
                        A(PT2[:, 0:2, :], PS[:, 2, :].rearrange("p (n c) -> p n c", c=256), ACT.Copy)\
                            .then_inc(emptied(("PT2", h, 0)), 1)
                        act.wait_ge(*emptying(("PT2", h, 0)))
                    if t + 2 < KT:
                        load_bias(act, t + 2)
            for m in range(KT):
                if m >= 2:
                    act.wait_ge(*emptying(("pa", m - 2)))
                act.wait_ge(*filling(("ga", m)))
                A(rg[:, m % 2, :], PS[:, uses[("ga", m)][0], :], ACT.Sigmoid)\
                    .then_inc(emptied(("ga", m)), 1)
                act.wait_ge(*emptying(("ga", m)))
            act.wait_ge(*filling(("pa", KT - 1)))
            for t in range(KT):
                if t == KT - 1:
                    act.wait_ge(*emptying(("O2", t)))
                A(y_hi[:, t, :], yb[:, t, :], ACT.Copy).then_inc(h_hi.sem, 1)
                act.wait_ge(h_hi.sem, h_hi.raised())
            for m in range(KT):
                if m >= 2:
                    act.wait_ge(*emptying(("pb", m - 2)))
                act.wait_ge(*filling(("gb", m)))
                A(rg[:, 2 + m % 2, :], PS[:, uses[("gb", m)][0], :], ACT.Sigmoid)\
                    .then_inc(emptied(("gb", m)), 1)
                act.wait_ge(*emptying(("gb", m)))
            for m in range(KT):
                act.wait_ge(to_act.sem, to_act.seen_by("act"))
                A(a_hi[:, m, :], xc[:, m, :], ACT.Copy).then_inc(h_hi.sem, 1)
                act.wait_ge(h_hi.sem, h_hi.raised())
            for k in range(KT):
                act.wait_ge(*emptying(("wo", k)))
                square(k)
            inverse_rms(("n3",), D)
            A(rstd[:, :], rstd[:, :], ACT.Exp, scale=-0.5).then_inc(rstd_ok.sem, 1)
            act.wait_ge(rstd_ok.sem, rstd_ok.raised())

        @block.vector
        def _(dve):
            V = nc.vector
            TT, TS, STT, CP = V.tensor_tensor, V.tensor_scalar, V.scalar_tensor_tensor, V.tensor_copy

            V.memset(epst[:, :], EPS).then_inc(eps_ok.sem, 1)
            dve.wait_ge(eps_ok.sem, eps_ok.raised())
            dve.wait_ge(const_in, 32)
            dve.wait_ge(to_dve.sem, to_dve.seen_by("dve"))
            TT(c_lo[:, :], csil[:, :], c_hi[:, :].bitcast(F32), ALU.subtract).then_inc(c_ready.sem, 1)
            dve.wait_ge(c_ready.sem, c_ready.raised())
            dve.wait_ge(to_dve.sem, to_dve.seen_by("dve"))
            TS(lam_s[:, :], lam_z[:, :], 2.0, None, ALU.add).then_inc(dve_chain.sem, 1)
            dve.wait_ge(dve_chain.sem, dve_chain.raised())
            V.reciprocal(lam_s[:, :], lam_s[:, :]).then_inc(dve_chain.sem, 1)
            dve.wait_ge(dve_chain.sem, dve_chain.raised())
            TT(lam_s[:, :], lam_s[:, :], lam_z[:, :], ALU.mult).then_inc(dve_chain.sem, 1)
            dve.wait_ge(dve_chain.sem, dve_chain.raised())
            TT(lam_q[:, :], lam_s[:, :], lam_s[:, :], ALU.mult).then_inc(dve_chain.sem, 1)
            dve.wait_ge(dve_chain.sem, dve_chain.raised())
            TS(lam_p[:, :], lam_q[:, :], 1.0 / 15, 1.0 / 13, ALU.mult, ALU.add).then_inc(dve_chain.sem, 1)
            dve.wait_ge(dve_chain.sem, dve_chain.raised())
            for k in (11, 9, 7, 5, 3, 1):
                TT(lam_p[:, :], lam_p[:, :], lam_q[:, :], ALU.mult).then_inc(dve_chain.sem, 1)
                dve.wait_ge(dve_chain.sem, dve_chain.raised())
                TS(lam_p[:, :], lam_p[:, :], 1.0 / k, None, ALU.add).then_inc(dve_chain.sem, 1)
                dve.wait_ge(dve_chain.sem, dve_chain.raised())
            TT(lam_p[:, :], lam_p[:, :], lam_s[:, :], ALU.mult).then_inc(dve_chain.sem, 1)
            dve.wait_ge(dve_chain.sem, dve_chain.raised())
            TS(lam_n[:, :], v_("lam"), -1.0, 0.0, ALU.mult, ALU.max).then_inc(dve_chain.sem, 1)
            dve.wait_ge(dve_chain.sem, dve_chain.raised())
            STT(lam_p[:, :], lam_p[:, :], 2.0, lam_n[:, :], ALU.mult, ALU.add).then_inc(dve_chain.sem, 1)
            dve.wait_ge(dve_chain.sem, dve_chain.raised())
            TS(lam_p[:, :], lam_p[:, :], RG_C, None, ALU.mult).then_inc(dve_chain.sem, 1)
            dve.wait_ge(dve_chain.sem, dve_chain.raised())
            TS(lam_n[:, :], lam_p[:, :], -1.0, None, ALU.mult).then_inc(dve_chain.sem, 1)
            dve.wait_ge(dve_chain.sem, dve_chain.raised())

            def windows(r, b, h):
                ap = PS[r, b, h:h + 1].unsqueeze(2).to_broadcast([HD, 16, NC])
                return bass.AP(ap.tensor, ap.offset, [list(ap.ap[0]), [2, 16], [CMP_STRIDE, NC]])

            def norm(gain):
                for k in range(KT):
                    dve.wait_ge(h_hi.sem, h_hi.seen_by("dve"))
                    STT(a_lo[:, k, :], x[:, k, :], gain[:, k:k + 1], a_hi[:, k, :].bitcast(F32),
                                     ALU.mult, ALU.subtract).then_inc(h_lo.sem, 1)
                    dve.wait_ge(h_lo.sem, h_lo.raised())
                dve.wait_ge(rstd_ok.sem, rstd_ok.seen_by("dve"))

            for l in range(DEPTH):
                dve.wait_ge(misc_in, 16 * (l + 1))
                norm(m_("g_attn"))

                def further(name):
                    t = T.get(name)
                    if name in ("kc", "vc"):
                        pos = m_("pos_k" if name == "kc" else "pos_v")
                        for g in range(GROUPS):
                            key = (l, name, "dup", g)
                            dve.wait_ge(*filling(key))
                            b = uses[key][0]
                            for h in range(2):
                                r = slice(HD * h, HD * h + HD)
                                src = windows(r, b, h)
                                ins = TT(X[r, :, g * NC:(g + 1) * NC], src,
                                         pos[r, :].unsqueeze(2).to_broadcast([HD, 16, NC]), ALU.add)
                                if h == 0:
                                    ins.then_inc(dve_chain.sem, 1)
                                    dve.wait_ge(dve_chain.sem, dve_chain.raised())
                                else:
                                    ins.then_inc(emptied(key), 1)
                                    dve.wait_ge(*emptying(key))
                        CP(small[:, 63:64], epst[:, :]).then_inc(to_act.sem, 1)
                        dve.wait_ge(to_act.sem, to_act.raised())
                        dve.wait_ge(to_dve.sem, to_dve.seen_by("dve"))
                        if name == "vc":
                            dve.wait_ge(*filling((l, "CK", 1)))
                        TT(X_lo[:, :, :], X, X_hi[:, :, :].bitcast(F32), ALU.subtract).then_inc(to_pe.sem, 1)
                        dve.wait_ge(to_pe.sem, to_pe.raised())
                    elif name in ("ksl", "kwn"):
                        for g in range(GROUPS):
                            kd, kr = (l, name, "dup", g), (l, name, "rot", g)
                            dst = keys[:, int(name == "kwn"), g, :]
                            dve.wait_ge(*filling(kd))
                            TT(dst, PS[:, uses[kd][0], :], c_("cos"), ALU.mult).then_inc(emptied(kd), 1)
                            dve.wait_ge(*emptying(kd))
                            dve.wait_ge(*filling(kr))
                            TT(tmp[:, :], PS[:, uses[kr][0], :], c_("sin"), ALU.mult).then_inc(emptied(kr), 1)
                            dve.wait_ge(*emptying(kr))
                            TT(dst, dst, tmp[:, :], ALU.add).then_inc(roped.sem, 1)
                            dve.wait_ge(roped.sem, roped.raised())
                    elif name[0] == "q":
                        key = (l, name, "rot")
                        dve.wait_ge(*filling(key))
                        q = proj[:, t, :]
                        STT(tmp[:, :], PS[:, uses[key][0], :], HD ** -0.5, c_("sin"), ALU.mult, ALU.mult)\
                            .then_inc(emptied(key), 1)
                        dve.wait_ge(*emptying(key))
                        STT(q, q, HD ** -0.5, c_("cos"), ALU.mult, ALU.mult).then_inc(dve_chain.sem, 1)
                        dve.wait_ge(dve_chain.sem, dve_chain.raised())
                        TT(q, q, tmp[:, :], ALU.add).then_inc(roped.sem, 1)
                        dve.wait_ge(roped.sem, roped.raised())
                    elif name == "gate":
                        dve.wait_ge(*emptying((l, "gate", "T")))
                        g = gN[:, 0, 2:24:3]
                        TS(g, g, c_("rowok"), None, ALU.mult).then_inc(dve_chain.sem, 1)
                        dve.wait_ge(dve_chain.sem, dve_chain.raised())
                    elif name == "CK":
                        dve.wait_ge(*filling((l, "kc2")))
                        CP(kc0[:, :], PS[:, uses[(l, "kc2")][0], 0:2 * NC]).then_inc(emptied((l, "kc2")), 1)
                        dve.wait_ge(*emptying((l, "kc2")))
                        dve.wait_ge(*filling((l, "kc2rot")))
                        TT(kcr[:, :], PS[:, uses[(l, "kc2rot")][0], 0:2 * NC], c_("sinc"), ALU.mult)\
                            .then_inc(emptied((l, "kc2rot")), 1)
                        dve.wait_ge(*emptying((l, "kc2rot")))
                        TT(tmp[:, 0:2 * NC], kc0[:, :], c_("cosc"), ALU.mult).then_inc(dve_chain.sem, 1)
                        dve.wait_ge(dve_chain.sem, dve_chain.raised())
                        TT(kcr[:, :], kcr[:, :], tmp[:, 0:2 * NC], ALU.add).then_inc(roped.sem, 1)
                        dve.wait_ge(roped.sem, roped.raised())

                for idx, name in enumerate(ORDER):
                    if name not in ("CK", "CV"):
                        dve.wait_ge(*filling((l, name)))
                        TT(proj[:, T[name], :], PS[:, uses[(l, name)][0], :], rstd[:, :], ALU.mult)\
                            .then_inc(emptied((l, name)), 1)
                        dve.wait_ge(*emptying((l, name)))
                    if idx >= LAG:
                        further(ORDER[idx - LAG])
                for name in ORDER[-LAG:]:
                    further(name)

                U = HEADS * NT
                cm = c_("cmask").rearrange("p (n c) -> p n c", c=NC)

                def maxima(u):
                    i, par = u % NT, u % 2
                    w = (i + 1) * P
                    for br in range(2):
                        dve.wait_ge(*filling((l, "S", br, u)))
                    s2 = PS[:, 2 * par:2 * par + 2, :]
                    TT(s2[:, :, i * P:w], s2[:, :, i * P:w], c_("causal").unsqueeze(1).to_broadcast([P, 2, P]), ALU.add)\
                        .then_inc(dve_chain.sem, 1)
                    dve.wait_ge(dve_chain.sem, dve_chain.raised())
                    V.tensor_reduce(nmax[:, par, 0:2], s2[:, :, 0:w], AX.X, ALU.max, negate=True)\
                        .then_inc(max_ok.sem, 1)
                    dve.wait_ge(max_ok.sem, max_ok.raised())

                def compressed_maxima(h):
                    dve.wait_ge(*filling((l, "Sc", h)))
                    sc = PS[:, 7, 0:NT * 32].rearrange("p (n c) -> p n c", c=32)[:, :, 0:NC]
                    TT(sc, sc, cm, ALU.add).then_inc(dve_chain.sem, 1)
                    dve.wait_ge(dve_chain.sem, dve_chain.raised())
                    V.tensor_reduce(nmaxc[:, h % 2, :], sc, AX.X, ALU.max, negate=True).then_inc(maxc_ok.sem, 1)
                    dve.wait_ge(maxc_ok.sem, maxc_ok.raised())

                def compressed_diagonals(h):
                    dve.wait_ge(*emptying((l, "Sc", h)))
                    V.reciprocal(r3[:, 0:NT], sumsc[:, h % 2, :]).then_inc(dve_chain.sem, 1)
                    dve.wait_ge(dve_chain.sem, dve_chain.raised())
                    TT(r3[:, 0:NT], r3[:, 0:NT], gN[:, :, h * BR + 2], ALU.mult).then_inc(dve_chain.sem, 1)
                    dve.wait_ge(dve_chain.sem, dve_chain.raised())
                    for i in range(NT):
                        ins = TS(diagc[:, i, :], ident, r3[:, i:i + 1], None, ALU.mult)
                        if i < NT - 1:
                            ins.then_inc(dve_chain.sem, 1)
                            dve.wait_ge(dve_chain.sem, dve_chain.raised())
                        else:
                            ins.then_inc(diagc_ok.sem, 1)
                            dve.wait_ge(diagc_ok.sem, diagc_ok.raised())

                def compressed_turned(h):
                    dve.wait_ge(*filling((l, "PTc", h)))
                    CP(PTc[0:NC, h % 2, :], PS[0:NC, 7, :]).then_inc(emptied((l, "PTc", h)), 1)
                    dve.wait_ge(*emptying((l, "PTc", h)))

                def diagonals(u):
                    h, i, par = u // NT, u % NT, u % 2
                    for br in range(2):
                        dve.wait_ge(*emptying((l, "S", br, u)))
                    V.reciprocal(r3[:, 0:2], sums[:, par, 0:2]).then_inc(dve_chain.sem, 1)
                    dve.wait_ge(dve_chain.sem, dve_chain.raised())
                    TT(r3[:, 0:2], r3[:, 0:2], gN[:, i, h * BR:h * BR + 2], ALU.mult).then_inc(dve_chain.sem, 1)
                    dve.wait_ge(dve_chain.sem, dve_chain.raised())
                    for br in range(2):
                        ins = TS(diag[:, par, br, :], ident, r3[:, br:br + 1], None, ALU.mult)
                        if br == 0:
                            ins.then_inc(dve_chain.sem, 1)
                            dve.wait_ge(dve_chain.sem, dve_chain.raised())
                        else:
                            ins.then_inc(diag_ok.sem, 1)
                            dve.wait_ge(diag_ok.sem, diag_ok.raised())

                compressed_maxima(0)
                maxima(0)
                maxima(1)
                compressed_diagonals(0)
                compressed_turned(0)
                for u in range(U):
                    i, par = u % NT, u % 2
                    diagonals(u)
                    if u >= 2:
                        pv_finished(dve, l, u - 2)
                    dve.wait_ge(*filling((l, "PT", 1, u)))
                    CP(work[:, 5 + 2 * par, 0:(i + 1) * P], PS[:, 5, 0:(i + 1) * P])\
                        .then_inc(emptied((l, "PT", 1, u)), 1)
                    dve.wait_ge(*emptying((l, "PT", 1, u)))
                    if u + 2 < U:
                        maxima(u + 2)
                    h = u // NT
                    if i == 0 and h + 1 < HEADS:
                        compressed_maxima(h + 1)
                    if i == 1 and h + 1 < HEADS:
                        compressed_diagonals(h + 1)
                    if i == 2:
                        key, n = (l, "mod", h), mod_tiles(h)
                        m = l * MOD_PER_LAYER + sum(mod_tiles(k) for k in range(h))
                        dve.wait_ge(*filling(key))
                        TT(modv[:, m:m + n], PS[:, 7, 0:2 * n:2], v_("b_c")[:, m:m + n], ALU.add)\
                            .then_inc(emptied(key), 1)
                        dve.wait_ge(*emptying(key))
                    if i == 3 and h + 1 < HEADS:
                        compressed_turned(h + 1)
                    if u % 8 == 0 and u:
                        t = u // 8 - 1
                        dve.wait_ge(h_hi.sem, h_hi.seen_by("dve"))
                        TT(a_lo[:, t, :], PS[:, 6, :], a_hi[:, t, :].bitcast(F32), ALU.subtract)\
                            .then_inc(emptied((l, "O", t)), 1)
                        dve.wait_ge(*emptying((l, "O", t)))
                t = HEADS // 2 - 1
                dve.wait_ge(h_hi.sem, h_hi.seen_by("dve"))
                TT(a_lo[:, t, :], PS[:, 6, :], a_hi[:, t, :].bitcast(F32), ALU.subtract)\
                    .then_inc(emptied((l, "O", t)), 1)
                dve.wait_ge(*emptying((l, "O", t)))

                B = work[:, 0, :]
                gq, gk = proj[:, T["gq"], :], proj[:, T["gk"], :]
                dve.wait_ge(*filling((l, "z")))
                ins = TS(B, PS[:, uses[(l, "z")][0], :], m_("b_up"), None, ALU.add)
                ins.then_inc(emptied((l, "z")), 1)
                dve.wait_ge(*emptying((l, "z")))
                V.memset(Ad, 0.0).then_inc(to_act.sem, 1)
                dve.wait_ge(to_act.sem, to_act.raised())
                dve.wait_ge(to_dve.sem, to_dve.seen_by("dve"))
                STT(work[:, 2, :], B, 0.0, work[:, 1, :], ALU.min, ALU.subtract).then_inc(dve_chain.sem, 1)
                dve.wait_ge(dve_chain.sem, dve_chain.raised())
                V.tensor_tensor_scan(B, c_("ones")[:, 0:1].to_broadcast([P, S]), work[:, 2, :], 0.0, ALU.mult, ALU.add)\
                    .then_inc(dve_chain.sem, 1)
                dve.wait_ge(dve_chain.sem, dve_chain.raised())

                def distances(lv):
                    s = 64 >> lv
                    bb = B.rearrange("p (n c) -> p n c", c=2 * s)
                    out = work[:, 2 + lv % 2, :].rearrange("p (n c) -> p n c", c=2 * s)
                    n = S // (2 * s)
                    TT(out, bb, bb[:, :, s - 1:s].to_broadcast([P, n, 2 * s]), ALU.subtract).then_inc(to_act.sem, 1)
                    dve.wait_ge(to_act.sem, to_act.raised())

                def gather(lv):
                    for h in range(GH):
                        dve.wait_ge(*filling((l, "lv", lv, h)))
                        mask = c_("levels")[:, lv * P:(lv + 1) * P].bitcast(U32).unsqueeze(1).to_broadcast([P, NT, P])
                        V.copy_predicated(Ad[:, h, :, :], mask, PS[:, h, :].rearrange("p (n c) -> p n c", c=P))\
                            .then_inc(emptied((l, "lv", lv, h)), 1)
                        dve.wait_ge(*emptying((l, "lv", lv, h)))

                distances(0)
                for lv in range(8):
                    if lv + 1 < 7:
                        distances(lv + 1)
                    qd, kd, e = work[:, 4 + lv % 2, :], work[:, 6 + lv % 2, :], work[:, 2 + lv % 2, :]
                    if lv < 7:
                        dve.wait_ge(to_dve.sem, to_dve.seen_by("dve"))
                        STT(qd, gq, GDK_SCALE, e, ALU.mult, ALU.mult).then_inc(dve_chain.sem, 1)
                        dve.wait_ge(dve_chain.sem, dve_chain.raised())
                        TT(kd, gk, e, ALU.mult).then_inc(to_pe.sem, 1)
                        dve.wait_ge(to_pe.sem, to_pe.raised())
                    else:
                        TS(qd, gq, GDK_SCALE, None, ALU.mult).then_inc(dve_chain.sem, 1)
                        dve.wait_ge(dve_chain.sem, dve_chain.raised())
                        CP(kd, gk).then_inc(to_pe.sem, 1)
                        dve.wait_ge(to_pe.sem, to_pe.raised())
                    if lv >= 1:
                        gather(lv - 1)
                gather(7)
                TS(small[:, 0:4], B[:, P - 1:S:P], -1.0 / TAU, None, ALU.mult).then_inc(dve_chain.sem, 1)
                dve.wait_ge(dve_chain.sem, dve_chain.raised())
                TS(small[:, 4:8], B[:, P - 1:S:P], 1.0 / TAU, None, ALU.mult).then_inc(to_act.sem, 1)
                dve.wait_ge(to_act.sem, to_act.raised())
                for j in range(NT - 1):
                    w = (NT - 1 - j) * P
                    dve.wait_ge(to_dve.sem, to_dve.seen_by("dve"))
                    if j == 2:
                        dve.wait_ge(*filling((l, "cross", 0, GH - 1)))
                    eq = work[:, 2 + j, 0:w] if j < 2 else work[:, 1, 3 * P:4 * P]
                    STT(work[:, 4 + j % 2, 0:w], gq[:, (j + 1) * P:S], GDK_SCALE, eq, ALU.mult, ALU.mult)\
                        .then_inc(dve_chain.sem, 1)
                    dve.wait_ge(dve_chain.sem, dve_chain.raised())
                    TT(work[:, 6 + j % 2, 0:P], gk[:, j * P:(j + 1) * P], work[:, 1, j * P:(j + 1) * P], ALU.mult)\
                        .then_inc(to_pe.sem, 1)
                    dve.wait_ge(to_pe.sem, to_pe.raised())
                sv = proj[:, T["sv0"]:T["sv0"] + 2, :].rearrange("p t (n c) -> p t n c", c=P)
                dve.wait_ge(*emptying((l, "sv1", "T")))
                for n in range(NT):
                    V.bn_stats(small[:, 8 + 6 * n:14 + 6 * n], sv[:, :, n, :]).then_inc(dve_chain.sem, 1)
                    dve.wait_ge(dve_chain.sem, dve_chain.raised())
                for n in range(NT):
                    V.bn_aggr(small[:, 32 + 2 * n:34 + 2 * n], small[:, 8 + 6 * n:14 + 6 * n])\
                        .then_inc(dve_chain.sem, 1)
                    dve.wait_ge(dve_chain.sem, dve_chain.raised())
                dve.wait_ge(to_dve.sem, to_dve.seen_by("dve", 2))
                for t in range(2):
                    key = (l, "og", t)
                    dve.wait_ge(*filling(key))
                    STT(work[:, 4 + t, :], PS[:, 4 + t, :], m_("gnorm"), work[:, 2 + t, :], ALU.mult, ALU.mult)\
                        .then_inc(emptied(key), 1)
                    dve.wait_ge(*emptying(key))
                dve.wait_ge(to_dve.sem, to_dve.seen_by("dve", 2))
                for t in range(2):
                    TT(work[:, 4 + t, :], work[:, 4 + t, :], proj[:, T["gr0"] + t, :], ALU.mult)\
                        .then_inc(to_act.sem, 1)
                    dve.wait_ge(to_act.sem, to_act.raised())
                for t in range(2):
                    dve.wait_ge(h_hi.sem, h_hi.seen_by("dve"))
                    TT(a_lo[:, 4 + t, :], work[:, 4 + t, :], a_hi[:, 4 + t, :].bitcast(F32), ALU.subtract)\
                        .then_inc(h_lo.sem, 1)
                    dve.wait_ge(h_lo.sem, h_lo.raised())
                CP(small[:, 62:63], epst[:, :]).then_inc(to_act.sem, 1)
                dve.wait_ge(to_act.sem, to_act.raised())
                dve.wait_ge(to_dve.sem, to_dve.seen_by("dve"))
                for n in range(NT):
                    TS(sv[:, :, n, :], sv[:, :, n, :], small[:, 32 + 2 * n:33 + 2 * n], small[:, 48 + n:49 + n],
                            ALU.subtract, ALU.mult).then_inc(dve_chain.sem, 1)
                    dve.wait_ge(dve_chain.sem, dve_chain.raised())
                for name, op in (("lng", ALU.mult), ("lnb", ALU.add)):
                    tab = m_(name).rearrange("p (t c) -> p t c", c=P).unsqueeze(2).to_broadcast([P, 2, NT, P])
                    TT(sv, sv, tab, op).then_inc(dve_chain.sem, 1)
                    dve.wait_ge(dve_chain.sem, dve_chain.raised())
                sw = m_("swt").rearrange("p (g c) -> p g c", c=P)
                TT(sw, sw, c_("triu").unsqueeze(1).to_broadcast([P, 4, P]), ALU.mult).then_inc(to_pe.sem, 1)
                dve.wait_ge(to_pe.sem, to_pe.raised())
                dve.wait_ge(to_dve.sem, to_dve.seen_by("dve", 2))
                for t in range(2):
                    key = (l, "sg", t)
                    dve.wait_ge(*filling(key))
                    wv = work[:, 6 + t, :]
                    TT(wv.rearrange("p (n c) -> p n c", c=P), PS[:, t, :].rearrange("p (n c) -> p n c", c=P),
                                    m_("sgb")[:, t * P:(t + 1) * P].unsqueeze(1).to_broadcast([P, NT, P]), ALU.add)\
                        .then_inc(emptied(key), 1)
                    dve.wait_ge(*emptying(key))
                    TT(wv, wv, proj[:, T["su0"] + t, :], ALU.mult).then_inc(to_act.sem, 1)
                    dve.wait_ge(to_act.sem, to_act.raised())
                for t in range(2):
                    dve.wait_ge(h_hi.sem, h_hi.seen_by("dve"))
                    TT(a_lo[:, 6 + t, :], work[:, 6 + t, :], a_hi[:, 6 + t, :].bitcast(F32), ALU.subtract)\
                        .then_inc(h_lo.sem, 1)
                    dve.wait_ge(h_lo.sem, h_lo.raised())

                for m in range(KT):
                    key = (l, "out", m)
                    dve.wait_ge(*filling(key))
                    TT(x[:, m, :], PS[:, uses[key][0], :], x[:, m, :], ALU.add).then_inc(emptied(key), 1)
                    dve.wait_ge(*emptying(key))

                norm(m_("g_ffn"))
                if l + 1 < DEPTH:
                    CP(small[:, 61:62], epst[:, :]).then_inc(misc_free.sem, 1)
                    dve.wait_ge(misc_free.sem, misc_free.raised())
                for c in range(FCH):
                    for f in range(FT + 1):
                        if f < FT:
                            for kind, b0, w0, sig in (("g", 0, 0, None), ("u", 2, 2, None)):
                                key = (l, kind, c, f)
                                dve.wait_ge(*filling(key))
                                TT(work[:, w0 + f % 2, :], PS[:, b0 + f % 2, :], rstd[:, :], ALU.mult)\
                                    .then_inc(emptied(key), 1)
                                dve.wait_ge(*emptying(key))
                                if kind == "g":
                                    CP(small[:, 60:61], epst[:, :]).then_inc(to_act.sem, 1)
                                    dve.wait_ge(to_act.sem, to_act.raised())
                        if f > 0:
                            k = f - 1
                            dve.wait_ge(to_dve.sem, to_dve.seen_by("dve"))
                            TT(work[:, 4 + k % 2, :], work[:, k % 2, :], work[:, 2 + k % 2, :], ALU.mult)\
                                .then_inc(to_act.sem, 1)
                            dve.wait_ge(to_act.sem, to_act.raised())
                            dve.wait_ge(h_hi.sem, h_hi.seen_by("dve"))
                            TT(f_lo[:, k, :], work[:, 4 + k % 2, :], f_hi[:, k, :].bitcast(F32), ALU.subtract)\
                                .then_inc(h_lo.sem, 1)
                            dve.wait_ge(h_lo.sem, h_lo.raised())
                    for m in range(KT):
                        key = (l, "d", c, m)
                        dve.wait_ge(*filling(key))
                        TT(x[:, m, :], PS[:, uses[key][0], :], x[:, m, :], ALU.add).then_inc(emptied(key), 1)
                        dve.wait_ge(*emptying(key))

            dve.wait_ge(rstd_ok.sem, rstd_ok.seen_by("dve"))
            for k in range(KT):
                STT(x[:, k, :], x[:, k, :], v_("g_fin1")[:, k:k + 1], rstd[:, :], ALU.mult, ALU.mult)\
                    .then_inc(x_ok.sem, 1)
                dve.wait_ge(x_ok.sem, x_ok.raised())
            STT(gainm[:, :], modv[:, KT:2 * KT], 1.0, v_("g_pre"), ALU.add, ALU.mult).then_inc(dve_chain.sem, 1)
            dve.wait_ge(dve_chain.sem, dve_chain.raised())
            dve.wait_ge(rstd_ok.sem, rstd_ok.seen_by("dve"))
            for k in range(KT):
                STT(xc[:, k, :], x[:, k, :], gainm[:, k:k + 1], rstd[:, :], ALU.mult, ALU.mult)\
                    .then_inc(to_act.sem, 1)
                dve.wait_ge(to_act.sem, to_act.raised())
            for k in range(KT):
                dve.wait_ge(h_hi.sem, h_hi.seen_by("dve"))
                STT(a_lo[:, k, :], xc[:, k, :], modv[:, k:k + 1], a_hi[:, k, :].bitcast(F32),
                                 ALU.add, ALU.subtract).then_inc(h_lo.sem, 1)
                dve.wait_ge(h_lo.sem, h_lo.raised())
            V.memset(xpad[:, 0:2], 0.0).then_inc(dve_chain.sem, 1)
            dve.wait_ge(dve_chain.sem, dve_chain.raised())
            V.memset(xpad[:, S + 2:S + 3], 0.0).then_inc(dve_chain.sem, 1)
            dve.wait_ge(dve_chain.sem, dve_chain.raised())
            cw = v_("conv_w")
            for m in range(KT):
                dve.wait_ge(*filling(("xa", m)))
                CP(xpad[:, 2:S + 2], PS[:, m % 4, :]).then_inc(emptied(("xa", m)), 1)
                dve.wait_ge(*emptying(("xa", m)))
                TS(xc[:, m, :], xpad[:, 0:S], cw[:, m:m + 1], v_("conv_b")[:, m:m + 1], ALU.mult, ALU.add)\
                    .then_inc(dve_chain.sem, 1)
                dve.wait_ge(dve_chain.sem, dve_chain.raised())
                for j in range(1, 4):
                    ins = STT(xc[:, m, :], xpad[:, j:j + S], cw[:, j * KT + m:j * KT + m + 1], xc[:, m, :], ALU.mult, ALU.add)
                    if j == 3 and m == KT - 1:
                        ins.then_inc(to_pe.sem, 1)
                        dve.wait_ge(to_pe.sem, to_pe.raised())
                    else:
                        ins.then_inc(dve_chain.sem, 1)
                        dve.wait_ge(dve_chain.sem, dve_chain.raised())
            nm = c_("nmask").rearrange("p (n c) -> p n c", c=KC)
            for g in range(4):
                for j in range(2):
                    t = 2 * g + j
                    dve.wait_ge(*filling(("q", t)))
                    TS(by_column(qkv[:, j, :]), by_row(PS[:, uses[("q", t)][0], :]), HD ** -0.5, None, ALU.mult)\
                        .then_inc(emptied(("q", t)), 1)
                    dve.wait_ge(*emptying(("q", t)))
                for j in range(2):
                    t = 2 * g + j
                    dve.wait_ge(to_dve.sem, to_dve.seen_by("dve", 2))
                    for d in range(2):
                        e = rg[:, 4 + d, :]
                        TS(tmp[:, :], e, 1.0, None, ALU.add).then_inc(dve_chain.sem, 1)
                        dve.wait_ge(dve_chain.sem, dve_chain.raised())
                        V.reciprocal(tmp[:, :], tmp[:, :]).then_inc(dve_chain.sem, 1)
                        dve.wait_ge(dve_chain.sem, dve_chain.raised())
                        TT(e, e, tmp[:, :], ALU.mult).then_inc(to_act.sem, 1)
                        dve.wait_ge(to_act.sem, to_act.raised())
                    for d in range(2):
                        a, i_, e = rg[:, 2 * d, :], rg[:, 2 * d + 1, :], rg[:, 4 + d, :]
                        TT(i_, i_, xc[:, t, :], ALU.mult).then_inc(dve_chain.sem, 1)
                        dve.wait_ge(dve_chain.sem, dve_chain.raised())
                        dve.wait_ge(to_dve.sem, to_dve.seen_by("dve"))
                        TT(i_, i_, e, ALU.mult).then_inc(dve_chain.sem, 1)
                        dve.wait_ge(dve_chain.sem, dve_chain.raised())
                        if d == 0:
                            V.tensor_tensor_scan(e, a, i_, 0.0, ALU.mult, ALU.add).then_inc(dve_chain.sem, 1)
                            dve.wait_ge(dve_chain.sem, dve_chain.raised())
                        else:
                            V.tensor_tensor_scan(e[:, ::-1], a[:, ::-1], i_[:, ::-1], 0.0, ALU.mult, ALU.add)\
                                .then_inc(dve_chain.sem, 1)
                            dve.wait_ge(dve_chain.sem, dve_chain.raised())
                    TT(tmp[:, :], rg[:, 4, :], rg[:, 5, :], ALU.add).then_inc(dve_chain.sem, 1)
                    dve.wait_ge(dve_chain.sem, dve_chain.raised())
                    TT(tmp[:, :], tmp[:, :], sq[:, j, :], ALU.mult).then_inc(to_act.sem, 1)
                    dve.wait_ge(to_act.sem, to_act.raised())
                    dve.wait_ge(h_hi.sem, h_hi.seen_by("dve"))
                    TT(y_lo[:, t, :], tmp[:, :], y_hi[:, t, :].bitcast(F32), ALU.subtract)\
                        .then_inc(h_lo.sem, 1)
                    dve.wait_ge(h_lo.sem, h_lo.raised())
                for j in range(2):
                    t = 2 * g + j
                    dve.wait_ge(*filling(("vT", t, 1)))
                    CP(vW[:, 4:8, :], PS[:, 5, :].rearrange("p (n c) -> p n c", c=P))\
                        .then_inc(emptied(("vT", t, 1)), 1)
                    dve.wait_ge(*emptying(("vT", t, 1)))
                    dve.wait_ge(bias_in[t % 2], 16 * 2 * QC * (t // 2 + 1))
                    for hh in range(2):
                        h = 2 * t + hh
                        for half in range(2):
                            key = ("S2", h, half)
                            dve.wait_ge(*filling(key))
                            for n in range(2):
                                i = 2 * half + n
                                off = LOW[i] - QC * i + QC
                                ins = TT(P2[:, i, :].rearrange("p (c r) -> p r c", r=ROWS),
                                         PS[:, half, n * 256:(n + 1) * 256].rearrange("p (c r) -> p r c", r=ROWS),
                                         bias[:, 2 * (t % 2) + hh, ::-1, off:off + KC], ALU.add)
                                if n:
                                    ins.then_inc(emptied(key), 1)
                                    dve.wait_ge(*emptying(key))
                                else:
                                    ins.then_inc(dve_chain.sem, 1)
                                    dve.wait_ge(dve_chain.sem, dve_chain.raised())
                        p4 = P2[:, :, :].rearrange("p n (c r) -> p n c r", r=ROWS)
                        TT(p4, p4, nm.unsqueeze(3).to_broadcast([P, 4, KC, ROWS]), ALU.add).then_inc(dve_chain.sem, 1)
                        dve.wait_ge(dve_chain.sem, dve_chain.raised())
                        V.tensor_reduce(sm2[:, 0:4], P2[:, :, :], AX.X, ALU.max, negate=True).then_inc(max_ok.sem, 1)
                        dve.wait_ge(max_ok.sem, max_ok.raised())
                        dve.wait_ge(exp_ok.sem, exp_ok.seen_by("dve", 4))
                        V.reciprocal(sm2[:, 8:12], sm2[:, 4:8]).then_inc(dve_chain.sem, 1)
                        dve.wait_ge(dve_chain.sem, dve_chain.raised())
                        for i in range(4):
                            ins = TS(dg2[:, i, :], ident, sm2[:, 8 + i:9 + i], None, ALU.mult)
                            if i < 3:
                                ins.then_inc(dve_chain.sem, 1)
                                dve.wait_ge(dve_chain.sem, dve_chain.raised())
                            else:
                                ins.then_inc(diag_ok.sem, 1)
                                dve.wait_ge(diag_ok.sem, diag_ok.raised())
                        if hh == 1:
                            dve.wait_ge(pv_done.sem, 56 + t + 1)
                        dve.wait_ge(*filling(("PT2", h, 1)))
                        CP(PT2[:, 2:4, :], PS[:, 3, :].rearrange("p (n c) -> p n c", c=256))\
                            .then_inc(emptied(("PT2", h, 1)), 1)
                        dve.wait_ge(*emptying(("PT2", h, 1)))
                    dve.wait_ge(*filling(("O2", t)))
                    dve.wait_ge(*emptying(("z", t)))
                    TT(by_row(yb[:, t, :]), by_column(PS[:, 6, :]), by_row(yb[:, t, :]), ALU.mult)\
                        .then_inc(emptied(("O2", t)), 1)
                    dve.wait_ge(*emptying(("O2", t)))
            for m in range(KT):
                dve.wait_ge(*emptying(("ga", m)))
                dve.wait_ge(*filling(("pa", m)))
                TT(xc[:, m, :], PS[:, 4 + m % 2, :], rg[:, m % 2, :], ALU.mult).then_inc(emptied(("pa", m)), 1)
                dve.wait_ge(*emptying(("pa", m)))
            for t in range(KT):
                dve.wait_ge(h_hi.sem, h_hi.seen_by("dve"))
                TT(y_lo[:, t, :], yb[:, t, :], y_hi[:, t, :].bitcast(F32), ALU.subtract)\
                    .then_inc(h_lo.sem, 1)
                dve.wait_ge(h_lo.sem, h_lo.raised())
            for m in range(KT):
                dve.wait_ge(*emptying(("gb", m)))
                dve.wait_ge(*filling(("pb", m)))
                TT(tmp[:, :], PS[:, 4 + m % 2, :], rg[:, 2 + m % 2, :], ALU.mult).then_inc(emptied(("pb", m)), 1)
                dve.wait_ge(*emptying(("pb", m)))
                TT(xc[:, m, :], xc[:, m, :], tmp[:, :], ALU.add).then_inc(to_act.sem, 1)
                dve.wait_ge(to_act.sem, to_act.raised())
            for m in range(KT):
                dve.wait_ge(h_hi.sem, h_hi.seen_by("dve"))
                TT(a_lo[:, m, :], xc[:, m, :], a_hi[:, m, :].bitcast(F32), ALU.subtract)\
                    .then_inc(h_lo.sem, 1)
                dve.wait_ge(h_lo.sem, h_lo.raised())
            gate = modv[:, 2 * KT:3 * KT]
            for m in range(KT):
                key = ("wo", m)
                dve.wait_ge(*filling(key))
                STT(x[:, m, :], PS[:, m % 4, :], gate[:, m:m + 1], x[:, m, :], ALU.mult, ALU.add)\
                    .then_inc(emptied(key), 1)
                dve.wait_ge(*emptying(key))
            dve.wait_ge(rstd_ok.sem, rstd_ok.seen_by("dve"))
            for k in range(KT):
                STT(xc[:, k, :], x[:, k, :], v_("g_fin2")[:, k:k + 1], rstd[:, :], ALU.mult, ALU.mult)\
                    .then_inc(out_ok.sem, 1)
                dve.wait_ge(out_ok.sem, out_ok.raised())

        @block.gpsimd
        def _(pool):
            G = nc.gpsimd

            def split(r, arrival, used, chain):
                pool.wait_ge(raw_in[r], arrival)
                if used is not None:
                    pool.wait_ge(slot_used, used)
                G.tensor_tensor(w_hi[:, r, :, :], raw[:, r, :, :], ones, ALU.mult).then_inc(pool_chain, 1)
                pool.wait_ge(pool_chain, chain)
                G.tensor_tensor(w_lo[:, r, :, :], raw[:, r, :, :], w_hi[:, r, :, :].bitcast(F32), ALU.subtract)\
                    .then_inc(split_done, 1)

            ones = c_("ones")[:, 0:1].unsqueeze(2).to_broadcast([P, 8, P])
            pool.wait_ge(const_in, 32)
            for r in range(RING):
                split(r, 16, None, r + 1)
            with pool.Fori(1, SLOTS // RING) as i:
                for r in range(RING):
                    split(r, i * 16 + 16, i * RING + (r - RING + 1), i * RING + (r + 1))
            last = SLOTS // RING
            for r in range(SLOTS % RING):
                split(r, 16 * (last + 1), last * RING + r - RING + 1, last * RING + r + 1)

        @block.sync
        def _(sp):
            for k in range(KT):
                sp.dma_start(x[:, k, :], a_x[:, k, :]).then_inc(x_in, 16)
            for r in range(RING):
                sp.dma_start(raw[:, r, :, :], w_sl[r]).then_inc(raw_in[r], 16)
            with sp.Fori(1, SLOTS // RING) as i:
                for r in range(RING):
                    sp.wait_ge(split_done, i * RING + (r - RING + 1))
                    sp.dma_start(raw[:, r, :, :], w_rows[bass.ds((i * RING + r) * P, P), :]).then_inc(raw_in[r], 16)
            last = SLOTS // RING * RING
            for r in range(SLOTS - last):
                sp.wait_ge(split_done, last + r - RING + 1)
                sp.dma_start(raw[:, r, :, :], w_sl[last + r]).then_inc(raw_in[r], 16)
            for k in range(KT):
                sp.wait_ge(out_ok.sem, k + 1)
                sp.dma_start(a_out[:, k, :], xc[:, k, :]).then_inc(out_done, 16)
            sp.wait_ge(out_done, 16 * KT)


def kernel(**inputs):
    import numpy as np
    import concourse.bacc as bacc
    from concourse.bass_utils import run_bass_kernel_spmd

    f32 = np.float32
    a = {k: np.asarray(v) for k, v in inputs.items()}

    const = np.zeros((P, CONST_N), f32)

    def put(name, v):
        const[:, CONST[name][0]:CONST[name][1]] = np.asarray(v, f32).reshape(P, -1)

    p = np.arange(P)
    tok = np.arange(S)
    inv = 1.0 / (10000.0 ** ((p % (HD // 2)).astype(f32) / (HD // 2)))
    put("ident", np.eye(P))
    put("ones", np.ones((P, P)))
    ang = inv[:, None].astype(f32) * tok[None, :].astype(f32)
    put("cos", np.cos(ang))
    put("sin", np.sin(ang))
    ends = np.tile(np.arange(NC) * CMP_STRIDE + CMP_LEN - 1, 2)
    angc = inv[:, None].astype(f32) * ends[None, :].astype(f32)
    put("cosc", np.cos(angc))
    put("sinc", np.sin(angc))
    NEG = -1e30
    put("causal", np.where(p[None, :] <= p[:, None], 0.0, NEG))
    t_of = p[:, None] + P * np.arange(NT)[None, :]
    put("cmask", np.where(ends[None, None, :NC] <= t_of[:, :, None], 0.0, NEG))
    put("rowok", (p >= CMP_LEN - 1).astype(f32))
    rot = np.zeros((P, P))
    for m in range(P):
        if m % HD < HD // 2:
            rot[m + HD // 2, m] = -1.0
        else:
            rot[m - HD // 2, m] = 1.0
    put("rot", rot)
    dup = np.zeros((P, GROUPS, P))
    for g in range(GROUPS):
        dup[g * HD + p % HD, g, p] = 1.0
    put("dup", dup)
    put("rotdup", np.stack([dup_g @ rot for dup_g in dup.transpose(1, 0, 2)], 1))
    put("headones", (p[:, None] // HD == p[None, :] // HD))
    put("triu", p[:, None] <= p[None, :])
    levels = np.zeros((P, 8, P))
    for lv in range(7):
        s = 64 >> lv
        levels[:, lv, :] = ((p[:, None] // (2 * s) == p[None, :] // (2 * s))
                            & (p[:, None] % (2 * s) < s) & (p[None, :] % (2 * s) >= s))
    levels[:, 7, :] = np.eye(P)
    put("levels", levels)
    nmask = np.zeros((P, NT, KC))
    for i in range(NT):
        c = QC * i + p // ROWS
        c0 = np.clip(c - QC // 2, 0, GRID - QC)
        kc = LOW[i] + np.arange(KC)
        nmask[:, i, :] = np.where((kc[None, :] >= c0[:, None]) & (kc[None, :] < c0[:, None] + QC), 0.0, NEG)
    put("nmask", nmask)

    def vecs(v):
        return np.ascontiguousarray(v.reshape(-1, P).T)

    misc = np.zeros((DEPTH, P, MISC_N), f32)
    for l in range(DEPTH):
        def mput(name, v):
            misc[l, :, MISC[name][0]:MISC[name][1]] = v.reshape(P, -1)

        mput("g_attn", vecs(a["attn_norm"][l]))
        mput("g_ffn", vecs(a["ffn_norm"][l]))
        mput("pos_k", vecs(a["cmp_pos_k"][l].reshape(-1)))
        mput("pos_v", vecs(a["cmp_pos_v"][l].reshape(-1)))
        mput("b_up", a["gla_b_up"][l])
        mput("gnorm", np.tile(a["gla_norm"][l], 2))
        w2k = a["cmp_w2_k"][l].reshape(2, P, HD).transpose(1, 0, 2)
        mput("w2k", np.concatenate([w2k, w2k], 2))
        mput("w2v", a["cmp_w2_v"][l].reshape(2, P, HD).transpose(1, 0, 2))
        misc[l, 32:48, MISC["w_up"][0]:MISC["w_up"][1]] = a["gla_w_up"][l]
        mput("swt", a["sg_w"][l].transpose(2, 0, 1))
        mput("lng", np.broadcast_to(a["sg_ln_g"][l], (P, 2 * P)))
        mput("lnb", np.broadcast_to(a["sg_ln_b"][l], (P, 2 * P)))
        mput("sgb", np.repeat(a["sg_b"][l].reshape(2, 2, P), HD, 1).transpose(1, 0, 2))
    vec = np.zeros((P, VEC_N), f32)

    def vput(name, v):
        vec[:, VEC[name][0]:VEC[name][1]] = v.reshape(P, -1)

    vput("g_fin1", vecs(a["final_norm"]))
    vput("c", np.repeat(vecs(a["c_2"][0]), 2, 1))
    vput("b_c", vecs(a["b_c_2"][0]))
    vput("g_pre", vecs(a["g_pre_2"][0]))
    vput("conv_w", vecs(a["conv_w_2"][0].reshape(-1)))
    vput("conv_b", vecs(a["conv_b_2"][0]))
    vput("b_gate", np.concatenate([vecs(a[k][0]) for k in ("b_r_f_2", "b_i_f_2", "b_r_b_2", "b_i_b_2")], 1))
    vput("lam", np.concatenate([vecs(a["lam_f_2"][0]), vecs(a["lam_b_2"][0])], 1))
    vput("g_fin2", vecs(a["g_final_2"]))
    rgw = np.zeros((KT, P, 4, P), f32)
    for m, k in enumerate(("w_r_f_2", "w_i_f_2", "w_r_b_2", "w_i_b_2")):
        w = a[k][0].reshape(KT, 2, HD, HD)
        for hh in range(2):
            rgw[:, HD * hh:HD * hh + HD, m, HD * hh:HD * hh + HD] = w[:, hh]
    rpb = np.zeros(RPB_LEN + 2 * RPB_PAD, f32)
    rpb[RPB_PAD:RPB_PAD + RPB_LEN] = a["rpb_2"][0][:, ::-1].reshape(-1)

    cols = {}
    at = 0
    for name, n in (("q", 512), ("kc", P), ("vc", P), ("ksl", P), ("vsl", P), ("kwn", P), ("vwn", P), ("gts", 24),
                    ("gq", P), ("gk", P), ("gv", 2 * P), ("ga", 16), ("gr", 2 * P), ("su", 2 * P), ("sv", 2 * P)):
        cols[name] = at
        at += n

    def tile(w, c):
        return w[:, c:c + P].reshape(-1, P, P).transpose(1, 0, 2)

    stream = []
    for item in stream_plan():
        kind = item[0]
        if kind == "in":
            w, name = a["w_in"][item[1]], item[2]
            if name == "gate":
                g = w[:, cols["gts"]:cols["gts"] + 24].reshape(D, HEADS, BR)[:, :, [1, 2, 0]].reshape(D, 24)
                wide = np.zeros((D, P), f32)
                wide[:, 0:24] = g
                wide[:, 32:48] = w[:, cols["ga"]:cols["ga"] + 16]
                stream.append(tile(wide, 0))
            else:
                base = name if name in cols else name[:-1]
                n = 0 if name in cols else int(name[-1])
                stream.append(tile(w, cols[base] + n * P))
        elif kind == "cmp":
            w = a["cmp_w1_k" if item[2] == "CK" else "cmp_w1_v"][item[1]]
            m, half = divmod(item[3], 2)
            stream.append(w[half * D:(half + 1) * D, m * P:(m + 1) * P].reshape(8, P, P).transpose(1, 0, 2))
        elif kind == "mod":
            stream.append(tile(a["w_c_2"][0], item[1] * P))
        elif kind == "out":
            stream.append(tile(a["w_out"][item[1]], item[2] * P))
        elif kind in ("gate", "up"):
            stream.append(tile(a["w_gate" if kind == "gate" else "w_up"][item[1]], item[2] * P))
        elif kind == "down":
            l, c, i = item[1:]
            w = a["w_down"][l][c * FT * P:(c + 1) * FT * P].reshape(FT, P, KT, P).transpose(2, 0, 1, 3)
            stream.append(w.reshape(KT * FT, P, P)[8 * i:8 * i + 8].transpose(1, 0, 2))
        elif kind == "in2":
            stream.append(tile(a["w_in_2"][0], item[1] * P))
        else:
            w = a[{"pa": "w_pa_2", "pb": "w_pb_2", "wo": "w_o_2"}[kind]][0]
            stream.append(tile(w, item[1] * P))
    stream = np.stack(stream).reshape(-1, P, 8 * P)

    arrays = {
        "x_t": np.ascontiguousarray(a["x"][0].T.reshape(KT, P, S).transpose(1, 0, 2)),
        "weights": stream, "const": const, "misc": misc, "vec": vec, "rgw": rgw, "rpb": rpb,
    }
    nc = bacc.Bacc("TRN2", target_bir_lowering=False, num_devices=1)
    F32 = mybir.dt.float32
    args = [nc.dram_tensor(k, v.shape, F32, kind="ExternalInput").ap() for k, v in arrays.items()]
    out = nc.dram_tensor("out", (P, KT, S), F32, kind="ExternalOutput").ap()
    build(nc, *args, out)
    r = run_bass_kernel_spmd(nc, [arrays], core_ids=[0])
    y = np.asarray(r.results[0]["out"])
    return np.ascontiguousarray(y.transpose(1, 0, 2).reshape(D, S).T).reshape(1, S, D)
```

```python
import concourse.bass as bass
from concourse import mybir
from contextlib import ExitStack

S, D, P = 512, 1024, 128
DEPTH = 2
KT = D // P
NT = S // P
HD = 64
HEADS, GROUPS, BR = 8, 2, 3
CMP_LEN, CMP_STRIDE = 32, 16
NC = (S - CMP_LEN) // CMP_STRIDE + 1
GH, GDK, GDV = 4, 32, 64
TAU = 16.0
DFF = 2816
FCH = 2
FT = DFF // P // FCH
EPS = 1e-6
NH2, GRID, ROWS = 16, 64, 8
QC, KC = 16, 32
RW = QC + KC
LOW = [0, 8, 24, 32]
RG_C = 8.0
AHEAD = 2

T = {"q0": 0, "q1": 1, "q2": 2, "q3": 3, "ksl": 4, "vsl": 5, "kwn": 6, "vwn": 7, "kc": 8, "vc": 9,
     "gk": 10, "gq": 11, "gv0": 12, "gv1": 13, "gr0": 14, "gr1": 15, "sv0": 16, "sv1": 17,
     "su0": 18, "su1": 19, "gate": 20}
ORDER = ["kc", "gate", "ksl", "vsl", "CK", "vc", "kwn", "vwn", "q0", "q1", "CV", "q2", "q3",
         "gk", "gq", "gv0", "gv1", "gr0", "gr1", "sv0", "sv1", "su0", "su1"]
LAG = 2
MOD_SLOTS = 3 * KT
MOD_PER_LAYER = MOD_SLOTS // DEPTH


def mod_tiles(h):
    return 2 if h < MOD_PER_LAYER - HEADS else 1


CMP_SLOTS = 2 * (CMP_LEN * HD // P) // 8

def columns(fields):
    at, out = 0, {}
    for name, n in fields:
        out[name] = (at, at + n)
        at += n
    return out, at


CONST, CONST_N = columns([
    ("ident", P), ("ones", P), ("nmask", NT * KC), ("cos", S), ("sin", S), ("cosc", 2 * NC), ("sinc", 2 * NC),
    ("causal", P), ("cmask", NT * NC), ("rowok", 1), ("rot", P), ("dup", 2 * P), ("rotdup", 2 * P),
    ("headones", P), ("triu", P), ("levels", 8 * P)])
MISC, MISC_N = columns([
    ("g_attn", KT), ("g_ffn", KT), ("pos_k", 16), ("pos_v", 16), ("b_up", 1), ("gnorm", 1),
    ("w2k", 2 * P), ("w2v", 2 * HD), ("w_up", P), ("swt", 4 * P), ("lng", 2 * P), ("lnb", 2 * P),
    ("sgb", 2 * P)])
VEC, VEC_N = columns([
    ("g_fin1", KT), ("c", 2 * KT), ("b_c", MOD_SLOTS), ("g_pre", KT), ("conv_w", 4 * KT),
    ("conv_b", KT), ("b_gate", 4 * KT), ("lam", 2 * KT), ("g_fin2", KT)])
RPB_PAD = QC
RPB_LEN = NH2 * 15 * 31


def stream_plan():
    out = []
    for l in range(DEPTH):
        for name in ORDER:
            out += [("cmp", l, name, i) for i in range(CMP_SLOTS)] if name in ("CK", "CV") else [("in", l, name)]
        out += [("mod", l * MOD_PER_LAYER + m) for m in range(MOD_PER_LAYER)]
        out += [("out", l, m) for m in range(KT)]
        for c in range(FCH):
            for f in range(FT):
                out += [("gate", l, c * FT + f), ("up", l, c * FT + f)]
            out += [("down", l, c, i) for i in range(FT)]
    out += [("in2", m) for m in range(8)]
    for t in range(KT):
        out += [("in2", part * KT + t) for part in (2, 3, 4, 5, 1)]
    gates = [("in2", 6 * KT + n) for n in range(2 * KT)]
    out += gates[:AHEAD]
    for n in range(2 * KT):
        out += [("pa" if n < KT else "pb", n % KT)] + gates[n + AHEAD:n + AHEAD + 1]
    out += [("wo", m) for m in range(8)]
    return out


def build(nc, a_x, a_w, a_const, a_misc, a_vec, a_rgw, a_rpb, a_out, dbg=None):
    F32, F32R, U32 = mybir.dt.float32, mybir.dt.float32r, mybir.dt.uint32
    ALU, ACT, AX = mybir.AluOpType, mybir.ActivationFunctionType, mybir.AxisListType
    PLAN = stream_plan()
    SLOTS = len(PLAN)
    RING = 4
    assert SLOTS % RING == 2
    ctx = ExitStack()
    with ctx:
        place = [0]

        def at(name, shape, dt, offset):
            return nc.alloc_sbuf_tensor_at(name, shape, dt, offset=offset)

        base = nc.sbuf_base if not callable(nc.sbuf_base) else nc.sbuf_base()
        place[0] = (int(base) + 63) // 64 * 64

        def sb(name, shape, dt=F32):
            n = 4
            for k in shape[1:]:
                n *= k
            t = at(name, shape, dt, place[0])
            place[0] += (n + 31) // 32 * 32
            return t

        def sem(name):
            return ctx.enter_context(nc.semaphore(name))

        x = sb("x", [P, KT, S])
        a_hi = sb("a_hi", [P, KT, S], F32R)
        a_lo = sb("a_lo", [P, KT, S], F32R)
        raw = sb("raw", [P, RING, 8, P])
        w_hi = sb("w_hi", [P, RING, 8, P], F32R)
        w_lo = sb("w_lo", [P, RING, 8, P], F32R)
        const = sb("const", [P, CONST_N])
        tail = place[0] - (CONST_N - CONST["cos"][0]) * 4
        vec = sb("vec", [P, VEC_N])
        rstd = sb("rstd", [P, S])
        tmp = sb("tmp", [P, S])
        sq = sb("sq", [P, 2, S])
        modv = sb("modv", [P, MOD_SLOTS])
        csil = sb("csil", [P, 2 * KT])
        c_hi = sb("c_hi", [P, 2 * KT], F32R)
        c_lo = sb("c_lo", [P, 2 * KT], F32R)
        lam_z = sb("lam_z", [P, 2 * KT])
        lam_s = sb("lam_s", [P, 2 * KT])
        lam_q = sb("lam_q", [P, 2 * KT])
        lam_p = sb("lam_p", [P, 2 * KT])
        lam_n = sb("lam_n", [P, 2 * KT])
        epst = sb("epst", [P, 1])
        gainm = sb("gainm", [P, KT])
        arena = place[0]
        proj = sb("proj", [P, 21, S])
        after = place[0]
        place[0] = arena
        f_hi = sb("f_hi", [P, FT, S], F32R)
        f_lo = sb("f_lo", [P, FT, S], F32R)
        place[0] = max(after, place[0])
        misc = sb("misc", [P, MISC_N])
        keys = sb("keys", [P, 2, GROUPS, S])
        work = sb("work", [P, 8, S])
        X_hi = at("X_hi", [P, 16, 2 * NC], F32R, place[0] - 4 * S * 4)
        X_lo = at("X_lo", [P, 16, 2 * NC], F32R, place[0] - 2 * S * 4)
        hid = sb("hid", [P, 2, 2, 2 * NC])
        kcr = sb("kcr", [P, 2 * NC])
        kc0 = sb("kc0", [P, 2 * NC])
        vcn = sb("vcn", [32, GROUPS * HD])
        gN = sb("gN", [P, NT, 24])
        Pc = sb("Pc", [P, 2, NT, 32])
        PTc = sb("PTc", [32, 2, S])
        diag = sb("diag", [P, 2, 2, P])
        diagc = sb("diagc", [P, NT, P])
        nmaxc = sb("nmaxc", [P, 2, NT])
        sumsc = sb("sumsc", [P, 2, NT])
        nmax = sb("nmax", [P, 2, 4])
        sums = sb("sums", [P, 2, 4])
        r3 = sb("r3", [P, 4])
        small = sb("small", [P, 64])
        end1 = place[0]
        place[0] = arena
        y_hi = sb("y_hi", [P, KT, S], F32R)
        y_lo = sb("y_lo", [P, KT, S], F32R)
        xc = sb("xc", [P, KT, S])
        merged = at("merged", [P, KT, S], F32, place[0])
        qkv = sb("qkv", [P, 2, 3, S])
        rg = sb("rg", [P, 6, S])
        zs = sb("zs", [P, 2, S])
        P2 = sb("P2", [P, 4, 256])
        PT2 = sb("PT2", [P, 4, 256])
        vW = sb("vW", [P, 8, P])
        end2 = place[0]
        place[0] = (tail + 31) // 32 * 32
        xpad = sb("xpad", [P, S + 3])
        rgw = sb("rgw", [P, 4, P])
        bias = sb("bias", [P, 4, ROWS, RW])
        dg2 = sb("dg2", [P, 4, P])
        sm2 = sb("sm2", [P, 12])
        assert place[0] <= tail + (CONST_N - CONST["cos"][0]) * 4
        assert max(end1, end2) <= nc.sbuf_usable_end
        PS = ctx.enter_context(nc.psum_tensor("PS", [P, 8, S], F32))
        rpb_dram = a_rpb

        def gate_tile(n):
            return (zs, sq)[n % 2][:, n // 2 % 2, :]

        def c_(name):
            return const[:, CONST[name][0]:CONST[name][1]]

        def m_(name):
            return misc[:, MISC[name][0]:MISC[name][1]]

        def v_(name):
            return vec[:, VEC[name][0]:VEC[name][1]]

        ident = c_("ident")
        Ad = proj[:, 0:4, :].rearrange("p h (n c) -> p h n c", c=P)
        Ax = proj[:, 4:10, :].rearrange("p a b -> p (a b)").rearrange("p (h c) -> p h c", h=GH)
        X = work[:, 0:2, :].rearrange("p a b -> p (a b)")[:, 0:16 * 2 * NC].rearrange("p (k c) -> p k c", c=2 * NC)

        full = [sem(f"full{b}") for b in range(8)]
        free = [sem(f"free{b}") for b in range(8)]
        fills = [0] * 8
        uses = {}

        class Signal:

            def __init__(self, name):
                self.sem, self.n, self.seen = sem(name), 0, {}

            def raised(self):
                self.n += 1
                return self.n

            def seen_by(self, who, k=1):
                self.seen[who] = self.seen.get(who, 0) + k
                return self.seen[who]

        raw_in = [sem(f"raw_in{r}") for r in range(RING)]
        split_done = sem("split_done")
        slot_used = sem("slot_used")
        const_in = sem("const_in")
        misc_in = sem("misc_in")
        rgw_in = sem("rgw_in")
        bias_in = [sem("bias_in0"), sem("bias_in1")]
        x_in = sem("x_in")
        out_done = sem("out_done")
        pool_chain = sem("pool_chain")
        dve_chain = Signal("dve_chain")
        act_chain = Signal("act_chain")
        h_hi = Signal("h_hi")
        h_lo = Signal("h_lo")
        squares = Signal("squares")
        sq_used = Signal("sq_used")
        rstd_ok = Signal("rstd_ok")
        x_ok = Signal("x_ok")
        roped = Signal("roped")
        to_act = Signal("to_act")
        to_dve = Signal("to_dve")
        to_pe = Signal("to_pe")
        maxc_ok = Signal("maxc_ok")
        max_ok = Signal("max_ok")
        diagc_ok = Signal("diagc_ok")
        diag_ok = Signal("diag_ok")
        pv_done = Signal("pv_done")
        misc_free = Signal("misc_free")
        eps_ok = Signal("eps_ok")
        c_ready = Signal("c_ready")
        out_ok = Signal("out_ok")

        def filling(name):
            b, k = uses[name]
            return full[b], k + 1

        def emptying(name):
            b, k = uses[name]
            return free[b], k + 1

        def room(name):
            b, k = uses[name]
            return free[b], k

        def emptied(name):
            return free[uses[name][0]]

        block = ctx.enter_context(nc.Block())
        w_rows = a_w.rearrange("n p c -> (n p) c")
        w_sl = a_w.rearrange("n p (k c) -> n p k c", c=P)

        @block.tensor
        def _(pe):
            st = {"n": 0, "sub": 0}

            def claim(name, b):
                uses[name] = (b, fills[b])
                fills[b] += 1
                return fills[b] > 1

            def weights():
                if st["sub"] == 0:
                    pe.wait_ge(split_done, st["n"] + 1)
                first = st["sub"] == 0 and st["n"] > 0
                r, k = st["n"] % RING, st["sub"]
                st["sub"] += 1
                if st["sub"] == 8:
                    st["sub"], st["n"] = 0, st["n"] + 1
                return w_hi[:, r, k, :], w_lo[:, r, k, :], first

            def product(out, hi, lo, start, stop):
                wh, wl, first = weights()
                ins = nc.tensor.matmul(out, wh, hi, start=start, stop=False)
                if first:
                    ins.then_inc(slot_used, 1)
                nc.tensor.matmul(out, wh, lo, start=False, stop=False)
                return nc.tensor.matmul(out, wl, hi, start=False, stop=stop)

            def gemm(name, b, hi, lo, n=KT):
                if claim(name, b):
                    pe.wait_ge(*room(name))
                out = PS[:, b, :]
                for k in range(n):
                    ins = product(out, hi[:, k, :], lo[:, k, :], k == 0, k == n - 1)
                ins.then_inc(filling(name)[0], 1)

            def stats_step(key, k):
                if k == 0:
                    if claim(key, 7):
                        pe.wait_ge(*room(key))
                pe.wait_ge(squares.sem, squares.seen_by("pe"))
                ins = nc.tensor.matmul(PS[:, 7, :], c_("ones"), sq[:, k % 2, :], start=k == 0, stop=k == KT - 1)
                if k < KT - 1:
                    ins.then_inc(sq_used.sem, 1)
                    sq_used.raised()
                else:
                    ins.then_inc(filling(key)[0], 1)

            def normed_gemm(key, name, b):
                if claim(name, b):
                    pe.wait_ge(*room(name))
                for k in range(KT):
                    pe.wait_ge(h_lo.sem, h_lo.seen_by("pe"))
                    ins = product(PS[:, b, :], a_hi[:, k, :], a_lo[:, k, :], k == 0, k == KT - 1)
                    if k == KT - 1:
                        ins.then_inc(filling(name)[0], 1)
                    stats_step(key, k)

            aux = [0]

            def aux_bank():
                aux[0] += 1
                return 4 + aux[0] % 3

            def one(name, lhsT, rhs, cols=S, rows=P):
                b = aux_bank()
                if claim(name, b):
                    pe.wait_ge(*room(name))
                nc.tensor.matmul(PS[0:rows, b, 0:cols], lhsT, rhs, start=True, stop=True)\
                    .then_inc(filling(name)[0], 1)

            pe.wait_ge(const_in, 32)
            for l in range(DEPTH):
                gb = 0

                def further(name):
                    t = T.get(name)
                    if name in ("kc", "vc"):
                        pe.wait_ge(*emptying((l, name)))
                        for g in range(GROUPS):
                            one((l, name, "dup", g), c_("dup")[:, g * P:(g + 1) * P], proj[:, t, :])
                    elif name in ("ksl", "kwn"):
                        pe.wait_ge(*emptying((l, name)))
                        for g in range(GROUPS):
                            one((l, name, "dup", g), c_("dup")[:, g * P:(g + 1) * P], proj[:, t, :])
                            one((l, name, "rot", g), c_("rotdup")[:, g * P:(g + 1) * P], proj[:, t, :])
                    elif name[0] == "q":
                        pe.wait_ge(*emptying((l, name)))
                        one((l, name, "rot"), c_("rot"), proj[:, t, :])
                    elif name in ("vsl", "vwn", "gv0", "gv1", "sv0", "sv1", "gate"):
                        pe.wait_ge(*emptying((l, name)))
                        w = 24 if name == "gate" else P
                        b = aux_bank()
                        if claim((l, name, "T"), b):
                            pe.wait_ge(*room((l, name, "T")))
                        for i in range(NT):
                            ins = nc.tensor.transpose(PS[:, b, i * w:(i + 1) * w], proj[0:w, t, i * P:(i + 1) * P],
                                                      ident[0:w, 0:w])
                        ins.then_inc(filling((l, name, "T"))[0], 1)
                    elif name == "CK":
                        pe.wait_ge(*emptying((l, "CK", 1)))
                        b = aux_bank()
                        if claim((l, "kc2"), b):
                            pe.wait_ge(*room((l, "kc2")))
                        for m in range(2):
                            ins = nc.tensor.matmul(PS[:, b, 0:2 * NC], m_("w2k")[:, m * P:(m + 1) * P], hid[:, 0, m, :],
                                                   start=m == 0, stop=m == 1)
                        ins.then_inc(filling((l, "kc2"))[0], 1)
                        pe.wait_ge(*emptying((l, "kc2")))
                        one((l, "kc2rot"), c_("rot"), kc0[:, :], cols=2 * NC)
                    elif name == "CV":
                        pe.wait_ge(*emptying((l, "CV", 1)))
                        b = aux_bank()
                        if claim((l, "vc2"), b):
                            pe.wait_ge(*room((l, "vc2")))
                        for g in range(GROUPS):
                            for m in range(2):
                                ins = nc.tensor.matmul(PS[0:NC, b, g * HD:(g + 1) * HD], hid[:, 1, m, g * NC:(g + 1) * NC],
                                                       m_("w2v")[:, m * HD:(m + 1) * HD], start=m == 0, stop=m == 1)
                        ins.then_inc(filling((l, "vc2"))[0], 1)

                for idx, name in enumerate(ORDER):
                    if idx == 0:
                        normed_gemm((l, "ss"), (l, name), 0)
                        gb = 1
                        pe.wait_ge(misc_in, 16 * (l + 1))
                    elif name in ("CK", "CV"):
                        for m in range(2):
                            key, b = (l, name, m), gb % 4
                            gb += 1
                            if claim(key, b):
                                pe.wait_ge(*room(key))
                            if m == 0:
                                pe.wait_ge(to_pe.sem, to_pe.seen_by("pe"))
                            for k in range(16):
                                ins = product(PS[:, b, 0:2 * NC], X_hi[:, k, :], X_lo[:, k, :], k == 0, k == 15)
                            ins.then_inc(filling(key)[0], 1)
                    else:
                        gemm((l, name), gb % 4, a_hi, a_lo)
                        gb += 1
                    if idx >= LAG:
                        further(ORDER[idx - LAG])
                for name in ORDER[-LAG:]:
                    further(name)

                U = HEADS * NT

                def scores(u):
                    h, i, par = u // NT, u % NT, u % 2
                    p0, g = HD * (h % 2), h // (HEADS // GROUPS)
                    q = proj[p0:p0 + HD, h // 2, i * P:(i + 1) * P]
                    w = (i + 1) * P
                    for br in range(2):
                        key = (l, "S", br, u)
                        if claim(key, 2 * par + br):
                            pe.wait_ge(*room(key))
                        nc.tensor.matmul(PS[:, 2 * par + br, 0:w], q, keys[p0:p0 + HD, br, g, 0:w],
                                                start=True, stop=True).then_inc(filling(key)[0], 1)

                def turn(u):
                    i, par = u % NT, u % 2
                    pe.wait_ge(diag_ok.sem, diag_ok.seen_by("pe"))
                    for br in range(2):
                        key = (l, "PT", br, u)
                        if claim(key, 4 + br):
                            pe.wait_ge(*room(key))
                        for j in range(i + 1):
                            ins = nc.tensor.matmul(PS[:, 4 + br, j * P:(j + 1) * P],
                                                   work[:, 2 * par + br, j * P:(j + 1) * P], diag[:, par, br, :],
                                                   start=True, stop=True)
                        ins.then_inc(filling(key)[0], 1)

                def compressed_scores(h):
                    p0, g = HD * (h % 2), h // (HEADS // GROUPS)
                    key = (l, "Sc", h)
                    if claim(key, 7):
                        pe.wait_ge(*room(key))
                    for i in range(NT):
                        ins = nc.tensor.matmul(PS[:, 7, i * 32:i * 32 + NC], proj[p0:p0 + HD, h // 2, i * P:(i + 1) * P],
                                               kcr[p0:p0 + HD, g * NC:(g + 1) * NC], start=True, stop=True)
                    ins.then_inc(filling(key)[0], 1)

                def turn_compressed(h):
                    pe.wait_ge(diagc_ok.sem, diagc_ok.seen_by("pe"))
                    key = (l, "PTc", h)
                    if claim(key, 7):
                        pe.wait_ge(*room(key))
                    for i in range(NT):
                        ins = nc.tensor.matmul(PS[0:NC, 7, i * P:(i + 1) * P], Pc[:, h % 2, i, 0:NC], diagc[:, i, :],
                                               start=True, stop=True)
                    ins.then_inc(filling(key)[0], 1)

                def values(u):
                    h, i, par = u // NT, u % NT, u % 2
                    p0, g = HD * (h % 2), h // (HEADS // GROUPS)
                    key = (l, "O", h // 2)
                    if u % (2 * NT) == 0:
                        if claim(key, 6):
                            pe.wait_ge(*room(key))
                    out = PS[p0:p0 + HD, 6, i * P:(i + 1) * P]
                    pe.wait_ge(*emptying((l, "PTc", h)))
                    nc.tensor.matmul(out, vcn[0:NC, g * HD:(g + 1) * HD], PTc[0:NC, h % 2, i * P:(i + 1) * P],
                                     start=True, stop=False)
                    for br in range(2):
                        pe.wait_ge(*emptying((l, "PT", br, u)))
                        v = proj[:, T["vsl"] + 2 * br, :].rearrange("p (n c) -> p n c", c=P)
                        for j in range(i + 1):
                            ins = nc.tensor.matmul(out, v[:, j, g * HD:(g + 1) * HD],
                                                   work[:, 4 + 2 * par + br, j * P:(j + 1) * P],
                                                   start=False, stop=br == 1 and j == i)
                    if u % (2 * NT) == 2 * NT - 1:
                        ins.then_inc(filling(key)[0], 1)
                    else:
                        ins.then_inc(pv_done.sem, 1)
                        pv_done.raised()

                def modulation(h):
                    if l == 0 and h == 0:
                        pe.wait_ge(c_ready.sem, 1)
                    if claim((l, "mod", h), 7):
                        pe.wait_ge(*room((l, "mod", h)))
                    for n in range(mod_tiles(h)):
                        for k in range(KT):
                            ins = product(PS[:, 7, 2 * n:2 * n + 2], c_hi[:, 2 * k:2 * k + 2], c_lo[:, 2 * k:2 * k + 2],
                                          k == 0, k == KT - 1)
                    ins.then_inc(filling((l, "mod", h))[0], 1)

                pe.wait_ge(roped.sem, roped.seen_by("pe", 2 * GROUPS + 4 + 1))
                pe.wait_ge(*emptying((l, "vc2")))
                pe.wait_ge(*emptying((l, "vwn", "T")))
                compressed_scores(0)
                scores(0)
                scores(1)
                turn_compressed(0)
                for u in range(U):
                    h, i = u // NT, u % NT
                    turn(u)
                    if u + 2 < U:
                        scores(u + 2)
                    if i == 0 and h + 1 < HEADS:
                        compressed_scores(h + 1)
                    if i == 2:
                        modulation(h)
                    if i == 3 and h + 1 < HEADS:
                        turn_compressed(h + 1)
                    if u >= 1:
                        values(u - 1)
                values(U - 1)

                one((l, "z"), m_("w_up")[32:48, :], proj[32:48, T["gate"], :])
                for lv in range(8):
                    pe.wait_ge(to_pe.sem, to_pe.seen_by("pe"))
                    for h in range(GH):
                        key = (l, "lv", lv, h)
                        if claim(key, h):
                            pe.wait_ge(*room(key))
                        for i in range(NT):
                            r = slice(GDK * h, GDK * h + GDK)
                            ins = nc.tensor.matmul(PS[:, h, i * P:(i + 1) * P], work[r, 6 + lv % 2, i * P:(i + 1) * P],
                                                   work[r, 4 + lv % 2, i * P:(i + 1) * P], start=True, stop=True,
                                                   tile_position=(GDK * h, 0))
                        ins.then_inc(filling(key)[0], 1)
                for j in range(NT - 1):
                    pe.wait_ge(to_pe.sem, to_pe.seen_by("pe"))
                    w = (NT - 1 - j) * P
                    for h in range(GH):
                        key = (l, "cross", j, h)
                        if claim(key, h):
                            pe.wait_ge(*room(key))
                        r = slice(GDK * h, GDK * h + GDK)
                        nc.tensor.matmul(PS[:, h, 0:w], work[r, 6 + j % 2, 0:P], work[r, 4 + j % 2, 0:w],
                                                start=True, stop=True, tile_position=(GDK * h, 0))\
                            .then_inc(filling(key)[0], 1)
                for h in range(GH):
                    pe.wait_ge(*emptying((l, "cross", NT - 2, h)))
                for t in range(2):
                    key = (l, "og", t)
                    if claim(key, 4 + t):
                        pe.wait_ge(*room(key))
                    for hh in range(2):
                        h = 2 * t + hh
                        v = proj[:, T["gv0"] + t, :].rearrange("p (n c) -> p n c", c=P)
                        rows = slice(HD * hh, HD * hh + HD)
                        for j in range(NT):
                            vj = v[:, j, hh * HD:(hh + 1) * HD]
                            if j < NT - 1:
                                off = [0, 384, 640][j]
                                w = (NT - 1 - j) * P
                                nc.tensor.matmul(PS[rows, 4 + t, (j + 1) * P:S], vj,
                                                 Ax[:, h, off:off + w], start=j == 0, stop=False)
                            ins = nc.tensor.matmul(PS[rows, 4 + t, j * P:(j + 1) * P], vj,
                                                   Ad[:, h, j, :], start=False, stop=j == NT - 1)
                    ins.then_inc(filling(key)[0], 1)
                for t in range(2):
                    pe.wait_ge(squares.sem, squares.seen_by("pe"))
                    if claim((l, "hn", t), 6):
                        pe.wait_ge(*room((l, "hn", t)))
                    nc.tensor.matmul(PS[:, 6, :], c_("headones"), sq[:, t, :], start=True, stop=True)\
                        .then_inc(filling((l, "hn", t))[0], 1)

                pe.wait_ge(to_pe.sem, to_pe.seen_by("pe"))
                for t in range(2):
                    key = (l, "sg", t)
                    if claim(key, t):
                        pe.wait_ge(*room(key))
                    v = proj[:, T["sv0"] + t, :].rearrange("p (n c) -> p n c", c=P)
                    for hh in range(2):
                        for n in range(NT):
                            ins = nc.tensor.matmul(PS[HD * hh:HD * hh + HD, t, n * P:(n + 1) * P], v[:, n, hh * HD:(hh + 1) * HD],
                                                   m_("swt")[:, (2 * t + hh) * P:(2 * t + hh + 1) * P], start=True, stop=True)
                    ins.then_inc(filling(key)[0], 1)

                pe.wait_ge(h_lo.sem, h_lo.seen_by("pe", 4))
                pe.wait_ge(*emptying((l, "O", HEADS // 2 - 1)))
                for m in range(KT):
                    gemm((l, "out", m), m % 4, a_hi, a_lo)

                for c in range(FCH):
                    for f in range(FT):
                        if c == 0 and f == 0:
                            normed_gemm((l, "ss2"), (l, "g", c, f), f % 2)
                        else:
                            gemm((l, "g", c, f), f % 2, a_hi, a_lo)
                        gemm((l, "u", c, f), 2 + f % 2, a_hi, a_lo)
                    pe.wait_ge(h_lo.sem, h_lo.seen_by("pe", FT))
                    for m in range(KT):
                        gemm((l, "d", c, m), 4 + m % 3, f_hi, f_lo, n=FT)

            for key in ("n1", "n2"):
                for k in range(KT):
                    stats_step((key,), k)
            pe.wait_ge(h_lo.sem, h_lo.seen_by("pe", KT))
            for m in range(KT):
                gemm(("xa", m), m % 4, a_hi, a_lo)
            gb = 0

            def turn_values(p, half):
                if claim(("vT", p, half), 7):
                    pe.wait_ge(*room(("vT", p, half)))
                for n in range(4):
                    i, c = 2 * half + n // 2, n % 2
                    k0 = LOW[i] * ROWS + c * P
                    ins = nc.tensor.transpose(PS[:, 7, n * P:(n + 1) * P], qkv[:, p % 2, 2, k0:k0 + P], ident)
                ins.then_inc(filling(("vT", p, half))[0], 1)

            def near_scores(h):
                p, p0 = h // 2, HD * (h % 2)
                for half in range(2):
                    if claim(("S2", h, half), 2 + half):
                        pe.wait_ge(*room(("S2", h, half)))
                    for n in range(2):
                        i = 2 * half + n
                        ins = nc.tensor.matmul(PS[:, 2 + half, n * 256:(n + 1) * 256],
                                               qkv[p0:p0 + HD, p % 2, 0, i * P:(i + 1) * P],
                                               qkv[p0:p0 + HD, p % 2, 1, LOW[i] * ROWS:(LOW[i] + KC) * ROWS],
                                               start=True, stop=True)
                    ins.then_inc(filling(("S2", h, half))[0], 1)

            def near_turn(h):
                pe.wait_ge(diag_ok.sem, diag_ok.seen_by("pe"))
                for half in range(2):
                    if claim(("PT2", h, half), 4 + half):
                        pe.wait_ge(*room(("PT2", h, half)))
                    for n in range(4):
                        i, c = 2 * half + n // 2, n % 2
                        ins = nc.tensor.matmul(PS[:, 4 + half, n * P:(n + 1) * P], P2[:, i, c * P:(c + 1) * P],
                                               dg2[:, i, :], start=True, stop=True)
                    ins.then_inc(filling(("PT2", h, half))[0], 1)

            def near_values(h):
                p, p0 = h // 2, HD * (h % 2)
                if h % 2 == 0:
                    if claim(("O2", p), 6):
                        pe.wait_ge(*room(("O2", p)))
                    for half in range(2):
                        pe.wait_ge(*emptying(("vT", p, half)))
                for half in range(2):
                    pe.wait_ge(*emptying(("PT2", h, half)))
                    for n in range(4):
                        i, c = 2 * half + n // 2, n % 2
                        ins = nc.tensor.matmul(PS[p0:p0 + HD, 6, i * P:(i + 1) * P], vW[:, 2 * i + c, p0:p0 + HD],
                                               PT2[:, i, c * P:(c + 1) * P], start=c == 0, stop=c == 1)
                if h % 2 == 0:
                    ins.then_inc(pv_done.sem, 1)
                    pv_done.raised()
                else:
                    ins.then_inc(filling(("O2", p))[0], 1)

            for t in range(KT + 1):
                p = t - 1
                for place_, part in enumerate(("q", "k", "v", "z", "za")):
                    if t < KT:
                        gemm((part, t), gb % 2, a_hi, a_lo)
                        gb += 1
                    elif place_ < AHEAD:
                        gemm(("gate", place_), gb % 2, a_hi, a_lo)
                        gb += 1
                    if p >= 0 and part == "q":
                        pe.wait_ge(*emptying(("q", p)))
                        pe.wait_ge(*emptying(("k", p)))
                        pe.wait_ge(*emptying(("v", p)))
                        turn_values(p, 0)
                        near_scores(2 * p)
                    elif p >= 0 and part == "k":
                        turn_values(p, 1)
                        near_scores(2 * p + 1)
                    elif p >= 0 and part == "v":
                        near_turn(2 * p)
                    elif p >= 0 and part == "z":
                        near_values(2 * p)
                        near_turn(2 * p + 1)
                    elif p >= 0:
                        near_values(2 * p + 1)
                if t < KT:
                    pe.wait_ge(rgw_in, 16 * (t + 1))
                    if t == 0:
                        pe.wait_ge(to_pe.sem, to_pe.seen_by("pe"))
                    for m in range(4):
                        if claim(("rg", t, m), (7, 4, 5, 2)[m]):
                            pe.wait_ge(*room(("rg", t, m)))
                        ins = nc.tensor.matmul(PS[:, uses[("rg", t, m)][0], :], rgw[:, m, :], xc[:, t, :],
                                               start=True, stop=True)
                        ins.then_inc(filling(("rg", t, m))[0], 1)
            pe.wait_ge(h_lo.sem, h_lo.seen_by("pe", KT))
            for n in range(2 * KT):
                if n == KT:
                    pe.wait_ge(h_lo.sem, h_lo.seen_by("pe", KT))
                gemm(("prod", n), 2 + n % 2, y_hi, y_lo)
                if n + AHEAD < 2 * KT:
                    gemm(("gate", n + AHEAD), gb % 2, a_hi, a_lo)
                    gb += 1
            pe.wait_ge(h_lo.sem, h_lo.seen_by("pe", KT))
            for m in range(KT):
                gemm(("wo", m), m % 4, a_hi, a_lo)
            for k in range(KT):
                stats_step(("n3",), k)

        def pv_finished(eng, l, u):
            if u % (2 * NT) == 2 * NT - 1:
                eng.wait_ge(*filling((l, "O", u // (2 * NT))))
            else:
                eng.wait_ge(pv_done.sem, l * 28 + u // 8 * 7 + u % 8 + 1)

        A_ID = ACT.Identity

        def by_row(ap):
            return ap.rearrange("p (r c) -> p r c", c=GRID)

        def by_column(ap):
            return ap.rearrange("p (c r) -> p r c", r=ROWS)

        def load_bias(eng, t):
            for hh in range(2):
                for c in range(QC):
                    first = RPB_PAD + (2 * t + hh) * 15 * 31 - c - 1
                    src = bass.AP(a_rpb.tensor, first, [[31, ROWS], [31, ROWS], [1, RW]])
                    eng.dma_start(bias[c * ROWS:(c + 1) * ROWS, 2 * (t % 2) + hh, :, :], src)\
                       .then_inc(bias_in[t % 2], 16)

        GDK_SCALE = GDK ** -0.5
        OFF = [0, 384, 640]

        @block.scalar
        def _(act):
            A = nc.scalar.activation

            def inverse_rms(key, n, dst=None, src=None):
                act.wait_ge(*filling(key))
                d = rstd[:, :] if dst is None else dst
                A(d, PS[:, 7, :] if src is None else src, ACT.Ln, scale=1.0 / n, bias=epst[:, 0:1])\
                    .then_inc(emptied(key), 1)
                act.wait_ge(*emptying(key))

            def norm(key, gain, made_by):
                for k in range(KT):
                    if made_by:
                        act.wait_ge(*emptying(made_by(k)))
                    A(a_hi[:, k, :], x[:, k, :], ACT.Copy, scale=gain[:, k:k + 1]).then_inc(h_hi.sem, 1)
                    act.wait_ge(h_hi.sem, h_hi.raised())
                    square(k)
                inverse_rms(key, D)
                A(rstd[:, :], rstd[:, :], ACT.Exp, scale=-0.5).then_inc(rstd_ok.sem, 1)
                act.wait_ge(rstd_ok.sem, rstd_ok.raised())

            def square(k):
                if k >= 2:
                    act.wait_ge(sq_used.sem, sq_used.seen_by("act"))
                A(sq[:, k % 2, :], x[:, k, :], ACT.Square).then_inc(squares.sem, 1)
                act.wait_ge(squares.sem, squares.raised())
                if k == KT - 1:
                    act.wait_ge(sq_used.sem, sq_used.seen_by("act"))

            act.dma_start(const[:, :], a_const).then_inc(const_in, 16)
            act.dma_start(vec[:, :], a_vec).then_inc(const_in, 16)
            act.dma_start(misc[:, :], a_misc[0]).then_inc(misc_in, 16)
            act.wait_ge(const_in, 32)
            act.wait_ge(eps_ok.sem, eps_ok.seen_by("act"))
            A(csil[:, :], v_("c"), ACT.Silu).then_inc(act_chain.sem, 1)
            act.wait_ge(act_chain.sem, act_chain.raised())
            A(c_hi[:, :], csil[:, :], ACT.Copy).then_inc(to_dve.sem, 1)
            act.wait_ge(to_dve.sem, to_dve.raised())
            A(lam_z[:, :], v_("lam"), ACT.Abs).then_inc(act_chain.sem, 1)
            act.wait_ge(act_chain.sem, act_chain.raised())
            A(lam_z[:, :], lam_z[:, :], ACT.Exp, scale=-1.0).then_inc(to_dve.sem, 1)
            act.wait_ge(to_dve.sem, to_dve.raised())

            for l in range(DEPTH):
                if l == 0:
                    act.wait_ge(x_in, 16 * KT)
                act.wait_ge(misc_in, 16 * (l + 1))
                norm((l, "ss"), m_("g_attn"),
                     (lambda k: (l - 1, "d", FCH - 1, k)) if l else None)

                def further(name):
                    t = T.get(name)
                    if name in ("vsl", "vwn", "gv0", "gv1"):
                        act.wait_ge(*filling((l, name, "T")))
                        A(proj[:, t, :], PS[:, uses[(l, name, "T")][0], :], ACT.Copy)\
                            .then_inc(emptied((l, name, "T")), 1)
                        act.wait_ge(*emptying((l, name, "T")))
                    elif name in ("sv0", "sv1"):
                        act.wait_ge(*filling((l, name, "T")))
                        A(proj[:, t, :], PS[:, uses[(l, name, "T")][0], :], ACT.Gelu_apprx_tanh)\
                            .then_inc(emptied((l, name, "T")), 1)
                        act.wait_ge(*emptying((l, name, "T")))
                    elif name == "gate":
                        act.wait_ge(*filling((l, name, "T")))
                        A(gN[:, :, :], PS[:, uses[(l, name, "T")][0], 0:NT * 24].rearrange("p (n c) -> p n c", c=24), ACT.Sigmoid)\
                            .then_inc(emptied((l, name, "T")), 1)
                        act.wait_ge(*emptying((l, name, "T")))
                    elif name in ("kc", "vc"):
                        act.wait_ge(to_act.sem, to_act.seen_by("act"))
                        A(X_hi[:, :, :], X, ACT.Copy).then_inc(to_dve.sem, 1)
                        act.wait_ge(to_dve.sem, to_dve.raised())
                    elif name == "CV":
                        act.wait_ge(*filling((l, "vc2")))
                        A(vcn[0:NC, :], PS[0:NC, uses[(l, "vc2")][0], 0:GROUPS * HD], ACT.Copy)\
                            .then_inc(emptied((l, "vc2")), 1)
                        act.wait_ge(*emptying((l, "vc2")))

                for idx, name in enumerate(ORDER):
                    if name in ("CK", "CV"):
                        for m in range(2):
                            act.wait_ge(*filling((l, name, m)))
                            A(hid[:, int(name == "CV"), m, :], PS[:, uses[(l, name, m)][0], 0:2 * NC], ACT.Gelu_apprx_tanh)\
                                .then_inc(emptied((l, name, m)), 1)
                            act.wait_ge(*emptying((l, name, m)))
                    if idx >= LAG:
                        further(ORDER[idx - LAG])
                for name in ORDER[-LAG:]:
                    further(name)

                U = HEADS * NT

                def exps(u):
                    i, par = u % NT, u % 2
                    w = (i + 1) * P
                    act.wait_ge(max_ok.sem, max_ok.seen_by("act"))
                    for br in range(2):
                        A(work[:, 2 * par + br, 0:w], PS[:, 2 * par + br, 0:w], ACT.Exp,
                                       bias=nmax[:, par, br:br + 1], accum_out=sums[:, par, br:br + 1])\
                            .then_inc(emptied((l, "S", br, u)), 1)
                        act.wait_ge(*emptying((l, "S", br, u)))

                def compressed_exps(h):
                    act.wait_ge(maxc_ok.sem, maxc_ok.seen_by("act"))
                    for i in range(NT):
                        ins = A(Pc[:, h % 2, i, 0:NC], PS[:, 7, i * 32:i * 32 + NC], ACT.Exp,
                                bias=nmaxc[:, h % 2, i:i + 1], accum_out=sumsc[:, h % 2, i:i + 1])
                        if i < NT - 1:
                            ins.then_inc(act_chain.sem, 1)
                            act.wait_ge(act_chain.sem, act_chain.raised())
                        else:
                            ins.then_inc(emptied((l, "Sc", h)), 1)
                            act.wait_ge(*emptying((l, "Sc", h)))

                compressed_exps(0)
                exps(0)
                exps(1)
                for u in range(U):
                    i, par = u % NT, u % 2
                    if u >= 2:
                        pv_finished(act, l, u - 2)
                    act.wait_ge(*filling((l, "PT", 0, u)))
                    A(work[:, 4 + 2 * par, 0:(i + 1) * P], PS[:, 4, 0:(i + 1) * P], ACT.Copy)\
                        .then_inc(emptied((l, "PT", 0, u)), 1)
                    act.wait_ge(*emptying((l, "PT", 0, u)))
                    if u + 2 < U:
                        exps(u + 2)
                    if i == 0 and u // NT + 1 < HEADS:
                        compressed_exps(u // NT + 1)
                    if u % 8 == 0 and u:
                        t = u // 8 - 1
                        act.wait_ge(*filling((l, "O", t)))
                        A(a_hi[:, t, :], PS[:, 6, :], ACT.Copy).then_inc(h_hi.sem, 1)
                        act.wait_ge(h_hi.sem, h_hi.raised())
                act.wait_ge(*filling((l, "O", HEADS // 2 - 1)))
                A(a_hi[:, HEADS // 2 - 1, :], PS[:, 6, :], ACT.Copy).then_inc(h_hi.sem, 1)
                act.wait_ge(h_hi.sem, h_hi.raised())

                act.wait_ge(to_act.sem, to_act.seen_by("act"))
                A(work[:, 1, :], work[:, 0, :], ACT.Abs).then_inc(act_chain.sem, 1)
                act.wait_ge(act_chain.sem, act_chain.raised())
                A(work[:, 1, :], work[:, 1, :], ACT.Exp, scale=-1.0).then_inc(act_chain.sem, 1)
                act.wait_ge(act_chain.sem, act_chain.raised())
                A(work[:, 1, :], work[:, 1, :], ACT.Ln, bias=1.0).then_inc(to_dve.sem, 1)
                act.wait_ge(to_dve.sem, to_dve.raised())
                for lv in range(7):
                    act.wait_ge(to_act.sem, to_act.seen_by("act"))
                    e = work[:, 2 + lv % 2, :]
                    A(e, e, ACT.Abs).then_inc(act_chain.sem, 1)
                    act.wait_ge(act_chain.sem, act_chain.raised())
                    A(e, e, ACT.Exp, scale=-1.0 / TAU).then_inc(to_dve.sem, 1)
                    act.wait_ge(to_dve.sem, to_dve.raised())
                act.wait_ge(to_act.sem, to_act.seen_by("act"))
                for j in range(NT - 1):
                    w = (NT - 1 - j) * P
                    eq = work[:, 2 + j, 0:w] if j < 2 else work[:, 1, 3 * P:4 * P]
                    A(eq, work[:, 0, (j + 1) * P:S], ACT.Exp, scale=1.0 / TAU, bias=small[:, j:j + 1])\
                        .then_inc(act_chain.sem, 1)
                    act.wait_ge(act_chain.sem, act_chain.raised())
                    A(work[:, 1, j * P:(j + 1) * P], work[:, 0, j * P:(j + 1) * P], ACT.Exp,
                                     scale=-1.0 / TAU, bias=small[:, 4 + j:5 + j]).then_inc(to_dve.sem, 1)
                    act.wait_ge(to_dve.sem, to_dve.raised())
                for j in range(NT - 1):
                    w = (NT - 1 - j) * P
                    for h in range(GH):
                        act.wait_ge(*filling((l, "cross", j, h)))
                        A(Ax[:, h, OFF[j]:OFF[j] + w], PS[:, h, 0:w], ACT.Copy)\
                            .then_inc(emptied((l, "cross", j, h)), 1)
                        act.wait_ge(*emptying((l, "cross", j, h)))
                for t in range(2):
                    act.wait_ge(*filling((l, "og", t)))
                    A(sq[:, t, :], PS[:, 4 + t, :], ACT.Square).then_inc(squares.sem, 1)
                    act.wait_ge(squares.sem, squares.raised())
                for t in range(2):
                    act.wait_ge(*filling((l, "hn", t)))
                    A(work[:, 2 + t, :], PS[:, 6, :], ACT.Ln, scale=1.0 / GDV, bias=epst[:, 0:1])\
                        .then_inc(emptied((l, "hn", t)), 1)
                    act.wait_ge(*emptying((l, "hn", t)))
                    A(work[:, 2 + t, :], work[:, 2 + t, :], ACT.Exp, scale=-0.5).then_inc(to_dve.sem, 1)
                    act.wait_ge(to_dve.sem, to_dve.raised())
                for t in range(2):
                    g = proj[:, T["gr0"] + t, :]
                    A(g, g, ACT.Silu).then_inc(to_dve.sem, 1)
                    act.wait_ge(to_dve.sem, to_dve.raised())
                for t in range(2):
                    act.wait_ge(to_act.sem, to_act.seen_by("act"))
                    A(a_hi[:, 4 + t, :], work[:, 4 + t, :], ACT.Copy).then_inc(h_hi.sem, 1)
                    act.wait_ge(h_hi.sem, h_hi.raised())
                act.wait_ge(to_act.sem, to_act.seen_by("act"))
                A(small[:, 48:52], small[:, 33:40:2], ACT.Ln, bias=epst[:, 0:1]).then_inc(act_chain.sem, 1)
                act.wait_ge(act_chain.sem, act_chain.raised())
                A(small[:, 48:52], small[:, 48:52], ACT.Exp, scale=-0.5).then_inc(to_dve.sem, 1)
                act.wait_ge(to_dve.sem, to_dve.raised())
                for t in range(2):
                    u_ = proj[:, T["su0"] + t, :]
                    A(u_, u_, ACT.Gelu_apprx_tanh).then_inc(to_dve.sem, 1)
                    act.wait_ge(to_dve.sem, to_dve.raised())
                for t in range(2):
                    act.wait_ge(to_act.sem, to_act.seen_by("act"))
                    A(a_hi[:, 6 + t, :], work[:, 6 + t, :], ACT.Copy).then_inc(h_hi.sem, 1)
                    act.wait_ge(h_hi.sem, h_hi.raised())

                for k in range(KT):
                    act.wait_ge(*filling((l, "out", k)))
                norm((l, "ss2"), m_("g_ffn"), lambda k: (l, "out", k))
                if l + 1 < DEPTH:
                    act.wait_ge(misc_free.sem, misc_free.seen_by("act"))
                    act.dma_start(misc[:, :], a_misc[l + 1]).then_inc(misc_in, 16)
                for c in range(FCH):
                    for f in range(FT + 1):
                        if f < FT:
                            act.wait_ge(to_act.sem, to_act.seen_by("act"))
                            A(work[:, f % 2, :], work[:, f % 2, :], ACT.Silu).then_inc(to_dve.sem, 1)
                            act.wait_ge(to_dve.sem, to_dve.raised())
                        if f > 0:
                            act.wait_ge(to_act.sem, to_act.seen_by("act"))
                            A(f_hi[:, f - 1, :], work[:, 4 + (f - 1) % 2, :], ACT.Copy).then_inc(h_hi.sem, 1)
                            act.wait_ge(h_hi.sem, h_hi.raised())

            for k in range(KT):
                act.wait_ge(*emptying((DEPTH - 1, "d", FCH - 1, k)))
                square(k)
            inverse_rms(("n1",), D)
            A(rstd[:, :], rstd[:, :], ACT.Exp, scale=-0.5).then_inc(rstd_ok.sem, 1)
            act.wait_ge(rstd_ok.sem, rstd_ok.raised())
            for k in range(KT):
                act.wait_ge(x_ok.sem, x_ok.seen_by("act"))
                square(k)
            inverse_rms(("n2",), D)
            A(rstd[:, :], rstd[:, :], ACT.Exp, scale=-0.5).then_inc(rstd_ok.sem, 1)
            act.wait_ge(rstd_ok.sem, rstd_ok.raised())
            act.dma_start(rgw[:, :, :], a_rgw[0]).then_inc(rgw_in, 16)
            for t in range(2):
                load_bias(act, t)
            for k in range(KT):
                act.wait_ge(to_act.sem, to_act.seen_by("act"))
                A(a_hi[:, k, :], xc[:, k, :], A_ID, bias=modv[:, k:k + 1]).then_inc(h_hi.sem, 1)
                act.wait_ge(h_hi.sem, h_hi.raised())

            def near_exps(h):
                act.wait_ge(max_ok.sem, max_ok.seen_by("act"))
                if h:
                    for half in range(2):
                        act.wait_ge(*filling(("PT2", h - 1, half)))
                for i in range(4):
                    ins = A(P2[:, i, :], PS[:, 2 + i // 2, i % 2 * 256:(i % 2 + 1) * 256], ACT.Exp,
                            bias=sm2[:, i:i + 1], accum_out=sm2[:, 4 + i:5 + i])
                    if i % 2:
                        ins.then_inc(emptied(("S2", h, i // 2)), 1)
                        act.wait_ge(*emptying(("S2", h, i // 2)))
                    else:
                        ins.then_inc(act_chain.sem, 1)
                        act.wait_ge(act_chain.sem, act_chain.raised())

            def near_turned(h):
                if h % 2:
                    act.wait_ge(pv_done.sem, 56 + h // 2 + 1)
                act.wait_ge(*filling(("PT2", h, 0)))
                A(PT2[:, 0:2, :], PS[:, 4, :].rearrange("p (n c) -> p n c", c=256), ACT.Copy)\
                    .then_inc(emptied(("PT2", h, 0)), 1)
                act.wait_ge(*emptying(("PT2", h, 0)))

            def merging_gate(n):
                if n >= 4:
                    act.wait_ge(*emptying(("prod", n - 4)))
                act.wait_ge(*filling(("gate", n)))
                A(gate_tile(n), PS[:, uses[("gate", n)][0], :], ACT.Sigmoid).then_inc(emptied(("gate", n)), 1)
                act.wait_ge(*emptying(("gate", n)))

            for t in range(KT + 1):
                p = t - 1
                if p >= 0:
                    if p:
                        act.wait_ge(*filling(("O2", p - 1)))
                    act.wait_ge(*filling(("vT", p, 0)))
                    A(vW[:, 0:4, :], PS[:, 7, :].rearrange("p (n c) -> p n c", c=P), ACT.Copy)\
                        .then_inc(emptied(("vT", p, 0)), 1)
                    act.wait_ge(*emptying(("vT", p, 0)))
                    near_exps(2 * p)
                if t < KT:
                    for part, name in ((1, "k"), (2, "v")):
                        act.wait_ge(*filling((name, t)))
                        A(by_column(qkv[:, t % 2, part, :]), by_row(PS[:, uses[(name, t)][0], :]), ACT.Copy)\
                            .then_inc(emptied((name, t)), 1)
                        act.wait_ge(*emptying((name, t)))
                if p >= 0:
                    near_turned(2 * p)
                    near_exps(2 * p + 1)
                    for d in range(2):
                        act.wait_ge(to_act.sem, to_act.seen_by("act"))
                        A(rg[:, 4 + d, :], rg[:, 4 + d, :], ACT.Sqrt, scale=2.0).then_inc(to_dve.sem, 1)
                        act.wait_ge(to_dve.sem, to_dve.raised())
                if t < KT:
                    if t >= 2:
                        act.wait_ge(*emptying(("O2", t - 2)))
                    act.wait_ge(*filling(("z", t)))
                    A(zs[:, t % 2, :], PS[:, uses[("z", t)][0], :], ACT.Silu)\
                        .then_inc(emptied(("z", t)), 1)
                    act.wait_ge(*emptying(("z", t)))
                if p >= 0:
                    near_turned(2 * p + 1)
                    act.wait_ge(to_act.sem, to_act.seen_by("act"))
                    A(y_hi[:, p, :], tmp[:, :], ACT.Copy).then_inc(h_hi.sem, 1)
                    act.wait_ge(h_hi.sem, h_hi.raised())
                if t < KT:
                    act.wait_ge(*filling(("za", t)))
                    A(sq[:, t % 2, :], PS[:, uses[("za", t)][0], :], ACT.Silu)\
                        .then_inc(emptied(("za", t)), 1)
                    act.wait_ge(*emptying(("za", t)))
                    for m in range(4):
                        col = VEC["b_gate"][0] + m * KT + t
                        act.wait_ge(*filling(("rg", t, m)))
                        A(rg[:, m, :], PS[:, uses[("rg", t, m)][0], :], ACT.Sigmoid, bias=vec[:, col:col + 1])\
                            .then_inc(emptied(("rg", t, m)), 1)
                        act.wait_ge(*emptying(("rg", t, m)))
                    if t + 1 < KT:
                        act.dma_start(rgw[:, :, :], a_rgw[t + 1]).then_inc(rgw_in, 16)
                    for d in range(2):
                        lc = d * KT + t
                        A(rg[:, 4 + d, :], rg[:, 2 * d, :], ACT.Tanh, scale=lam_p[:, lc:lc + 1])\
                            .then_inc(act_chain.sem, 1)
                        act.wait_ge(act_chain.sem, act_chain.raised())
                    for d in range(2):
                        lc = d * KT + t
                        A(rg[:, 2 * d, :], rg[:, 2 * d, :], ACT.Exp, scale=lam_n[:, lc:lc + 1])\
                            .then_inc(to_dve.sem, 1)
                        act.wait_ge(to_dve.sem, to_dve.raised())
                else:
                    act.wait_ge(*emptying(("O2", p - 1)))
                    for n in range(AHEAD):
                        merging_gate(n)
                if 0 <= p < KT - 2:
                    load_bias(act, p + 2)
            act.wait_ge(*emptying(("O2", KT - 1)))
            for n in range(AHEAD, 2 * KT):
                merging_gate(n)
                if n == KT:
                    act.wait_ge(*filling(("prod", KT - 1)))
                    for k in range(KT):
                        A(y_hi[:, k, :], xc[:, k, :], ACT.Copy).then_inc(h_hi.sem, 1)
                        act.wait_ge(h_hi.sem, h_hi.raised())
            for m in range(KT):
                act.wait_ge(to_act.sem, to_act.seen_by("act"))
                A(a_hi[:, m, :], merged[:, m, :], ACT.Copy).then_inc(h_hi.sem, 1)
                act.wait_ge(h_hi.sem, h_hi.raised())
            for k in range(KT):
                act.wait_ge(*emptying(("wo", k)))
                square(k)
            inverse_rms(("n3",), D)
            A(rstd[:, :], rstd[:, :], ACT.Exp, scale=-0.5).then_inc(rstd_ok.sem, 1)
            act.wait_ge(rstd_ok.sem, rstd_ok.raised())

        @block.vector
        def _(dve):
            V = nc.vector
            TT, TS, STT, CP = V.tensor_tensor, V.tensor_scalar, V.scalar_tensor_tensor, V.tensor_copy

            V.memset(epst[:, :], EPS).then_inc(eps_ok.sem, 1)
            dve.wait_ge(eps_ok.sem, eps_ok.raised())
            dve.wait_ge(const_in, 32)
            dve.wait_ge(to_dve.sem, to_dve.seen_by("dve"))
            TT(c_lo[:, :], csil[:, :], c_hi[:, :].bitcast(F32), ALU.subtract).then_inc(c_ready.sem, 1)
            dve.wait_ge(c_ready.sem, c_ready.raised())
            dve.wait_ge(to_dve.sem, to_dve.seen_by("dve"))
            TS(lam_s[:, :], lam_z[:, :], 2.0, None, ALU.add).then_inc(dve_chain.sem, 1)
            dve.wait_ge(dve_chain.sem, dve_chain.raised())
            V.reciprocal(lam_s[:, :], lam_s[:, :]).then_inc(dve_chain.sem, 1)
            dve.wait_ge(dve_chain.sem, dve_chain.raised())
            TT(lam_s[:, :], lam_s[:, :], lam_z[:, :], ALU.mult).then_inc(dve_chain.sem, 1)
            dve.wait_ge(dve_chain.sem, dve_chain.raised())
            TT(lam_q[:, :], lam_s[:, :], lam_s[:, :], ALU.mult).then_inc(dve_chain.sem, 1)
            dve.wait_ge(dve_chain.sem, dve_chain.raised())
            TS(lam_p[:, :], lam_q[:, :], 1.0 / 15, 1.0 / 13, ALU.mult, ALU.add).then_inc(dve_chain.sem, 1)
            dve.wait_ge(dve_chain.sem, dve_chain.raised())
            for k in (11, 9, 7, 5, 3, 1):
                TT(lam_p[:, :], lam_p[:, :], lam_q[:, :], ALU.mult).then_inc(dve_chain.sem, 1)
                dve.wait_ge(dve_chain.sem, dve_chain.raised())
                TS(lam_p[:, :], lam_p[:, :], 1.0 / k, None, ALU.add).then_inc(dve_chain.sem, 1)
                dve.wait_ge(dve_chain.sem, dve_chain.raised())
            TT(lam_p[:, :], lam_p[:, :], lam_s[:, :], ALU.mult).then_inc(dve_chain.sem, 1)
            dve.wait_ge(dve_chain.sem, dve_chain.raised())
            TS(lam_n[:, :], v_("lam"), -1.0, 0.0, ALU.mult, ALU.max).then_inc(dve_chain.sem, 1)
            dve.wait_ge(dve_chain.sem, dve_chain.raised())
            STT(lam_p[:, :], lam_p[:, :], 2.0, lam_n[:, :], ALU.mult, ALU.add).then_inc(dve_chain.sem, 1)
            dve.wait_ge(dve_chain.sem, dve_chain.raised())
            TS(lam_p[:, :], lam_p[:, :], RG_C, None, ALU.mult).then_inc(dve_chain.sem, 1)
            dve.wait_ge(dve_chain.sem, dve_chain.raised())
            TS(lam_n[:, :], lam_p[:, :], -1.0, None, ALU.mult).then_inc(dve_chain.sem, 1)
            dve.wait_ge(dve_chain.sem, dve_chain.raised())

            def windows(r, b, h):
                ap = PS[r, b, h:h + 1].unsqueeze(2).to_broadcast([HD, 16, NC])
                return bass.AP(ap.tensor, ap.offset, [list(ap.ap[0]), [2, 16], [CMP_STRIDE, NC]])

            def norm(gain):
                for k in range(KT):
                    dve.wait_ge(h_hi.sem, h_hi.seen_by("dve"))
                    STT(a_lo[:, k, :], x[:, k, :], gain[:, k:k + 1], a_hi[:, k, :].bitcast(F32),
                                     ALU.mult, ALU.subtract).then_inc(h_lo.sem, 1)
                    dve.wait_ge(h_lo.sem, h_lo.raised())
                dve.wait_ge(rstd_ok.sem, rstd_ok.seen_by("dve"))

            for l in range(DEPTH):
                dve.wait_ge(misc_in, 16 * (l + 1))
                norm(m_("g_attn"))

                def further(name):
                    t = T.get(name)
                    if name in ("kc", "vc"):
                        pos = m_("pos_k" if name == "kc" else "pos_v")
                        for g in range(GROUPS):
                            key = (l, name, "dup", g)
                            dve.wait_ge(*filling(key))
                            b = uses[key][0]
                            for h in range(2):
                                r = slice(HD * h, HD * h + HD)
                                src = windows(r, b, h)
                                ins = TT(X[r, :, g * NC:(g + 1) * NC], src,
                                         pos[r, :].unsqueeze(2).to_broadcast([HD, 16, NC]), ALU.add)
                                if h == 0:
                                    ins.then_inc(dve_chain.sem, 1)
                                    dve.wait_ge(dve_chain.sem, dve_chain.raised())
                                else:
                                    ins.then_inc(emptied(key), 1)
                                    dve.wait_ge(*emptying(key))
                        CP(small[:, 63:64], epst[:, :]).then_inc(to_act.sem, 1)
                        dve.wait_ge(to_act.sem, to_act.raised())
                        dve.wait_ge(to_dve.sem, to_dve.seen_by("dve"))
                        if name == "vc":
                            dve.wait_ge(*filling((l, "CK", 1)))
                        TT(X_lo[:, :, :], X, X_hi[:, :, :].bitcast(F32), ALU.subtract).then_inc(to_pe.sem, 1)
                        dve.wait_ge(to_pe.sem, to_pe.raised())
                    elif name in ("ksl", "kwn"):
                        for g in range(GROUPS):
                            kd, kr = (l, name, "dup", g), (l, name, "rot", g)
                            dst = keys[:, int(name == "kwn"), g, :]
                            dve.wait_ge(*filling(kd))
                            TT(dst, PS[:, uses[kd][0], :], c_("cos"), ALU.mult).then_inc(emptied(kd), 1)
                            dve.wait_ge(*emptying(kd))
                            dve.wait_ge(*filling(kr))
                            TT(tmp[:, :], PS[:, uses[kr][0], :], c_("sin"), ALU.mult).then_inc(emptied(kr), 1)
                            dve.wait_ge(*emptying(kr))
                            TT(dst, dst, tmp[:, :], ALU.add).then_inc(roped.sem, 1)
                            dve.wait_ge(roped.sem, roped.raised())
                    elif name[0] == "q":
                        key = (l, name, "rot")
                        dve.wait_ge(*filling(key))
                        q = proj[:, t, :]
                        STT(tmp[:, :], PS[:, uses[key][0], :], HD ** -0.5, c_("sin"), ALU.mult, ALU.mult)\
                            .then_inc(emptied(key), 1)
                        dve.wait_ge(*emptying(key))
                        STT(q, q, HD ** -0.5, c_("cos"), ALU.mult, ALU.mult).then_inc(dve_chain.sem, 1)
                        dve.wait_ge(dve_chain.sem, dve_chain.raised())
                        TT(q, q, tmp[:, :], ALU.add).then_inc(roped.sem, 1)
                        dve.wait_ge(roped.sem, roped.raised())
                    elif name == "gate":
                        dve.wait_ge(*emptying((l, "gate", "T")))
                        g = gN[:, 0, 2:24:3]
                        TS(g, g, c_("rowok"), None, ALU.mult).then_inc(dve_chain.sem, 1)
                        dve.wait_ge(dve_chain.sem, dve_chain.raised())
                    elif name == "CK":
                        dve.wait_ge(*filling((l, "kc2")))
                        CP(kc0[:, :], PS[:, uses[(l, "kc2")][0], 0:2 * NC]).then_inc(emptied((l, "kc2")), 1)
                        dve.wait_ge(*emptying((l, "kc2")))
                        dve.wait_ge(*filling((l, "kc2rot")))
                        TT(kcr[:, :], PS[:, uses[(l, "kc2rot")][0], 0:2 * NC], c_("sinc"), ALU.mult)\
                            .then_inc(emptied((l, "kc2rot")), 1)
                        dve.wait_ge(*emptying((l, "kc2rot")))
                        TT(tmp[:, 0:2 * NC], kc0[:, :], c_("cosc"), ALU.mult).then_inc(dve_chain.sem, 1)
                        dve.wait_ge(dve_chain.sem, dve_chain.raised())
                        TT(kcr[:, :], kcr[:, :], tmp[:, 0:2 * NC], ALU.add).then_inc(roped.sem, 1)
                        dve.wait_ge(roped.sem, roped.raised())

                for idx, name in enumerate(ORDER):
                    if name not in ("CK", "CV"):
                        dve.wait_ge(*filling((l, name)))
                        TT(proj[:, T[name], :], PS[:, uses[(l, name)][0], :], rstd[:, :], ALU.mult)\
                            .then_inc(emptied((l, name)), 1)
                        dve.wait_ge(*emptying((l, name)))
                    if idx >= LAG:
                        further(ORDER[idx - LAG])
                for name in ORDER[-LAG:]:
                    further(name)

                U = HEADS * NT
                cm = c_("cmask").rearrange("p (n c) -> p n c", c=NC)

                def maxima(u):
                    i, par = u % NT, u % 2
                    w = (i + 1) * P
                    for br in range(2):
                        dve.wait_ge(*filling((l, "S", br, u)))
                    s2 = PS[:, 2 * par:2 * par + 2, :]
                    TT(s2[:, :, i * P:w], s2[:, :, i * P:w], c_("causal").unsqueeze(1).to_broadcast([P, 2, P]), ALU.add)\
                        .then_inc(dve_chain.sem, 1)
                    dve.wait_ge(dve_chain.sem, dve_chain.raised())
                    V.tensor_reduce(nmax[:, par, 0:2], s2[:, :, 0:w], AX.X, ALU.max, negate=True)\
                        .then_inc(max_ok.sem, 1)
                    dve.wait_ge(max_ok.sem, max_ok.raised())

                def compressed_maxima(h):
                    dve.wait_ge(*filling((l, "Sc", h)))
                    sc = PS[:, 7, 0:NT * 32].rearrange("p (n c) -> p n c", c=32)[:, :, 0:NC]
                    TT(sc, sc, cm, ALU.add).then_inc(dve_chain.sem, 1)
                    dve.wait_ge(dve_chain.sem, dve_chain.raised())
                    V.tensor_reduce(nmaxc[:, h % 2, :], sc, AX.X, ALU.max, negate=True).then_inc(maxc_ok.sem, 1)
                    dve.wait_ge(maxc_ok.sem, maxc_ok.raised())

                def compressed_diagonals(h):
                    dve.wait_ge(*emptying((l, "Sc", h)))
                    V.reciprocal(r3[:, 0:NT], sumsc[:, h % 2, :]).then_inc(dve_chain.sem, 1)
                    dve.wait_ge(dve_chain.sem, dve_chain.raised())
                    TT(r3[:, 0:NT], r3[:, 0:NT], gN[:, :, h * BR + 2], ALU.mult).then_inc(dve_chain.sem, 1)
                    dve.wait_ge(dve_chain.sem, dve_chain.raised())
                    for i in range(NT):
                        ins = TS(diagc[:, i, :], ident, r3[:, i:i + 1], None, ALU.mult)
                        if i < NT - 1:
                            ins.then_inc(dve_chain.sem, 1)
                            dve.wait_ge(dve_chain.sem, dve_chain.raised())
                        else:
                            ins.then_inc(diagc_ok.sem, 1)
                            dve.wait_ge(diagc_ok.sem, diagc_ok.raised())

                def compressed_turned(h):
                    dve.wait_ge(*filling((l, "PTc", h)))
                    CP(PTc[0:NC, h % 2, :], PS[0:NC, 7, :]).then_inc(emptied((l, "PTc", h)), 1)
                    dve.wait_ge(*emptying((l, "PTc", h)))

                def diagonals(u):
                    h, i, par = u // NT, u % NT, u % 2
                    for br in range(2):
                        dve.wait_ge(*emptying((l, "S", br, u)))
                    V.reciprocal(r3[:, 0:2], sums[:, par, 0:2]).then_inc(dve_chain.sem, 1)
                    dve.wait_ge(dve_chain.sem, dve_chain.raised())
                    TT(r3[:, 0:2], r3[:, 0:2], gN[:, i, h * BR:h * BR + 2], ALU.mult).then_inc(dve_chain.sem, 1)
                    dve.wait_ge(dve_chain.sem, dve_chain.raised())
                    for br in range(2):
                        ins = TS(diag[:, par, br, :], ident, r3[:, br:br + 1], None, ALU.mult)
                        if br == 0:
                            ins.then_inc(dve_chain.sem, 1)
                            dve.wait_ge(dve_chain.sem, dve_chain.raised())
                        else:
                            ins.then_inc(diag_ok.sem, 1)
                            dve.wait_ge(diag_ok.sem, diag_ok.raised())

                compressed_maxima(0)
                maxima(0)
                maxima(1)
                compressed_diagonals(0)
                compressed_turned(0)
                diagonals(0)
                for u in range(U):
                    i, par = u % NT, u % 2
                    if u >= 2:
                        pv_finished(dve, l, u - 2)
                    dve.wait_ge(*filling((l, "PT", 1, u)))
                    CP(work[:, 5 + 2 * par, 0:(i + 1) * P], PS[:, 5, 0:(i + 1) * P])\
                        .then_inc(emptied((l, "PT", 1, u)), 1)
                    dve.wait_ge(*emptying((l, "PT", 1, u)))
                    if u + 1 < U:
                        diagonals(u + 1)
                    if u + 2 < U:
                        maxima(u + 2)
                    h = u // NT
                    if i == 0 and h + 1 < HEADS:
                        compressed_maxima(h + 1)
                    if i == 1 and h + 1 < HEADS:
                        compressed_diagonals(h + 1)
                    if i == 2:
                        key, n = (l, "mod", h), mod_tiles(h)
                        m = l * MOD_PER_LAYER + sum(mod_tiles(k) for k in range(h))
                        dve.wait_ge(*filling(key))
                        TT(modv[:, m:m + n], PS[:, 7, 0:2 * n:2], v_("b_c")[:, m:m + n], ALU.add)\
                            .then_inc(emptied(key), 1)
                        dve.wait_ge(*emptying(key))
                    if i == 3 and h + 1 < HEADS:
                        compressed_turned(h + 1)
                    if u % 8 == 0 and u:
                        t = u // 8 - 1
                        dve.wait_ge(h_hi.sem, h_hi.seen_by("dve"))
                        TT(a_lo[:, t, :], PS[:, 6, :], a_hi[:, t, :].bitcast(F32), ALU.subtract)\
                            .then_inc(emptied((l, "O", t)), 1)
                        dve.wait_ge(*emptying((l, "O", t)))
                t = HEADS // 2 - 1
                dve.wait_ge(h_hi.sem, h_hi.seen_by("dve"))
                TT(a_lo[:, t, :], PS[:, 6, :], a_hi[:, t, :].bitcast(F32), ALU.subtract)\
                    .then_inc(emptied((l, "O", t)), 1)
                dve.wait_ge(*emptying((l, "O", t)))

                B = work[:, 0, :]
                gq, gk = proj[:, T["gq"], :], proj[:, T["gk"], :]
                dve.wait_ge(*filling((l, "z")))
                ins = TS(B, PS[:, uses[(l, "z")][0], :], m_("b_up"), None, ALU.add)
                ins.then_inc(emptied((l, "z")), 1)
                dve.wait_ge(*emptying((l, "z")))
                V.memset(Ad, 0.0).then_inc(to_act.sem, 1)
                dve.wait_ge(to_act.sem, to_act.raised())
                dve.wait_ge(to_dve.sem, to_dve.seen_by("dve"))
                STT(work[:, 2, :], B, 0.0, work[:, 1, :], ALU.min, ALU.subtract).then_inc(dve_chain.sem, 1)
                dve.wait_ge(dve_chain.sem, dve_chain.raised())
                V.tensor_tensor_scan(B, c_("ones")[:, 0:1].to_broadcast([P, S]), work[:, 2, :], 0.0, ALU.mult, ALU.add)\
                    .then_inc(dve_chain.sem, 1)
                dve.wait_ge(dve_chain.sem, dve_chain.raised())

                def distances(lv):
                    s = 64 >> lv
                    bb = B.rearrange("p (n c) -> p n c", c=2 * s)
                    out = work[:, 2 + lv % 2, :].rearrange("p (n c) -> p n c", c=2 * s)
                    n = S // (2 * s)
                    TT(out, bb, bb[:, :, s - 1:s].to_broadcast([P, n, 2 * s]), ALU.subtract).then_inc(to_act.sem, 1)
                    dve.wait_ge(to_act.sem, to_act.raised())

                def gather(lv):
                    for h in range(GH):
                        dve.wait_ge(*filling((l, "lv", lv, h)))
                        mask = c_("levels")[:, lv * P:(lv + 1) * P].bitcast(U32).unsqueeze(1).to_broadcast([P, NT, P])
                        V.copy_predicated(Ad[:, h, :, :], mask, PS[:, h, :].rearrange("p (n c) -> p n c", c=P))\
                            .then_inc(emptied((l, "lv", lv, h)), 1)
                        dve.wait_ge(*emptying((l, "lv", lv, h)))

                distances(0)
                for lv in range(8):
                    if lv + 1 < 7:
                        distances(lv + 1)
                    qd, kd, e = work[:, 4 + lv % 2, :], work[:, 6 + lv % 2, :], work[:, 2 + lv % 2, :]
                    if lv < 7:
                        dve.wait_ge(to_dve.sem, to_dve.seen_by("dve"))
                        STT(qd, gq, GDK_SCALE, e, ALU.mult, ALU.mult).then_inc(dve_chain.sem, 1)
                        dve.wait_ge(dve_chain.sem, dve_chain.raised())
                        TT(kd, gk, e, ALU.mult).then_inc(to_pe.sem, 1)
                        dve.wait_ge(to_pe.sem, to_pe.raised())
                    else:
                        TS(qd, gq, GDK_SCALE, None, ALU.mult).then_inc(dve_chain.sem, 1)
                        dve.wait_ge(dve_chain.sem, dve_chain.raised())
                        CP(kd, gk).then_inc(to_pe.sem, 1)
                        dve.wait_ge(to_pe.sem, to_pe.raised())
                    if lv >= 1:
                        gather(lv - 1)
                gather(7)
                TS(small[:, 0:4], B[:, P - 1:S:P], -1.0 / TAU, None, ALU.mult).then_inc(dve_chain.sem, 1)
                dve.wait_ge(dve_chain.sem, dve_chain.raised())
                TS(small[:, 4:8], B[:, P - 1:S:P], 1.0 / TAU, None, ALU.mult).then_inc(to_act.sem, 1)
                dve.wait_ge(to_act.sem, to_act.raised())
                for j in range(NT - 1):
                    w = (NT - 1 - j) * P
                    dve.wait_ge(to_dve.sem, to_dve.seen_by("dve"))
                    if j == 2:
                        dve.wait_ge(*filling((l, "cross", 0, GH - 1)))
                    eq = work[:, 2 + j, 0:w] if j < 2 else work[:, 1, 3 * P:4 * P]
                    STT(work[:, 4 + j % 2, 0:w], gq[:, (j + 1) * P:S], GDK_SCALE, eq, ALU.mult, ALU.mult)\
                        .then_inc(dve_chain.sem, 1)
                    dve.wait_ge(dve_chain.sem, dve_chain.raised())
                    TT(work[:, 6 + j % 2, 0:P], gk[:, j * P:(j + 1) * P], work[:, 1, j * P:(j + 1) * P], ALU.mult)\
                        .then_inc(to_pe.sem, 1)
                    dve.wait_ge(to_pe.sem, to_pe.raised())
                sv = proj[:, T["sv0"]:T["sv0"] + 2, :].rearrange("p t (n c) -> p t n c", c=P)
                dve.wait_ge(*emptying((l, "sv1", "T")))
                for n in range(NT):
                    V.bn_stats(small[:, 8 + 6 * n:14 + 6 * n], sv[:, :, n, :]).then_inc(dve_chain.sem, 1)
                    dve.wait_ge(dve_chain.sem, dve_chain.raised())
                for n in range(NT):
                    V.bn_aggr(small[:, 32 + 2 * n:34 + 2 * n], small[:, 8 + 6 * n:14 + 6 * n])\
                        .then_inc(dve_chain.sem, 1)
                    dve.wait_ge(dve_chain.sem, dve_chain.raised())
                dve.wait_ge(to_dve.sem, to_dve.seen_by("dve", 2))
                for t in range(2):
                    key = (l, "og", t)
                    dve.wait_ge(*filling(key))
                    STT(work[:, 4 + t, :], PS[:, 4 + t, :], m_("gnorm"), work[:, 2 + t, :], ALU.mult, ALU.mult)\
                        .then_inc(emptied(key), 1)
                    dve.wait_ge(*emptying(key))
                dve.wait_ge(to_dve.sem, to_dve.seen_by("dve", 2))
                for t in range(2):
                    TT(work[:, 4 + t, :], work[:, 4 + t, :], proj[:, T["gr0"] + t, :], ALU.mult)\
                        .then_inc(to_act.sem, 1)
                    dve.wait_ge(to_act.sem, to_act.raised())
                for t in range(2):
                    dve.wait_ge(h_hi.sem, h_hi.seen_by("dve"))
                    TT(a_lo[:, 4 + t, :], work[:, 4 + t, :], a_hi[:, 4 + t, :].bitcast(F32), ALU.subtract)\
                        .then_inc(h_lo.sem, 1)
                    dve.wait_ge(h_lo.sem, h_lo.raised())
                CP(small[:, 62:63], epst[:, :]).then_inc(to_act.sem, 1)
                dve.wait_ge(to_act.sem, to_act.raised())
                dve.wait_ge(to_dve.sem, to_dve.seen_by("dve"))
                for n in range(NT):
                    TS(sv[:, :, n, :], sv[:, :, n, :], small[:, 32 + 2 * n:33 + 2 * n], small[:, 48 + n:49 + n],
                            ALU.subtract, ALU.mult).then_inc(dve_chain.sem, 1)
                    dve.wait_ge(dve_chain.sem, dve_chain.raised())
                for name, op in (("lng", ALU.mult), ("lnb", ALU.add)):
                    tab = m_(name).rearrange("p (t c) -> p t c", c=P).unsqueeze(2).to_broadcast([P, 2, NT, P])
                    TT(sv, sv, tab, op).then_inc(dve_chain.sem, 1)
                    dve.wait_ge(dve_chain.sem, dve_chain.raised())
                sw = m_("swt").rearrange("p (g c) -> p g c", c=P)
                TT(sw, sw, c_("triu").unsqueeze(1).to_broadcast([P, 4, P]), ALU.mult).then_inc(to_pe.sem, 1)
                dve.wait_ge(to_pe.sem, to_pe.raised())
                dve.wait_ge(to_dve.sem, to_dve.seen_by("dve", 2))
                for t in range(2):
                    key = (l, "sg", t)
                    dve.wait_ge(*filling(key))
                    wv = work[:, 6 + t, :]
                    TT(wv.rearrange("p (n c) -> p n c", c=P), PS[:, t, :].rearrange("p (n c) -> p n c", c=P),
                                    m_("sgb")[:, t * P:(t + 1) * P].unsqueeze(1).to_broadcast([P, NT, P]), ALU.add)\
                        .then_inc(emptied(key), 1)
                    dve.wait_ge(*emptying(key))
                    TT(wv, wv, proj[:, T["su0"] + t, :], ALU.mult).then_inc(to_act.sem, 1)
                    dve.wait_ge(to_act.sem, to_act.raised())
                for t in range(2):
                    dve.wait_ge(h_hi.sem, h_hi.seen_by("dve"))
                    TT(a_lo[:, 6 + t, :], work[:, 6 + t, :], a_hi[:, 6 + t, :].bitcast(F32), ALU.subtract)\
                        .then_inc(h_lo.sem, 1)
                    dve.wait_ge(h_lo.sem, h_lo.raised())

                for m in range(KT):
                    key = (l, "out", m)
                    dve.wait_ge(*filling(key))
                    TT(x[:, m, :], PS[:, uses[key][0], :], x[:, m, :], ALU.add).then_inc(emptied(key), 1)
                    dve.wait_ge(*emptying(key))

                norm(m_("g_ffn"))
                if l + 1 < DEPTH:
                    CP(small[:, 61:62], epst[:, :]).then_inc(misc_free.sem, 1)
                    dve.wait_ge(misc_free.sem, misc_free.raised())
                for c in range(FCH):
                    for f in range(FT + 1):
                        if f < FT:
                            for kind, b0, w0, sig in (("g", 0, 0, None), ("u", 2, 2, None)):
                                key = (l, kind, c, f)
                                dve.wait_ge(*filling(key))
                                TT(work[:, w0 + f % 2, :], PS[:, b0 + f % 2, :], rstd[:, :], ALU.mult)\
                                    .then_inc(emptied(key), 1)
                                dve.wait_ge(*emptying(key))
                                if kind == "g":
                                    CP(small[:, 60:61], epst[:, :]).then_inc(to_act.sem, 1)
                                    dve.wait_ge(to_act.sem, to_act.raised())
                        if f > 0:
                            k = f - 1
                            dve.wait_ge(to_dve.sem, to_dve.seen_by("dve"))
                            TT(work[:, 4 + k % 2, :], work[:, k % 2, :], work[:, 2 + k % 2, :], ALU.mult)\
                                .then_inc(to_act.sem, 1)
                            dve.wait_ge(to_act.sem, to_act.raised())
                            dve.wait_ge(h_hi.sem, h_hi.seen_by("dve"))
                            TT(f_lo[:, k, :], work[:, 4 + k % 2, :], f_hi[:, k, :].bitcast(F32), ALU.subtract)\
                                .then_inc(h_lo.sem, 1)
                            dve.wait_ge(h_lo.sem, h_lo.raised())
                    for m in range(KT):
                        key = (l, "d", c, m)
                        dve.wait_ge(*filling(key))
                        TT(x[:, m, :], PS[:, uses[key][0], :], x[:, m, :], ALU.add).then_inc(emptied(key), 1)
                        dve.wait_ge(*emptying(key))

            dve.wait_ge(rstd_ok.sem, rstd_ok.seen_by("dve"))
            for k in range(KT):
                STT(x[:, k, :], x[:, k, :], v_("g_fin1")[:, k:k + 1], rstd[:, :], ALU.mult, ALU.mult)\
                    .then_inc(x_ok.sem, 1)
                dve.wait_ge(x_ok.sem, x_ok.raised())
            STT(gainm[:, :], modv[:, KT:2 * KT], 1.0, v_("g_pre"), ALU.add, ALU.mult).then_inc(dve_chain.sem, 1)
            dve.wait_ge(dve_chain.sem, dve_chain.raised())
            dve.wait_ge(rstd_ok.sem, rstd_ok.seen_by("dve"))
            for k in range(KT):
                STT(xc[:, k, :], x[:, k, :], gainm[:, k:k + 1], rstd[:, :], ALU.mult, ALU.mult)\
                    .then_inc(to_act.sem, 1)
                dve.wait_ge(to_act.sem, to_act.raised())
            for k in range(KT):
                dve.wait_ge(h_hi.sem, h_hi.seen_by("dve"))
                STT(a_lo[:, k, :], xc[:, k, :], modv[:, k:k + 1], a_hi[:, k, :].bitcast(F32),
                                 ALU.add, ALU.subtract).then_inc(h_lo.sem, 1)
                dve.wait_ge(h_lo.sem, h_lo.raised())
            V.memset(xpad[:, 0:2], 0.0).then_inc(dve_chain.sem, 1)
            dve.wait_ge(dve_chain.sem, dve_chain.raised())
            V.memset(xpad[:, S + 2:S + 3], 0.0).then_inc(dve_chain.sem, 1)
            dve.wait_ge(dve_chain.sem, dve_chain.raised())
            cw = v_("conv_w")
            for m in range(KT):
                dve.wait_ge(*filling(("xa", m)))
                CP(xpad[:, 2:S + 2], PS[:, m % 4, :]).then_inc(emptied(("xa", m)), 1)
                dve.wait_ge(*emptying(("xa", m)))
                TS(xc[:, m, :], xpad[:, 0:S], cw[:, m:m + 1], v_("conv_b")[:, m:m + 1], ALU.mult, ALU.add)\
                    .then_inc(dve_chain.sem, 1)
                dve.wait_ge(dve_chain.sem, dve_chain.raised())
                for j in range(1, 4):
                    ins = STT(xc[:, m, :], xpad[:, j:j + S], cw[:, j * KT + m:j * KT + m + 1], xc[:, m, :], ALU.mult, ALU.add)
                    if j == 3 and m == KT - 1:
                        ins.then_inc(to_pe.sem, 1)
                        dve.wait_ge(to_pe.sem, to_pe.raised())
                    else:
                        ins.then_inc(dve_chain.sem, 1)
                        dve.wait_ge(dve_chain.sem, dve_chain.raised())
            nm = c_("nmask").rearrange("p (n c) -> p n c", c=KC)

            def near_maxima(h):
                for half in range(2):
                    dve.wait_ge(*filling(("S2", h, half)))
                for i in range(4):
                    off = LOW[i] - QC * i + QC
                    s = PS[:, 2 + i // 2, i % 2 * 256:(i % 2 + 1) * 256].rearrange("p (c r) -> p r c", r=ROWS)
                    TT(s, s, bias[:, h % 4, ::-1, off:off + KC], ALU.add).then_inc(dve_chain.sem, 1)
                    dve.wait_ge(dve_chain.sem, dve_chain.raised())
                s4 = PS[:, 2:4, :].rearrange("p b (n c r) -> p (b n) c r", c=KC, r=ROWS)
                TT(s4, s4, nm.unsqueeze(3).to_broadcast([P, 4, KC, ROWS]), ALU.add).then_inc(dve_chain.sem, 1)
                dve.wait_ge(dve_chain.sem, dve_chain.raised())
                V.tensor_reduce(sm2[:, 0:4], PS[:, 2:4, :].rearrange("p b (n c) -> p (b n) c", c=256), AX.X, ALU.max,
                                negate=True).then_inc(max_ok.sem, 1)
                dve.wait_ge(max_ok.sem, max_ok.raised())

            def near_diagonals(h):
                for half in range(2):
                    dve.wait_ge(*emptying(("S2", h, half)))
                V.reciprocal(sm2[:, 8:12], sm2[:, 4:8]).then_inc(dve_chain.sem, 1)
                dve.wait_ge(dve_chain.sem, dve_chain.raised())
                for i in range(4):
                    ins = TS(dg2[:, i, :], ident, sm2[:, 8 + i:9 + i], None, ALU.mult)
                    if i < 3:
                        ins.then_inc(dve_chain.sem, 1)
                        dve.wait_ge(dve_chain.sem, dve_chain.raised())
                    else:
                        ins.then_inc(diag_ok.sem, 1)
                        dve.wait_ge(diag_ok.sem, diag_ok.raised())

            def near_turned(h):
                if h % 2:
                    dve.wait_ge(pv_done.sem, 56 + h // 2 + 1)
                dve.wait_ge(*filling(("PT2", h, 1)))
                CP(PT2[:, 2:4, :], PS[:, 5, :].rearrange("p (n c) -> p n c", c=256))\
                    .then_inc(emptied(("PT2", h, 1)), 1)
                dve.wait_ge(*emptying(("PT2", h, 1)))

            def decay_factor(d):
                e = rg[:, 4 + d, :]
                TS(tmp[:, :], e, 1.0, None, ALU.add).then_inc(dve_chain.sem, 1)
                dve.wait_ge(dve_chain.sem, dve_chain.raised())
                V.reciprocal(tmp[:, :], tmp[:, :]).then_inc(dve_chain.sem, 1)
                dve.wait_ge(dve_chain.sem, dve_chain.raised())
                TT(e, e, tmp[:, :], ALU.mult).then_inc(to_act.sem, 1)
                dve.wait_ge(to_act.sem, to_act.raised())

            def recurrence(p, d):
                a, i_, e = rg[:, 2 * d, :], rg[:, 2 * d + 1, :], rg[:, 4 + d, :]
                TT(i_, i_, xc[:, p, :], ALU.mult).then_inc(dve_chain.sem, 1)
                dve.wait_ge(dve_chain.sem, dve_chain.raised())
                dve.wait_ge(to_dve.sem, to_dve.seen_by("dve"))
                TT(i_, i_, e, ALU.mult).then_inc(dve_chain.sem, 1)
                dve.wait_ge(dve_chain.sem, dve_chain.raised())
                if d == 0:
                    V.tensor_tensor_scan(e, a, i_, 0.0, ALU.mult, ALU.add).then_inc(dve_chain.sem, 1)
                    dve.wait_ge(dve_chain.sem, dve_chain.raised())
                else:
                    V.tensor_tensor_scan(e[:, ::-1], a[:, ::-1], i_[:, ::-1], 0.0, ALU.mult, ALU.add)\
                        .then_inc(dve_chain.sem, 1)
                    dve.wait_ge(dve_chain.sem, dve_chain.raised())

            for t in range(KT + 1):
                p = t - 1
                if t < KT:
                    dve.wait_ge(*filling(("q", t)))
                    TS(by_column(qkv[:, t % 2, 0, :]), by_row(PS[:, uses[("q", t)][0], :]), HD ** -0.5, None, ALU.mult)\
                        .then_inc(emptied(("q", t)), 1)
                    dve.wait_ge(*emptying(("q", t)))
                if p >= 0:
                    dve.wait_ge(bias_in[p % 2], 16 * 2 * QC * (p // 2 + 1))
                    near_maxima(2 * p)
                    dve.wait_ge(*filling(("vT", p, 1)))
                    CP(vW[:, 4:8, :], PS[:, 7, :].rearrange("p (n c) -> p n c", c=P))\
                        .then_inc(emptied(("vT", p, 1)), 1)
                    dve.wait_ge(*emptying(("vT", p, 1)))
                    near_diagonals(2 * p)
                    near_maxima(2 * p + 1)
                    dve.wait_ge(to_dve.sem, to_dve.seen_by("dve", 2))
                    decay_factor(0)
                    near_turned(2 * p)
                    near_diagonals(2 * p + 1)
                    decay_factor(1)
                    recurrence(p, 0)
                    near_turned(2 * p + 1)
                    recurrence(p, 1)
                    TT(tmp[:, :], rg[:, 4, :], rg[:, 5, :], ALU.add).then_inc(dve_chain.sem, 1)
                    dve.wait_ge(dve_chain.sem, dve_chain.raised())
                    TT(tmp[:, :], tmp[:, :], sq[:, p % 2, :], ALU.mult).then_inc(to_act.sem, 1)
                    dve.wait_ge(to_act.sem, to_act.raised())
                    dve.wait_ge(*filling(("O2", p)))
                    dve.wait_ge(*emptying(("z", p)))
                    TT(by_row(xc[:, p, :]), by_column(PS[:, 6, :]), by_row(zs[:, p % 2, :]), ALU.mult)\
                        .then_inc(emptied(("O2", p)), 1)
                    dve.wait_ge(*emptying(("O2", p)))
                    dve.wait_ge(h_hi.sem, h_hi.seen_by("dve"))
                    TT(y_lo[:, p, :], tmp[:, :], y_hi[:, p, :].bitcast(F32), ALU.subtract)\
                        .then_inc(h_lo.sem, 1)
                    dve.wait_ge(h_lo.sem, h_lo.raised())

            def low_merged(m):
                dve.wait_ge(h_hi.sem, h_hi.seen_by("dve"))
                TT(a_lo[:, m, :], merged[:, m, :], a_hi[:, m, :].bitcast(F32), ALU.subtract)\
                    .then_inc(h_lo.sem, 1)
                dve.wait_ge(h_lo.sem, h_lo.raised())

            for n in range(2 * KT):
                dve.wait_ge(*emptying(("gate", n)))
                dve.wait_ge(*filling(("prod", n)))
                if n < KT:
                    TT(merged[:, n, :], PS[:, 2 + n % 2, :], gate_tile(n), ALU.mult).then_inc(emptied(("prod", n)), 1)
                    dve.wait_ge(*emptying(("prod", n)))
                else:
                    m = n - KT
                    TT(tmp[:, :], PS[:, 2 + n % 2, :], gate_tile(n), ALU.mult).then_inc(emptied(("prod", n)), 1)
                    dve.wait_ge(*emptying(("prod", n)))
                    TT(merged[:, m, :], merged[:, m, :], tmp[:, :], ALU.add).then_inc(to_act.sem, 1)
                    dve.wait_ge(to_act.sem, to_act.raised())
                if n == KT - 1:
                    for t in range(KT):
                        dve.wait_ge(h_hi.sem, h_hi.seen_by("dve"))
                        TT(y_lo[:, t, :], xc[:, t, :], y_hi[:, t, :].bitcast(F32), ALU.subtract)\
                            .then_inc(h_lo.sem, 1)
                        dve.wait_ge(h_lo.sem, h_lo.raised())
                if n == 2 * KT - 2:
                    for m in range(KT - 2):
                        low_merged(m)
            for m in range(KT - 2, KT):
                low_merged(m)
            gate = modv[:, 2 * KT:3 * KT]
            for m in range(KT):
                key = ("wo", m)
                dve.wait_ge(*filling(key))
                STT(x[:, m, :], PS[:, m % 4, :], gate[:, m:m + 1], x[:, m, :], ALU.mult, ALU.add)\
                    .then_inc(emptied(key), 1)
                dve.wait_ge(*emptying(key))
            dve.wait_ge(rstd_ok.sem, rstd_ok.seen_by("dve"))
            for k in range(KT):
                STT(xc[:, k, :], x[:, k, :], v_("g_fin2")[:, k:k + 1], rstd[:, :], ALU.mult, ALU.mult)\
                    .then_inc(out_ok.sem, 1)
                dve.wait_ge(out_ok.sem, out_ok.raised())

        @block.gpsimd
        def _(pool):
            G = nc.gpsimd

            def split(r, arrival, used, chain):
                pool.wait_ge(raw_in[r], arrival)
                if used is not None:
                    pool.wait_ge(slot_used, used)
                G.tensor_tensor(w_hi[:, r, :, :], raw[:, r, :, :], ones, ALU.mult).then_inc(pool_chain, 1)
                pool.wait_ge(pool_chain, chain)
                G.tensor_tensor(w_lo[:, r, :, :], raw[:, r, :, :], w_hi[:, r, :, :].bitcast(F32), ALU.subtract)\
                    .then_inc(split_done, 1)

            ones = c_("ones")[:, 0:1].unsqueeze(2).to_broadcast([P, 8, P])
            pool.wait_ge(const_in, 32)
            for r in range(RING):
                split(r, 16, None, r + 1)
            with pool.Fori(1, SLOTS // RING) as i:
                for r in range(RING):
                    split(r, i * 16 + 16, i * RING + (r - RING + 1), i * RING + (r + 1))
            last = SLOTS // RING
            for r in range(SLOTS % RING):
                split(r, 16 * (last + 1), last * RING + r - RING + 1, last * RING + r + 1)

        @block.sync
        def _(sp):
            for k in range(KT):
                sp.dma_start(x[:, k, :], a_x[:, k, :]).then_inc(x_in, 16)
            for r in range(RING):
                sp.dma_start(raw[:, r, :, :], w_sl[r]).then_inc(raw_in[r], 16)
            with sp.Fori(1, SLOTS // RING) as i:
                for r in range(RING):
                    sp.wait_ge(split_done, i * RING + (r - RING + 1))
                    sp.dma_start(raw[:, r, :, :], w_rows[bass.ds((i * RING + r) * P, P), :]).then_inc(raw_in[r], 16)
            last = SLOTS // RING * RING
            for r in range(SLOTS - last):
                sp.wait_ge(split_done, last + r - RING + 1)
                sp.dma_start(raw[:, r, :, :], w_sl[last + r]).then_inc(raw_in[r], 16)
            for k in range(KT):
                sp.wait_ge(out_ok.sem, k + 1)
                sp.dma_start(a_out[:, k, :], xc[:, k, :]).then_inc(out_done, 16)
            sp.wait_ge(out_done, 16 * KT)


def kernel(**inputs):
    import numpy as np
    import concourse.bacc as bacc
    from concourse.bass_utils import run_bass_kernel_spmd

    f32 = np.float32
    a = {k: np.asarray(v) for k, v in inputs.items()}

    const = np.zeros((P, CONST_N), f32)

    def put(name, v):
        const[:, CONST[name][0]:CONST[name][1]] = np.asarray(v, f32).reshape(P, -1)

    p = np.arange(P)
    tok = np.arange(S)
    inv = 1.0 / (10000.0 ** ((p % (HD // 2)).astype(f32) / (HD // 2)))
    put("ident", np.eye(P))
    put("ones", np.ones((P, P)))
    ang = inv[:, None].astype(f32) * tok[None, :].astype(f32)
    put("cos", np.cos(ang))
    put("sin", np.sin(ang))
    ends = np.tile(np.arange(NC) * CMP_STRIDE + CMP_LEN - 1, 2)
    angc = inv[:, None].astype(f32) * ends[None, :].astype(f32)
    put("cosc", np.cos(angc))
    put("sinc", np.sin(angc))
    NEG = -1e30
    put("causal", np.where(p[None, :] <= p[:, None], 0.0, NEG))
    t_of = p[:, None] + P * np.arange(NT)[None, :]
    put("cmask", np.where(ends[None, None, :NC] <= t_of[:, :, None], 0.0, NEG))
    put("rowok", (p >= CMP_LEN - 1).astype(f32))
    rot = np.zeros((P, P))
    for m in range(P):
        if m % HD < HD // 2:
            rot[m + HD // 2, m] = -1.0
        else:
            rot[m - HD // 2, m] = 1.0
    put("rot", rot)
    dup = np.zeros((P, GROUPS, P))
    for g in range(GROUPS):
        dup[g * HD + p % HD, g, p] = 1.0
    put("dup", dup)
    put("rotdup", np.stack([dup_g @ rot for dup_g in dup.transpose(1, 0, 2)], 1))
    put("headones", (p[:, None] // HD == p[None, :] // HD))
    put("triu", p[:, None] <= p[None, :])
    levels = np.zeros((P, 8, P))
    for lv in range(7):
        s = 64 >> lv
        levels[:, lv, :] = ((p[:, None] // (2 * s) == p[None, :] // (2 * s))
                            & (p[:, None] % (2 * s) < s) & (p[None, :] % (2 * s) >= s))
    levels[:, 7, :] = np.eye(P)
    put("levels", levels)
    nmask = np.zeros((P, NT, KC))
    for i in range(NT):
        c = QC * i + p // ROWS
        c0 = np.clip(c - QC // 2, 0, GRID - QC)
        kc = LOW[i] + np.arange(KC)
        nmask[:, i, :] = np.where((kc[None, :] >= c0[:, None]) & (kc[None, :] < c0[:, None] + QC), 0.0, NEG)
    put("nmask", nmask)

    def vecs(v):
        return np.ascontiguousarray(v.reshape(-1, P).T)

    misc = np.zeros((DEPTH, P, MISC_N), f32)
    for l in range(DEPTH):
        def mput(name, v):
            misc[l, :, MISC[name][0]:MISC[name][1]] = v.reshape(P, -1)

        mput("g_attn", vecs(a["attn_norm"][l]))
        mput("g_ffn", vecs(a["ffn_norm"][l]))
        mput("pos_k", vecs(a["cmp_pos_k"][l].reshape(-1)))
        mput("pos_v", vecs(a["cmp_pos_v"][l].reshape(-1)))
        mput("b_up", a["gla_b_up"][l])
        mput("gnorm", np.tile(a["gla_norm"][l], 2))
        w2k = a["cmp_w2_k"][l].reshape(2, P, HD).transpose(1, 0, 2)
        mput("w2k", np.concatenate([w2k, w2k], 2))
        mput("w2v", a["cmp_w2_v"][l].reshape(2, P, HD).transpose(1, 0, 2))
        misc[l, 32:48, MISC["w_up"][0]:MISC["w_up"][1]] = a["gla_w_up"][l]
        mput("swt", a["sg_w"][l].transpose(2, 0, 1))
        mput("lng", np.broadcast_to(a["sg_ln_g"][l], (P, 2 * P)))
        mput("lnb", np.broadcast_to(a["sg_ln_b"][l], (P, 2 * P)))
        mput("sgb", np.repeat(a["sg_b"][l].reshape(2, 2, P), HD, 1).transpose(1, 0, 2))
    vec = np.zeros((P, VEC_N), f32)

    def vput(name, v):
        vec[:, VEC[name][0]:VEC[name][1]] = v.reshape(P, -1)

    vput("g_fin1", vecs(a["final_norm"]))
    vput("c", np.repeat(vecs(a["c_2"][0]), 2, 1))
    vput("b_c", vecs(a["b_c_2"][0]))
    vput("g_pre", vecs(a["g_pre_2"][0]))
    vput("conv_w", vecs(a["conv_w_2"][0].reshape(-1)))
    vput("conv_b", vecs(a["conv_b_2"][0]))
    vput("b_gate", np.concatenate([vecs(a[k][0]) for k in ("b_r_f_2", "b_i_f_2", "b_r_b_2", "b_i_b_2")], 1))
    vput("lam", np.concatenate([vecs(a["lam_f_2"][0]), vecs(a["lam_b_2"][0])], 1))
    vput("g_fin2", vecs(a["g_final_2"]))
    rgw = np.zeros((KT, P, 4, P), f32)
    for m, k in enumerate(("w_r_f_2", "w_i_f_2", "w_r_b_2", "w_i_b_2")):
        w = a[k][0].reshape(KT, 2, HD, HD)
        for hh in range(2):
            rgw[:, HD * hh:HD * hh + HD, m, HD * hh:HD * hh + HD] = w[:, hh]
    rpb = np.zeros(RPB_LEN + 2 * RPB_PAD, f32)
    rpb[RPB_PAD:RPB_PAD + RPB_LEN] = a["rpb_2"][0][:, ::-1].reshape(-1)

    cols = {}
    at = 0
    for name, n in (("q", 512), ("kc", P), ("vc", P), ("ksl", P), ("vsl", P), ("kwn", P), ("vwn", P), ("gts", 24),
                    ("gq", P), ("gk", P), ("gv", 2 * P), ("ga", 16), ("gr", 2 * P), ("su", 2 * P), ("sv", 2 * P)):
        cols[name] = at
        at += n

    def tile(w, c):
        return w[:, c:c + P].reshape(-1, P, P).transpose(1, 0, 2)

    stream = []
    for item in stream_plan():
        kind = item[0]
        if kind == "in":
            w, name = a["w_in"][item[1]], item[2]
            if name == "gate":
                g = w[:, cols["gts"]:cols["gts"] + 24].reshape(D, HEADS, BR)[:, :, [1, 2, 0]].reshape(D, 24)
                wide = np.zeros((D, P), f32)
                wide[:, 0:24] = g
                wide[:, 32:48] = w[:, cols["ga"]:cols["ga"] + 16]
                stream.append(tile(wide, 0))
            else:
                base = name if name in cols else name[:-1]
                n = 0 if name in cols else int(name[-1])
                stream.append(tile(w, cols[base] + n * P))
        elif kind == "cmp":
            w = a["cmp_w1_k" if item[2] == "CK" else "cmp_w1_v"][item[1]]
            m, half = divmod(item[3], 2)
            stream.append(w[half * D:(half + 1) * D, m * P:(m + 1) * P].reshape(8, P, P).transpose(1, 0, 2))
        elif kind == "mod":
            stream.append(tile(a["w_c_2"][0], item[1] * P))
        elif kind == "out":
            stream.append(tile(a["w_out"][item[1]], item[2] * P))
        elif kind in ("gate", "up"):
            stream.append(tile(a["w_gate" if kind == "gate" else "w_up"][item[1]], item[2] * P))
        elif kind == "down":
            l, c, i = item[1:]
            w = a["w_down"][l][c * FT * P:(c + 1) * FT * P].reshape(FT, P, KT, P).transpose(2, 0, 1, 3)
            stream.append(w.reshape(KT * FT, P, P)[8 * i:8 * i + 8].transpose(1, 0, 2))
        elif kind == "in2":
            stream.append(tile(a["w_in_2"][0], item[1] * P))
        else:
            w = a[{"pa": "w_pa_2", "pb": "w_pb_2", "wo": "w_o_2"}[kind]][0]
            stream.append(tile(w, item[1] * P))
    stream = np.stack(stream).reshape(-1, P, 8 * P)

    arrays = {
        "x_t": np.ascontiguousarray(a["x"][0].T.reshape(KT, P, S).transpose(1, 0, 2)),
        "weights": stream, "const": const, "misc": misc, "vec": vec, "rgw": rgw, "rpb": rpb,
    }
    nc = bacc.Bacc("TRN2", target_bir_lowering=False, num_devices=1)
    F32 = mybir.dt.float32
    args = [nc.dram_tensor(k, v.shape, F32, kind="ExternalInput").ap() for k, v in arrays.items()]
    out = nc.dram_tensor("out", (P, KT, S), F32, kind="ExternalOutput").ap()
    build(nc, *args, out)
    r = run_bass_kernel_spmd(nc, [arrays], core_ids=[0])
    y = np.asarray(r.results[0]["out"])
    return np.ascontiguousarray(y.transpose(1, 0, 2).reshape(D, S).T).reshape(1, S, D)
```

```python
import concourse.bass as bass
from concourse import mybir
from contextlib import ExitStack

S, D, P = 512, 1024, 128
DEPTH = 2
KT = D // P
NT = S // P
HD = 64
HEADS, GROUPS, BR = 8, 2, 3
CMP_LEN, CMP_STRIDE = 32, 16
NC = (S - CMP_LEN) // CMP_STRIDE + 1
GH, GDK, GDV = 4, 32, 64
TAU = 16.0
DFF = 2816
FCH = 2
FT = DFF // P // FCH
EPS = 1e-6
NH2, GRID, ROWS = 16, 64, 8
QC, KC = 16, 32
RW = QC + KC
LOW = [0, 8, 24, 32]
RG_C = 8.0
AHEAD = 4

T = {"q0": 0, "q1": 1, "q2": 2, "q3": 3, "ksl": 4, "vsl": 5, "kwn": 6, "vwn": 7, "kc": 8, "vc": 9,
     "gk": 10, "gq": 11, "gv0": 12, "gv1": 13, "gr0": 14, "gr1": 15, "sv0": 16, "sv1": 17,
     "su0": 18, "su1": 19, "gate": 20}
ORDER = ["kc", "gate", "ksl", "vsl", "CK0", "vc", "CK1", "kwn", "vwn", "q0", "CV0", "q1", "CV1", "q2", "q3"]
BEFORE = [("sv0", 6), ("sv1", 5)]
BESIDE = [("sv0", "T"), ("su0", ""), ("sv1", "T"), ("su1", ""), ("gk", ""), ("gq", ""),
          ("gv0", ""), ("gv1", ""), ("gv0", "T"), ("gr0", ""), ("gv1", "T"), ("gr1", "")]
LAG = 2
MOD_SLOTS = 3 * KT
MOD_EACH = MOD_SLOTS // (DEPTH * FCH)
MOD_FROM = FT - 1 - MOD_EACH
CMP_K = CMP_LEN * HD // P


def mod_tile(l, c, f):
    return (l * FCH + c) * MOD_EACH + f - MOD_FROM


def columns(fields):
    at, out = 0, {}
    for name, n in fields:
        out[name] = (at, at + n)
        at += n
    return out, at


CONST, CONST_N = columns([
    ("ident", P), ("ones", P), ("nmask", NT * KC), ("cos", S), ("sin", S), ("cosc", 2 * NC), ("sinc", 2 * NC),
    ("causal", P), ("cmask", NT * NC), ("rowok", 1), ("rot", P), ("dup", 2 * P), ("rotdup", 2 * P),
    ("headones", P), ("triu", P), ("levels", 7 * P // 2)])
HEAD = CONST["nmask"][0]
MISC, MISC_N = columns([
    ("g_ffn", KT), ("pos_k", 16), ("pos_v", 16), ("b_up", 1), ("gnorm", 1),
    ("w2k", 2 * P), ("w2v", 2 * HD), ("w_up", P), ("swt", 4 * P), ("lng", 2 * P), ("lnb", 2 * P),
    ("sgb", 2 * P)])
VEC, VEC_N = columns([
    ("g_attn", DEPTH * KT), ("g_fin1", KT), ("b_c", MOD_SLOTS), ("g_pre", KT), ("conv_w", 4 * KT),
    ("conv_b", KT), ("b_gate", 4 * KT), ("lam", 2 * KT), ("g_fin2", KT)])
RPB_PAD = QC
RPB_LEN = NH2 * 15 * 31


OUT_ROWS = [0, 1, 2, 3, 6, 7, 4, 5]
OUT_EARLY = 4
OUT_TILES = ([(m, k) for m in range(OUT_EARLY) for k in range(KT - 2)]
             + [(m, k) for m in range(OUT_EARLY) for k in range(KT - 2, KT)]
             + [(m, k) for m in range(OUT_EARLY, KT) for k in range(KT)])


def stream_plan():
    out = []
    for l in range(DEPTH):
        out += [("in", l, name) for name in ORDER if name[0] != "C"]
        out += [("in", l, name) for name, bank in BEFORE]
        out += [("in", l, name) for name, step in BESIDE if not step]
        out += [("out", l, m) for m in range(KT)]
        for c in range(FCH):
            for f in range(FT):
                out += [("gate", l, c * FT + f), ("up", l, c * FT + f)]
            out += [("down", l, c, i) for i in range(FT)]
    out += [("in2", m) for m in range(8)]
    for t in range(KT):
        out += [("in2", part * KT + t) for part in (2, 3, 4, 5, 1)]
    gates = [("in2", 6 * KT + n) for n in range(2 * KT)]
    out += gates[:AHEAD]
    for n in range(2 * KT):
        out += [("pa" if n < KT else "pb", n % KT)] + gates[n + AHEAD:n + AHEAD + 1]
    out += [("wo", m) for m in range(8)]
    return out


def build(nc, a_x, a_w, a_cmp, a_mod, a_c, a_const, a_misc, a_vec, a_rgw, a_rpb, a_out):
    F32, F32R, U32 = mybir.dt.float32, mybir.dt.float32r, mybir.dt.uint32
    ALU, ACT, AX = mybir.AluOpType, mybir.ActivationFunctionType, mybir.AxisListType
    PLAN = stream_plan()
    SLOTS = len(PLAN)
    RING = 4
    assert SLOTS % RING == 2
    ctx = ExitStack()
    with ctx:
        place = [0]

        def at(name, shape, dt, offset):
            return nc.alloc_sbuf_tensor_at(name, shape, dt, offset=offset)

        base = nc.sbuf_base if not callable(nc.sbuf_base) else nc.sbuf_base()
        place[0] = (int(base) + 63) // 64 * 64

        def sb(name, shape, dt=F32):
            n = 4
            for k in shape[1:]:
                n *= k
            t = at(name, shape, dt, place[0])
            place[0] += (n + 31) // 32 * 32
            return t

        def sem(name):
            return ctx.enter_context(nc.semaphore(name))

        x = sb("x", [P, KT, S])
        a_hi = sb("a_hi", [P, KT, S], F32R)
        a_lo = sb("a_lo", [P, KT, S], F32R)
        raw = sb("raw", [P, RING, 8, P])
        w_hi = sb("w_hi", [P, RING, 8, P], F32R)
        w_lo = sb("w_lo", [P, RING, 8, P], F32R)
        const = sb("const", [P, CONST_N])
        tail = place[0] - (CONST_N - CONST["cos"][0]) * 4
        vec = sb("vec", [P, VEC_N])
        rstd = sb("rstd", [P, S])
        tmp = sb("tmp", [P, S])
        sq = sb("sq", [P, 2, S])
        modv = sb("modv", [P, MOD_SLOTS])
        lam_z = sb("lam_z", [P, 2 * KT])
        lam_s = sb("lam_s", [P, 2 * KT])
        lam_q = sb("lam_q", [P, 2 * KT])
        lam_p = sb("lam_p", [P, 2 * KT])
        lam_n = sb("lam_n", [P, 2 * KT])
        epst = sb("epst", [P, 1])
        gainm = sb("gainm", [P, KT])
        arena = place[0]
        proj = sb("proj", [P, 21, S])
        after = place[0]
        place[0] = arena
        f_hi = sb("f_hi", [P, FT, S], F32R)
        f_lo = sb("f_lo", [P, FT, S], F32R)
        place[0] = max(after, place[0])
        misc = sb("misc", [P, MISC_N])
        keys = sb("keys", [P, 2, GROUPS, S])
        work = sb("work", [P, 8, S])
        hid = sb("hid", [P, 2, 2, 2 * NC])
        kcr = sb("kcr", [P, 2 * NC])
        kc0 = sb("kc0", [P, 2 * NC])
        vcn = sb("vcn", [32, GROUPS * HD])
        gN = sb("gN", [P, NT, 24])
        Pc = sb("Pc", [P, 2, NT, 32])
        PTc = sb("PTc", [32, 2, S])
        nmaxc = sb("nmaxc", [P, 2, NT])
        sumsc = sb("sumsc", [P, 2, NT])
        nmax = sb("nmax", [P, 2, 4])
        sums = sb("sums", [P, 2, 4])
        r3 = sb("r3", [P, 4])
        small = sb("small", [P, 64])
        end1 = place[0]
        place[0] = arena
        y_hi = sb("y_hi", [P, KT, S], F32R)
        y_lo = sb("y_lo", [P, KT, S], F32R)
        xc = sb("xc", [P, KT, S])
        merged = at("merged", [P, KT, S], F32, place[0])
        qkv = sb("qkv", [P, 2, 3, S])
        rg = sb("rg", [P, 6, S])
        zs = sb("zs", [P, 2, S])
        P2 = sb("P2", [P, 4, 256])
        PT2 = sb("PT2", [P, 4, 256])
        vW = sb("vW", [P, 8, P])
        end2 = place[0]
        place[0] = (tail + 31) // 32 * 32
        xpad = sb("xpad", [P, S + 3])
        rgw = sb("rgw", [P, 4, P])
        bias = sb("bias", [P, 4, ROWS, RW])
        sm2 = sb("sm2", [P, 12])
        assert place[0] <= tail + (CONST_N - CONST["cos"][0]) * 4
        assert max(end1, end2) <= nc.sbuf_usable_end
        PS = ctx.enter_context(nc.psum_tensor("PS", [P, 8, S], F32))

        def gate_tile(n):
            return (zs, sq)[n % 2][:, n // 2 % 2, :]

        def c_(name):
            return const[:, CONST[name][0]:CONST[name][1]]

        def m_(name):
            return misc[:, MISC[name][0]:MISC[name][1]]

        def v_(name):
            return vec[:, VEC[name][0]:VEC[name][1]]

        ident = c_("ident")
        Ad = proj[:, 0:4, :].rearrange("p h (n c) -> p h n c", c=P)
        Ax = proj[:, 4:10, :].rearrange("p a b -> p (a b)").rearrange("p (h c) -> p h c", h=GH)
        X = [work[:, n:n + 2, :].rearrange("p a b -> p (a b)")[:, 0:CMP_K * 2 * NC]
             .rearrange("p (k c) -> p k c", c=2 * NC) for n in (0, 2)]
        cmp_w = work[:, 4:8, :].rearrange("p a b -> p (a b)").rearrange("p (k c) -> p k c", c=P)
        csil = keys[:, 0, :, :].rearrange("p a b -> p (a b)")
        mod_w = work[:, 6:8, :].rearrange("p a b -> p (a b)")
        sums2 = [tmp[:, :], work[:, 4, :]]

        spread = [keys[:, b, :, :].rearrange("p a b -> p (a b)").rearrange("p (n h c) -> p n h c", n=NT, h=GH)
                  for b in range(2)]
        factors = [work[:, 0, :], work[:, 1, :], sq[:, 0, :]]

        full = [sem(f"full{b}") for b in range(8)]
        free = [sem(f"free{b}") for b in range(8)]
        fills = [0] * 8
        uses = {}

        class Signal:

            def __init__(self, name):
                self.sem, self.n, self.seen = sem(name), 0, {}

            def raised(self):
                self.n += 1
                return self.n

            def seen_by(self, who, k=1):
                self.seen[who] = self.seen.get(who, 0) + k
                return self.seen[who]

        raw_in = [sem(f"raw_in{r}") for r in range(RING)]
        split_done = sem("split_done")
        slot_used = sem("slot_used")
        head_in = sem("head_in")
        vec_in = sem("vec_in")
        const_in = sem("const_in")
        c_in = sem("c_in")
        misc_in = sem("misc_in")
        rgw_in = sem("rgw_in")
        cmp_in = sem("cmp_in")
        mod_in = sem("mod_in")
        bias_in = [sem("bias_in0"), sem("bias_in1")]
        x_in = [sem(f"x_in{k}") for k in range(KT)]
        out_done = sem("out_done")
        pool_chain = sem("pool_chain")
        dve_chain = Signal("dve_chain")
        act_chain = Signal("act_chain")
        h_hi = Signal("h_hi")
        h_lo = Signal("h_lo")
        squares = Signal("squares")
        sq_used = Signal("sq_used")
        sum_ok = Signal("sum_ok")
        squares_g = Signal("squares_g")
        mod_used = Signal("mod_used")
        rstd_ok = Signal("rstd_ok")
        roped = Signal("roped")
        to_act = Signal("to_act")
        to_dve = Signal("to_dve")
        to_pe = Signal("to_pe")
        maxc_ok = Signal("maxc_ok")
        max_ok = Signal("max_ok")
        scaledc = Signal("scaledc")
        scaled = Signal("scaled")
        pv_done = Signal("pv_done")
        misc_free = Signal("misc_free")
        eps_ok = Signal("eps_ok")
        c_ready = Signal("c_ready")
        out_ok = Signal("out_ok")

        def filling(name):
            b, k = uses[name]
            return full[b], k + 1

        def emptying(name):
            b, k = uses[name]
            return free[b], k + 1

        def room(name):
            b, k = uses[name]
            return free[b], k

        def emptied(name):
            return free[uses[name][0]]

        block = ctx.enter_context(nc.Block())
        w_rows = a_w.rearrange("n p c -> (n p) c")
        w_sl = a_w.rearrange("n p (k c) -> n p k c", c=P)

        @block.tensor
        def _(pe):
            st = {"n": 0, "sub": 0}

            def claim(name, b):
                uses[name] = (b, fills[b])
                fills[b] += 1
                return fills[b] > 1

            def weights():
                if st["sub"] == 0:
                    pe.wait_ge(split_done, st["n"] + 1)
                first = st["sub"] == 0 and st["n"] > 0
                r, k = st["n"] % RING, st["sub"]
                st["sub"] += 1
                if st["sub"] == 8:
                    st["sub"], st["n"] = 0, st["n"] + 1
                return w_hi[:, r, k, :], w_lo[:, r, k, :], first

            def product(out, hi, lo, start, stop):
                wh, wl, first = weights()
                ins = nc.tensor.matmul(out, wh, hi, start=start, stop=False)
                if first:
                    ins.then_inc(slot_used, 1)
                nc.tensor.matmul(out, wh, lo, start=False, stop=False)
                return nc.tensor.matmul(out, wl, hi, start=False, stop=stop)

            def gemm(name, b, hi, lo, n=KT, fresh=None):
                if claim(name, b):
                    pe.wait_ge(*room(name))
                out = PS[:, b, :]
                for k in range(n):
                    if fresh is not None and k >= fresh:
                        pe.wait_ge(h_lo.sem, h_lo.seen_by("pe"))
                    ins = product(out, hi[:, k, :], lo[:, k, :], k == 0, k == n - 1)
                ins.then_inc(filling(name)[0], 1)

            def stats(key, which=0):
                b = (7, 0)[which]
                if claim(key, b):
                    pe.wait_ge(*room(key))
                pe.wait_ge(sum_ok.sem, sum_ok.seen_by("pe"))
                nc.tensor.matmul(PS[:, b, :], c_("ones"), sums2[which], start=True, stop=True)\
                    .then_inc(filling(key)[0], 1)

            aux = [0]

            def aux_bank():
                aux[0] += 1
                return 4 + aux[0] % 3

            def one(name, lhsT, rhs, cols=S, rows=P):
                b = aux_bank()
                if claim(name, b):
                    pe.wait_ge(*room(name))
                nc.tensor.matmul(PS[0:rows, b, 0:cols], lhsT, rhs, start=True, stop=True)\
                    .then_inc(filling(name)[0], 1)

            pe.wait_ge(head_in, 16)
            for l in range(DEPTH):
                gb = 0

                def further(name):
                    t = T.get(name)
                    if name in ("kc", "vc"):
                        pe.wait_ge(*emptying((l, name)))
                        for g in range(GROUPS):
                            one((l, name, "dup", g), c_("dup")[:, g * P:(g + 1) * P], proj[:, t, :])
                    elif name in ("ksl", "kwn"):
                        pe.wait_ge(*emptying((l, name)))
                        for g in range(GROUPS):
                            one((l, name, "dup", g), c_("dup")[:, g * P:(g + 1) * P], proj[:, t, :])
                            one((l, name, "rot", g), c_("rotdup")[:, g * P:(g + 1) * P], proj[:, t, :])
                    elif name[0] == "q":
                        pe.wait_ge(*emptying((l, name)))
                        one((l, name, "rot"), c_("rot"), proj[:, t, :])
                    elif name in ("vsl", "vwn", "gate"):
                        pe.wait_ge(*emptying((l, name)))
                        w = 24 if name == "gate" else P
                        b = aux_bank()
                        if claim((l, name, "T"), b):
                            pe.wait_ge(*room((l, name, "T")))
                        for i in range(NT):
                            ins = nc.tensor.transpose(PS[:, b, i * w:(i + 1) * w], proj[0:w, t, i * P:(i + 1) * P],
                                                      ident[0:w, 0:w])
                        ins.then_inc(filling((l, name, "T"))[0], 1)
                    elif name == "CK1":
                        pe.wait_ge(*emptying((l, "CK1")))
                        b = aux_bank()
                        if claim((l, "kc2"), b):
                            pe.wait_ge(*room((l, "kc2")))
                        for m in range(2):
                            ins = nc.tensor.matmul(PS[:, b, 0:2 * NC], m_("w2k")[:, m * P:(m + 1) * P], hid[:, 0, m, :],
                                                   start=m == 0, stop=m == 1)
                        ins.then_inc(filling((l, "kc2"))[0], 1)
                        pe.wait_ge(*emptying((l, "kc2")))
                        one((l, "kc2rot"), c_("rot"), kc0[:, :], cols=2 * NC)
                    elif name == "CV1":
                        pe.wait_ge(*emptying((l, "CV1")))
                        b = aux_bank()
                        if claim((l, "vc2"), b):
                            pe.wait_ge(*room((l, "vc2")))
                        for g in range(GROUPS):
                            for m in range(2):
                                ins = nc.tensor.matmul(PS[0:NC, b, g * HD:(g + 1) * HD], hid[:, 1, m, g * NC:(g + 1) * NC],
                                                       m_("w2v")[:, m * HD:(m + 1) * HD], start=m == 0, stop=m == 1)
                        ins.then_inc(filling((l, "vc2"))[0], 1)

                for idx, name in enumerate(ORDER):
                    if idx == 0:
                        gemm((l, name), 0, a_hi, a_lo, fresh=0)
                        stats((l, "ss"))
                        gb = 1
                        pe.wait_ge(const_in, 16)
                        pe.wait_ge(misc_in, 16 * (l + 1))
                    elif name[0] == "C":
                        key, b = (l, name), gb % 4
                        gb += 1
                        values_ = name[1] == "V"
                        if claim(key, b):
                            pe.wait_ge(*room(key))
                        pe.wait_ge(*emptying((l, "vc" if values_ else "kc", "dup", GROUPS - 1)))
                        pe.wait_ge(cmp_in, 16 * (4 * l + 2 * values_ + int(name[2]) + 1))
                        for k in range(CMP_K):
                            ins = nc.tensor.matmul(PS[:, b, 0:2 * NC], cmp_w[:, k, :], X[values_][:, k, :],
                                                   start=k == 0, stop=k == CMP_K - 1)
                        ins.then_inc(filling(key)[0], 1)
                    else:
                        gemm((l, name), gb % 4, a_hi, a_lo)
                        gb += 1
                    if idx >= LAG:
                        further(ORDER[idx - LAG])
                for name in ORDER[-LAG:]:
                    further(name)

                U = HEADS * NT

                def scores(u):
                    h, i, par = u // NT, u % NT, u % 2
                    p0, g = HD * (h % 2), h // (HEADS // GROUPS)
                    q = proj[p0:p0 + HD, h // 2, i * P:(i + 1) * P]
                    w = (i + 1) * P
                    for br in range(2):
                        key = (l, "S", br, u)
                        if claim(key, 2 * par + br):
                            pe.wait_ge(*room(key))
                        nc.tensor.matmul(PS[:, 2 * par + br, 0:w], q, keys[p0:p0 + HD, br, g, 0:w],
                                                start=True, stop=True).then_inc(filling(key)[0], 1)

                def turn(u):
                    i, par = u % NT, u % 2
                    pe.wait_ge(scaled.sem, scaled.seen_by("pe"))
                    for br in range(2):
                        key = (l, "PT", br, u)
                        if claim(key, 4 + br):
                            pe.wait_ge(*room(key))
                        for j in range(i + 1):
                            ins = nc.tensor.transpose(PS[:, 4 + br, j * P:(j + 1) * P],
                                                      work[:, 2 * par + br, j * P:(j + 1) * P], ident)
                        ins.then_inc(filling(key)[0], 1)

                def compressed_scores(h):
                    p0, g = HD * (h % 2), h // (HEADS // GROUPS)
                    key = (l, "Sc", h)
                    if claim(key, 7):
                        pe.wait_ge(*room(key))
                    for i in range(NT):
                        ins = nc.tensor.matmul(PS[:, 7, i * 32:i * 32 + NC], proj[p0:p0 + HD, h // 2, i * P:(i + 1) * P],
                                               kcr[p0:p0 + HD, g * NC:(g + 1) * NC], start=True, stop=True)
                    ins.then_inc(filling(key)[0], 1)

                def turn_compressed(h):
                    pe.wait_ge(scaledc.sem, scaledc.seen_by("pe"))
                    key = (l, "PTc", h)
                    if claim(key, 7):
                        pe.wait_ge(*room(key))
                    for i in range(NT):
                        ins = nc.tensor.transpose(PS[0:NC, 7, i * P:(i + 1) * P], Pc[:, h % 2, i, 0:NC], ident)
                    ins.then_inc(filling(key)[0], 1)

                def values(u):
                    h, i, par = u // NT, u % NT, u % 2
                    p0, g = HD * (h % 2), h // (HEADS // GROUPS)
                    key = (l, "O", h // 2)
                    if u % (2 * NT) == 0:
                        if claim(key, 6):
                            pe.wait_ge(*room(key))
                    out = PS[p0:p0 + HD, 6, i * P:(i + 1) * P]
                    pe.wait_ge(*emptying((l, "PTc", h)))
                    nc.tensor.matmul(out, vcn[0:NC, g * HD:(g + 1) * HD], PTc[0:NC, h % 2, i * P:(i + 1) * P],
                                     start=True, stop=False)
                    for br in range(2):
                        pe.wait_ge(*emptying((l, "PT", br, u)))
                        v = proj[:, T["vsl"] + 2 * br, :].rearrange("p (n c) -> p n c", c=P)
                        for j in range(i + 1):
                            ins = nc.tensor.matmul(out, v[:, j, g * HD:(g + 1) * HD],
                                                   work[:, 4 + 2 * par + br, j * P:(j + 1) * P],
                                                   start=False, stop=br == 1 and j == i)
                    if u % (2 * NT) == 2 * NT - 1:
                        ins.then_inc(filling(key)[0], 1)
                    else:
                        ins.then_inc(pv_done.sem, 1)
                        pv_done.raised()

                def beside(name, step, b=7):
                    if step == "":
                        gemm((l, name), b, a_hi, a_lo)
                    else:
                        if claim((l, name, "T"), 7):
                            pe.wait_ge(*room((l, name, "T")))
                        pe.wait_ge(*emptying((l, name)))
                        for i in range(NT):
                            ins = nc.tensor.transpose(PS[:, 7, i * P:(i + 1) * P], proj[:, T[name], i * P:(i + 1) * P], ident)
                        ins.then_inc(filling((l, name, "T"))[0], 1)

                def spatial_gating(t):
                    if t == 0:
                        pe.wait_ge(to_pe.sem, to_pe.seen_by("pe"))
                    key = (l, "sg", t)
                    if claim(key, 7):
                        pe.wait_ge(*room(key))
                    v = proj[:, T["sv0"] + t, :].rearrange("p (n c) -> p n c", c=P)
                    for hh in range(2):
                        for n in range(NT):
                            ins = nc.tensor.matmul(PS[HD * hh:HD * hh + HD, 7, n * P:(n + 1) * P], v[:, n, hh * HD:(hh + 1) * HD],
                                                   m_("swt")[:, (2 * t + hh) * P:(2 * t + hh + 1) * P], start=True, stop=True)
                    ins.then_inc(filling(key)[0], 1)

                beside(BEFORE[0][0], "", BEFORE[0][1])
                pe.wait_ge(roped.sem, roped.seen_by("pe", 2 * GROUPS + 4 + 1))
                pe.wait_ge(*emptying((l, "vc2")))
                pe.wait_ge(*emptying((l, "vwn", "T")))
                compressed_scores(0)
                scores(0)
                scores(1)
                beside(BEFORE[1][0], "", BEFORE[1][1])
                turn_compressed(0)
                for u in range(U):
                    h, i = u // NT, u % NT
                    turn(u)
                    if u + 2 < U:
                        scores(u + 2)
                    if i == 0 and h + 1 < HEADS:
                        compressed_scores(h + 1)
                    if i in (1, 2) and 2 * h + i - 1 < len(BESIDE):
                        beside(*BESIDE[2 * h + i - 1])
                    elif h == HEADS - 1 and i == 0:
                        if claim((l, "z"), 7):
                            pe.wait_ge(*room((l, "z")))
                        nc.tensor.matmul(PS[:, 7, :], m_("w_up")[32:48, :], proj[32:48, T["gate"], :],
                                         start=True, stop=True).then_inc(filling((l, "z"))[0], 1)
                    elif h == HEADS - 1 and i < 3:
                        spatial_gating(i - 1)
                    if i == 3 and h + 1 < HEADS:
                        turn_compressed(h + 1)
                    if u >= 1:
                        values(u - 1)
                values(U - 1)

                def cross(j):
                    pe.wait_ge(to_pe.sem, to_pe.seen_by("pe"))
                    w = (NT - 1 - j) * P
                    for h in range(GH):
                        key = (l, "cross", j, h)
                        if claim(key, 4 + (j * GH + h) % 3):
                            pe.wait_ge(*room(key))
                        r = slice(GDK * h, GDK * h + GDK)
                        nc.tensor.matmul(PS[:, uses[key][0], 0:w], factors[j][r, 3 * P:4 * P], factors[j][r, 0:w],
                                         start=True, stop=True, tile_position=(GDK * h, 0))\
                            .then_inc(filling(key)[0], 1)

                def out_products(m, ks):
                    key = (l, "out", m)
                    if ks[0] == 0:
                        if claim(key, 7 if m == 0 else (m - 1) % 4):
                            pe.wait_ge(*room(key))
                    for k in ks:
                        ins = product(PS[:, uses[key][0], :], a_hi[:, k, :], a_lo[:, k, :], k == 0, k == KT - 1)
                    if ks[-1] == KT - 1:
                        ins.then_inc(filling(key)[0], 1)

                early, late = range(KT - 2), range(KT - 2, KT)
                for lv in (7, 0, 1, 2, 3, 4, 5, 6):
                    pe.wait_ge(to_pe.sem, to_pe.seen_by("pe"))
                    if lv < 7:
                        for i in range(NT):
                            key = (l, "lv", lv, i)
                            if claim(key, i):
                                pe.wait_ge(*room(key))
                            nc.tensor.matmul(PS[:, i, 0:S // 2], work[:, 6 + lv % 2, i * P:(i + 1) * P],
                                             spread[lv % 2][:, i, :, :].rearrange("p h c -> p (h c)"), start=True, stop=True)\
                                .then_inc(filling(key)[0], 1)
                    else:
                        for h in range(GH):
                            key, b = (l, "lv", lv, h), (4, 5, 7, 6)[h]
                            if claim(key, b):
                                pe.wait_ge(*room(key))
                            r = slice(GDK * h, GDK * h + GDK)
                            for i in range(NT):
                                ins = nc.tensor.matmul(PS[:, b, i * P:(i + 1) * P], proj[r, T["gk"], i * P:(i + 1) * P],
                                                       proj[r, T["gq"], i * P:(i + 1) * P], start=True, stop=True,
                                                       tile_position=(GDK * h, 0))
                            ins.then_inc(filling(key)[0], 1)
                    if lv in (1, 3, 5):
                        cross(lv // 2)
                    if lv == 4:
                        pe.wait_ge(h_lo.sem, h_lo.seen_by("pe", KT - 2))
                        out_products(0, early)
                for h in range(GH):
                    pe.wait_ge(*emptying((l, "cross", NT - 2, h)))
                    pe.wait_ge(*emptying((l, "lv", 6, h)))
                for t in range(2):
                    key = (l, "og", t)
                    if claim(key, 4 + t):
                        pe.wait_ge(*room(key))
                    for hh in range(2):
                        h = 2 * t + hh
                        v = proj[:, T["gv0"] + t, :].rearrange("p (n c) -> p n c", c=P)
                        rows = slice(HD * hh, HD * hh + HD)
                        for j in range(NT):
                            vj = v[:, j, hh * HD:(hh + 1) * HD]
                            if j < NT - 1:
                                off = [0, 384, 640][j]
                                w = (NT - 1 - j) * P
                                nc.tensor.matmul(PS[rows, 4 + t, (j + 1) * P:S], vj,
                                                 Ax[:, h, off:off + w], start=j == 0, stop=False)
                            ins = nc.tensor.matmul(PS[rows, 4 + t, j * P:(j + 1) * P], vj,
                                                   Ad[:, h, j, :], start=False, stop=j == NT - 1)
                    ins.then_inc(filling(key)[0], 1)
                out_products(1, early[:2])
                for t in range(2):
                    pe.wait_ge(squares_g.sem, squares_g.seen_by("pe"))
                    b = (6, 3)[t]
                    if claim((l, "hn", t), b):
                        pe.wait_ge(*room((l, "hn", t)))
                    nc.tensor.matmul(PS[:, b, :], c_("headones"), sq[:, t, :], start=True, stop=True)\
                        .then_inc(filling((l, "hn", t))[0], 1)
                out_products(1, early[2:])
                out_products(2, early)
                out_products(3, early)

                pe.wait_ge(h_lo.sem, h_lo.seen_by("pe", 2))
                for m in range(KT):
                    out_products(m, late if m < OUT_EARLY else range(KT))

                for c in range(FCH):
                    for f in range(FT):
                        gemm((l, "g", c, f), f % 2, a_hi, a_lo, fresh=0 if c == 0 and f == 0 else None)
                        if c == 0 and f == 0:
                            stats((l, "ss2"))
                        gemm((l, "u", c, f), 2 + f % 2, a_hi, a_lo)
                    for m in range(KT):
                        gemm((l, "d", c, m), 4 + m % 3, f_hi, f_lo, n=FT, fresh=0 if m == 0 else None)

            stats(("n1",), 0)
            stats(("n2",), 1)
            for m in range(KT):
                gemm(("xa", m), m % 4, a_hi, a_lo, fresh=0 if m == 0 else None)
            gb = 0

            def turn_values(p, half):
                if claim(("vT", p, half), 7):
                    pe.wait_ge(*room(("vT", p, half)))
                for n in range(4):
                    i, c = 2 * half + n // 2, n % 2
                    k0 = LOW[i] * ROWS + c * P
                    ins = nc.tensor.transpose(PS[:, 7, n * P:(n + 1) * P], qkv[:, p % 2, 2, k0:k0 + P], ident)
                ins.then_inc(filling(("vT", p, half))[0], 1)

            def near_scores(h):
                p, p0 = h // 2, HD * (h % 2)
                for half in range(2):
                    if claim(("S2", h, half), 2 + half):
                        pe.wait_ge(*room(("S2", h, half)))
                    for n in range(2):
                        i = 2 * half + n
                        ins = nc.tensor.matmul(PS[:, 2 + half, n * 256:(n + 1) * 256],
                                               qkv[p0:p0 + HD, p % 2, 0, i * P:(i + 1) * P],
                                               qkv[p0:p0 + HD, p % 2, 1, LOW[i] * ROWS:(LOW[i] + KC) * ROWS],
                                               start=True, stop=True)
                    ins.then_inc(filling(("S2", h, half))[0], 1)

            def near_turn(h):
                pe.wait_ge(scaled.sem, scaled.seen_by("pe"))
                for half in range(2):
                    if claim(("PT2", h, half), 4 + half):
                        pe.wait_ge(*room(("PT2", h, half)))
                    for n in range(4):
                        i, c = 2 * half + n // 2, n % 2
                        ins = nc.tensor.transpose(PS[:, 4 + half, n * P:(n + 1) * P], P2[:, i, c * P:(c + 1) * P], ident)
                    ins.then_inc(filling(("PT2", h, half))[0], 1)

            def near_values(h):
                p, p0 = h // 2, HD * (h % 2)
                if h % 2 == 0:
                    if claim(("O2", p), 6):
                        pe.wait_ge(*room(("O2", p)))
                    for half in range(2):
                        pe.wait_ge(*emptying(("vT", p, half)))
                for half in range(2):
                    pe.wait_ge(*emptying(("PT2", h, half)))
                    for n in range(4):
                        i, c = 2 * half + n // 2, n % 2
                        ins = nc.tensor.matmul(PS[p0:p0 + HD, 6, i * P:(i + 1) * P], vW[:, 2 * i + c, p0:p0 + HD],
                                               PT2[:, i, c * P:(c + 1) * P], start=c == 0, stop=c == 1)
                if h % 2 == 0:
                    ins.then_inc(pv_done.sem, 1)
                    pv_done.raised()
                else:
                    ins.then_inc(filling(("O2", p))[0], 1)

            for t in range(KT + 1):
                p = t - 1
                for place_, part in enumerate(("q", "k", "v", "z", "za")):
                    if t < KT:
                        gemm((part, t), gb % 2, a_hi, a_lo)
                        gb += 1
                    elif place_ < AHEAD:
                        gemm(("gate", place_), gb % 2, a_hi, a_lo)
                        gb += 1
                    if p >= 0 and part == "q":
                        pe.wait_ge(*emptying(("q", p)))
                        pe.wait_ge(*emptying(("k", p)))
                        pe.wait_ge(*emptying(("v", p)))
                        turn_values(p, 0)
                        near_scores(2 * p)
                    elif p >= 0 and part == "k":
                        turn_values(p, 1)
                        near_scores(2 * p + 1)
                    elif p >= 0 and part == "v":
                        near_turn(2 * p)
                    elif p >= 0 and part == "z":
                        near_values(2 * p)
                        near_turn(2 * p + 1)
                    elif p >= 0:
                        near_values(2 * p + 1)
                if t < KT:
                    pe.wait_ge(rgw_in, 16 * (t + 1))
                    if t == 0:
                        pe.wait_ge(to_pe.sem, to_pe.seen_by("pe"))
                    for m in range(4):
                        if claim(("rg", t, m), (7, 4, 5, 2)[m]):
                            pe.wait_ge(*room(("rg", t, m)))
                        ins = nc.tensor.matmul(PS[:, uses[("rg", t, m)][0], :], rgw[:, m, :], xc[:, t, :],
                                               start=True, stop=True)
                        ins.then_inc(filling(("rg", t, m))[0], 1)
            for n in range(2 * KT):
                gemm(("prod", n), 2 + n % 2, y_hi, y_lo, fresh=0 if n % KT == 0 else None)
                if n + AHEAD < 2 * KT:
                    gemm(("gate", n + AHEAD), gb % 2, a_hi, a_lo)
                    gb += 1
            for m in range(KT):
                gemm(("wo", m), m % 4, a_hi, a_lo, fresh=0 if m == 0 else None)
            stats(("n3",))

        def pv_finished(eng, l, u):
            if u % (2 * NT) == 2 * NT - 1:
                eng.wait_ge(*filling((l, "O", u // (2 * NT))))
            else:
                pair, v = divmod(u, 2 * NT)
                eng.wait_ge(pv_done.sem, (l * HEADS // 2 + pair) * (2 * NT - 1) + v + 1)

        A_ID = ACT.Identity
        PV_FIRST = DEPTH * HEADS // 2 * (2 * NT - 1)

        def by_row(ap):
            return ap.rearrange("p (r c) -> p r c", c=GRID)

        def by_column(ap):
            return ap.rearrange("p (c r) -> p r c", r=ROWS)

        BIAS_DMAS = 2 * QC

        def load_bias(eng, t, dmas):
            for n in dmas:
                hh, c = divmod(n, QC)
                first = RPB_PAD + (2 * t + hh) * 15 * 31 - c - 1
                src = bass.AP(a_rpb.tensor, first, [[31, ROWS], [31, ROWS], [1, RW]])
                eng.dma_start(bias[c * ROWS:(c + 1) * ROWS, 2 * (t % 2) + hh, :, :], src)\
                   .then_inc(bias_in[t % 2], 16)

        GDK_SCALE = GDK ** -0.5
        OFF = [0, 384, 640]

        @block.scalar
        def _(act):
            A = nc.scalar.activation

            def zero(ap):
                ones = c_("ones")[:, 0:1].unsqueeze(2).to_broadcast([P, 4, S])
                return A(ap, ones, ACT.Copy, scale=0.0)

            def inverse_rms(key, n, dst=None, src=None):
                act.wait_ge(*filling(key))
                d = rstd[:, :] if dst is None else dst
                A(d, PS[:, 7, :] if src is None else src, ACT.Ln, scale=1.0 / n, bias=epst[:, 0:1])\
                    .then_inc(emptied(key), 1)
                act.wait_ge(*emptying(key))

            def square(k):
                if k >= 2 and k != 3:
                    act.wait_ge(sq_used.sem, sq_used.seen_by("act"))
                A(sq[:, k % 2, :], x[:, k, :], ACT.Square).then_inc(squares.sem, 1)
                act.wait_ge(squares.sem, squares.raised())
                if k == KT - 1:
                    act.wait_ge(sq_used.sem, sq_used.seen_by("act"))

            act.dma_start(vec[:, :], a_vec).then_inc(vec_in, 16)
            act.dma_start(const[:, 0:HEAD], a_const[:, 0:HEAD]).then_inc(head_in, 16)
            for k in range(1, KT, 2):
                act.dma_start(x[:, k, :], a_x[:, k, :]).then_inc(x_in[k], 16)
            act.wait_ge(vec_in, 16)
            act.wait_ge(eps_ok.sem, eps_ok.seen_by("act"))

            for l in range(DEPTH):
                gain = v_("g_attn")[:, l * KT:(l + 1) * KT]
                for k in range(KT):
                    if l == 0:
                        act.wait_ge(x_in[k], 16)
                    else:
                        act.wait_ge(*emptying((l - 1, "d", FCH - 1, k)))
                    A(a_hi[:, k, :], x[:, k, :], ACT.Copy, scale=gain[:, k:k + 1]).then_inc(h_hi.sem, 1)
                    act.wait_ge(h_hi.sem, h_hi.raised())
                    square(k)
                inverse_rms((l, "ss"), D)
                A(rstd[:, :], rstd[:, :], ACT.Exp, scale=-0.5).then_inc(rstd_ok.sem, 1)
                act.wait_ge(rstd_ok.sem, rstd_ok.raised())
                act.wait_ge(misc_in, 16 * (l + 1))
                if l == 0:
                    A(lam_z[:, :], v_("lam"), ACT.Abs).then_inc(act_chain.sem, 1)
                    act.wait_ge(act_chain.sem, act_chain.raised())
                    A(lam_z[:, :], lam_z[:, :], ACT.Exp, scale=-1.0).then_inc(to_dve.sem, 1)
                    act.wait_ge(to_dve.sem, to_dve.raised())
                act.dma_start(cmp_w, a_cmp[4 * l]).then_inc(cmp_in, 16)

                def further(name):
                    t = T.get(name)
                    if name in ("vsl", "vwn"):
                        act.wait_ge(*filling((l, name, "T")))
                        A(proj[:, t, :], PS[:, uses[(l, name, "T")][0], :], ACT.Copy)\
                            .then_inc(emptied((l, name, "T")), 1)
                        act.wait_ge(*emptying((l, name, "T")))
                    elif name == "gate":
                        act.wait_ge(*filling((l, name, "T")))
                        A(gN[:, :, :], PS[:, uses[(l, name, "T")][0], 0:NT * 24].rearrange("p (n c) -> p n c", c=24), ACT.Sigmoid)\
                            .then_inc(emptied((l, name, "T")), 1)
                        act.wait_ge(*emptying((l, name, "T")))
                    elif name == "CV1":
                        act.wait_ge(*filling((l, "vc2")))
                        A(vcn[0:NC, :], PS[0:NC, uses[(l, "vc2")][0], 0:GROUPS * HD], ACT.Copy)\
                            .then_inc(emptied((l, "vc2")), 1)
                        act.wait_ge(*emptying((l, "vc2")))

                for idx, name in enumerate(ORDER):
                    if name[0] == "C":
                        values_, m = int(name[1] == "V"), int(name[2])
                        act.wait_ge(*filling((l, name)))
                        n = 2 * values_ + m + 1
                        if n < 4:
                            act.dma_start(cmp_w, a_cmp[4 * l + n]).then_inc(cmp_in, 16)
                        A(hid[:, values_, m, :], PS[:, uses[(l, name)][0], 0:2 * NC], ACT.Gelu_apprx_tanh)\
                            .then_inc(emptied((l, name)), 1)
                        act.wait_ge(*emptying((l, name)))
                    if idx >= LAG:
                        further(ORDER[idx - LAG])
                for name in ORDER[-LAG:]:
                    further(name)

                U = HEADS * NT

                def exps(u):
                    i, par = u % NT, u % 2
                    w = (i + 1) * P
                    act.wait_ge(max_ok.sem, max_ok.seen_by("act"))
                    for br in range(2):
                        A(work[:, 2 * par + br, 0:w], PS[:, 2 * par + br, 0:w], ACT.Exp,
                                       bias=nmax[:, par, br:br + 1], accum_out=sums[:, par, br:br + 1])\
                            .then_inc(emptied((l, "S", br, u)), 1)
                        act.wait_ge(*emptying((l, "S", br, u)))

                def compressed_exps(h):
                    act.wait_ge(maxc_ok.sem, maxc_ok.seen_by("act"))
                    for i in range(NT):
                        ins = A(Pc[:, h % 2, i, 0:NC], PS[:, 7, i * 32:i * 32 + NC], ACT.Exp,
                                bias=nmaxc[:, h % 2, i:i + 1], accum_out=sumsc[:, h % 2, i:i + 1])
                        if i < NT - 1:
                            ins.then_inc(act_chain.sem, 1)
                            act.wait_ge(act_chain.sem, act_chain.raised())
                        else:
                            ins.then_inc(emptied((l, "Sc", h)), 1)
                            act.wait_ge(*emptying((l, "Sc", h)))

                compressed_exps(0)
                exps(0)
                exps(1)
                for u in range(U):
                    i, par = u % NT, u % 2
                    if u >= 2:
                        pv_finished(act, l, u - 2)
                    act.wait_ge(*filling((l, "PT", 0, u)))
                    A(work[:, 4 + 2 * par, 0:(i + 1) * P], PS[:, 4, 0:(i + 1) * P], ACT.Copy)\
                        .then_inc(emptied((l, "PT", 0, u)), 1)
                    act.wait_ge(*emptying((l, "PT", 0, u)))
                    if u + 2 < U:
                        exps(u + 2)
                    if i == 0 and u // NT + 1 < HEADS:
                        compressed_exps(u // NT + 1)
                    if i in (1, 2) and u // NT * 2 + i - 1 < len(BESIDE):
                        name, step = BESIDE[u // NT * 2 + i - 1]
                        if step:
                            act.wait_ge(*filling((l, name, step)))
                            A(proj[:, T[name], :], PS[:, 7, :], ACT.Gelu_apprx_tanh if name[0] == "s" else ACT.Copy)\
                                .then_inc(emptied((l, name, step)), 1)
                            act.wait_ge(*emptying((l, name, step)))
                    if u == 13:
                        act.wait_ge(to_act.sem, to_act.seen_by("act"))
                        A(small[:, 48:52], small[:, 33:40:2], ACT.Ln, bias=epst[:, 0:1]).then_inc(act_chain.sem, 1)
                        act.wait_ge(act_chain.sem, act_chain.raised())
                        A(small[:, 48:52], small[:, 48:52], ACT.Exp, scale=-0.5).then_inc(to_dve.sem, 1)
                        act.wait_ge(to_dve.sem, to_dve.raised())
                    if u in (16, 27):
                        for t in range(2):
                            name = ("su" if u == 16 else "gr") + str(t)
                            act.wait_ge(*emptying((l, name)))
                            A(proj[:, T[name], :], proj[:, T[name], :], ACT.Gelu_apprx_tanh if u == 16 else ACT.Silu)\
                                .then_inc(to_dve.sem, 1)
                            act.wait_ge(to_dve.sem, to_dve.raised())
                    if u == U - NT:
                        act.wait_ge(to_act.sem, to_act.seen_by("act"))
                        A(tmp[:, :], rstd[:, :], ACT.Abs).then_inc(act_chain.sem, 1)
                        act.wait_ge(act_chain.sem, act_chain.raised())
                        A(tmp[:, :], tmp[:, :], ACT.Exp, scale=-1.0).then_inc(act_chain.sem, 1)
                        act.wait_ge(act_chain.sem, act_chain.raised())
                        A(tmp[:, :], tmp[:, :], ACT.Ln, bias=1.0).then_inc(to_dve.sem, 1)
                        act.wait_ge(to_dve.sem, to_dve.raised())
                    if u % 8 == 0 and u:
                        t = u // 8 - 1
                        act.wait_ge(*filling((l, "O", t)))
                        A(proj[:, t, :], PS[:, 6, :], ACT.Copy).then_inc(emptied((l, "O", t)), 1)
                        act.wait_ge(*emptying((l, "O", t)))
                    if u == U - 2:
                        zero(keys[:, :, :, :].rearrange("p a g c -> p (a g) c")).then_inc(act_chain.sem, 1)
                        act.wait_ge(act_chain.sem, act_chain.raised())
                    if u >= U - NT + 1:
                        act.wait_ge(*filling((l, "gr1")))
                        A(a_hi[:, i - 1, :], proj[:, i - 1, :], ACT.Copy).then_inc(h_hi.sem, 1)
                        act.wait_ge(h_hi.sem, h_hi.raised())
                B = rstd[:, :]
                act.wait_ge(to_act.sem, to_act.seen_by("act", 3))
                for lv in range(7):
                    act.wait_ge(to_act.sem, to_act.seen_by("act"))
                    e = work[:, 2 + lv % 2, :]
                    A(e, e, ACT.Abs).then_inc(act_chain.sem, 1)
                    act.wait_ge(act_chain.sem, act_chain.raised())
                    A(e, e, ACT.Exp, scale=-1.0 / TAU).then_inc(to_dve.sem, 1)
                    act.wait_ge(to_dve.sem, to_dve.raised())
                    if lv == 0:
                        act.wait_ge(*filling((l, "O", HEADS // 2 - 1)))
                        A(a_hi[:, HEADS // 2 - 1, :], PS[:, 6, :], ACT.Copy).then_inc(h_hi.sem, 1)
                        act.wait_ge(h_hi.sem, h_hi.raised())

                        for t in range(2):
                            A(a_hi[:, 4 + t, :], proj[:, T["su0"] + t, :], ACT.Copy).then_inc(h_hi.sem, 1)
                            act.wait_ge(h_hi.sem, h_hi.raised())
                        zero(proj[:, 0:4, :]).then_inc(to_dve.sem, 1)
                        act.wait_ge(to_dve.sem, to_dve.raised())
                    if lv in (1, 3, 5):
                        j = lv // 2
                        w = (NT - 1 - j) * P
                        A(factors[j][:, 0:w], B[:, (j + 1) * P:S], ACT.Exp, scale=1.0 / TAU, bias=small[:, j:j + 1])\
                            .then_inc(act_chain.sem, 1)
                        act.wait_ge(act_chain.sem, act_chain.raised())
                        A(factors[j][:, 3 * P:4 * P], B[:, j * P:(j + 1) * P], ACT.Exp,
                          scale=-1.0 / TAU, bias=small[:, 4 + j:5 + j]).then_inc(to_dve.sem, 1)
                        act.wait_ge(to_dve.sem, to_dve.raised())
                    elif lv:
                        j = lv // 2 - 1
                        w = (NT - 1 - j) * P
                        for h in range(GH):
                            act.wait_ge(*filling((l, "cross", j, h)))
                            A(Ax[:, h, OFF[j]:OFF[j] + w], PS[:, uses[(l, "cross", j, h)][0], 0:w], ACT.Copy)\
                                .then_inc(emptied((l, "cross", j, h)), 1)
                            act.wait_ge(*emptying((l, "cross", j, h)))
                for t in range(2):
                    act.wait_ge(*filling((l, "og", t)))
                    A(sq[:, t, :], PS[:, 4 + t, :], ACT.Square).then_inc(squares_g.sem, 1)
                    act.wait_ge(squares_g.sem, squares_g.raised())
                act.dma_start(csil, a_c).then_inc(c_in, 16)
                for t in range(2):
                    act.wait_ge(*filling((l, "hn", t)))
                    A(work[:, 2 + t, :], PS[:, (6, 3)[t], :], ACT.Ln, scale=1.0 / GDV, bias=epst[:, 0:1])\
                        .then_inc(emptied((l, "hn", t)), 1)
                    act.wait_ge(*emptying((l, "hn", t)))
                for t in range(2):
                    A(work[:, 2 + t, :], work[:, 2 + t, :], ACT.Exp, scale=-0.5).then_inc(to_dve.sem, 1)
                    act.wait_ge(to_dve.sem, to_dve.raised())
                for t in range(2):
                    act.wait_ge(to_act.sem, to_act.seen_by("act"))
                    A(a_hi[:, 6 + t, :], work[:, 4 + t, :], ACT.Copy).then_inc(h_hi.sem, 1)
                    act.wait_ge(h_hi.sem, h_hi.raised())

                for k in range(KT - 1):
                    act.wait_ge(*emptying((l, "out", k)))
                    square(k)
                act.wait_ge(*filling((l, "out", KT - 1)))
                gain = m_("g_ffn")
                for k in range(KT):
                    if k == KT - 1:
                        act.wait_ge(*emptying((l, "out", k)))
                        square(k)
                    A(a_hi[:, k, :], x[:, k, :], ACT.Copy, scale=gain[:, k:k + 1]).then_inc(h_hi.sem, 1)
                    act.wait_ge(h_hi.sem, h_hi.raised())
                inverse_rms((l, "ss2"), D)
                A(rstd[:, :], rstd[:, :], ACT.Exp, scale=-0.5).then_inc(rstd_ok.sem, 1)
                act.wait_ge(rstd_ok.sem, rstd_ok.raised())
                if l + 1 < DEPTH:
                    act.wait_ge(misc_free.sem, misc_free.seen_by("act"))
                    act.dma_start(misc[:, :], a_misc[l + 1]).then_inc(misc_in, 16)
                for c in range(FCH):
                    for f in range(FT + 1):
                        if f < FT:
                            act.wait_ge(to_act.sem, to_act.seen_by("act"))
                            if c == 0 and f == MOD_FROM - 1:
                                act.wait_ge(c_in, 16 * (l + 1))
                                A(csil, csil, ACT.Silu).then_inc(c_ready.sem, 1)
                                act.wait_ge(c_ready.sem, c_ready.raised())
                            if MOD_FROM <= f < MOD_FROM + MOD_EACH:
                                m = mod_tile(l, c, f)
                                if m:
                                    act.wait_ge(mod_used.sem, m)
                                act.dma_start(mod_w, a_mod[m]).then_inc(mod_in, 16)
                            A(work[:, f % 2, :], work[:, f % 2, :], ACT.Silu).then_inc(to_dve.sem, 1)
                            act.wait_ge(to_dve.sem, to_dve.raised())
                        if f > 0:
                            act.wait_ge(to_act.sem, to_act.seen_by("act"))
                            A(f_hi[:, f - 1, :], work[:, 4 + (f - 1) % 2, :], ACT.Copy).then_inc(h_hi.sem, 1)
                            act.wait_ge(h_hi.sem, h_hi.raised())

            for k in range(KT):
                act.wait_ge(*emptying((DEPTH - 1, "d", FCH - 1, k)))
                square(k)
                A(work[:, k % 2, :], x[:, k, :], ACT.Square, scale=v_("g_fin1")[:, k:k + 1]).then_inc(squares.sem, 1)
                act.wait_ge(squares.sem, squares.raised())
            inverse_rms(("n1",), D)
            A(rstd[:, :], rstd[:, :], ACT.Exp, scale=-0.5).then_inc(rstd_ok.sem, 1)
            act.wait_ge(rstd_ok.sem, rstd_ok.raised())
            act.wait_ge(to_act.sem, to_act.seen_by("act"))
            A(tmp[:, :], tmp[:, :], ACT.Ln, scale=1.0 / D, bias=epst[:, 0:1]).then_inc(act_chain.sem, 1)
            act.wait_ge(act_chain.sem, act_chain.raised())
            A(tmp[:, :], tmp[:, :], ACT.Exp, scale=-0.5).then_inc(to_dve.sem, 1)
            act.wait_ge(to_dve.sem, to_dve.raised())
            act.dma_start(rgw[:, :, :], a_rgw[0]).then_inc(rgw_in, 16)
            for k in range(KT):
                act.wait_ge(to_act.sem, to_act.seen_by("act"))
                A(a_hi[:, k, :], xc[:, k, :], A_ID, bias=modv[:, k:k + 1]).then_inc(h_hi.sem, 1)
                act.wait_ge(h_hi.sem, h_hi.raised())

            def near_exps(h):
                act.wait_ge(max_ok.sem, max_ok.seen_by("act"))
                if h:
                    for half in range(2):
                        act.wait_ge(*filling(("PT2", h - 1, half)))
                for i in range(4):
                    ins = A(P2[:, i, :], PS[:, 2 + i // 2, i % 2 * 256:(i % 2 + 1) * 256], ACT.Exp,
                            bias=sm2[:, i:i + 1], accum_out=sm2[:, 4 + i:5 + i])
                    if i % 2:
                        ins.then_inc(emptied(("S2", h, i // 2)), 1)
                        act.wait_ge(*emptying(("S2", h, i // 2)))
                    else:
                        ins.then_inc(act_chain.sem, 1)
                        act.wait_ge(act_chain.sem, act_chain.raised())

            def near_turned(h):
                if h % 2:
                    act.wait_ge(pv_done.sem, PV_FIRST + h // 2 + 1)
                act.wait_ge(*filling(("PT2", h, 0)))
                A(PT2[:, 0:2, :], PS[:, 4, :].rearrange("p (n c) -> p n c", c=256), ACT.Copy)\
                    .then_inc(emptied(("PT2", h, 0)), 1)
                act.wait_ge(*emptying(("PT2", h, 0)))

            def merging_gate(n):
                if n >= 4:
                    act.wait_ge(*emptying(("prod", n - 4)))
                act.wait_ge(*filling(("gate", n)))
                A(gate_tile(n), PS[:, uses[("gate", n)][0], :], ACT.Sigmoid).then_inc(emptied(("gate", n)), 1)
                act.wait_ge(*emptying(("gate", n)))

            for t in range(KT + 1):
                p = t - 1
                if p >= 0:
                    if p:
                        act.wait_ge(*filling(("O2", p - 1)))
                    act.wait_ge(*filling(("vT", p, 0)))
                    A(vW[:, 0:4, :], PS[:, 7, :].rearrange("p (n c) -> p n c", c=P), ACT.Copy)\
                        .then_inc(emptied(("vT", p, 0)), 1)
                    act.wait_ge(*emptying(("vT", p, 0)))
                    near_exps(2 * p)
                if t < KT:
                    for part, name in ((1, "k"), (2, "v")):
                        act.wait_ge(*filling((name, t)))
                        A(by_column(qkv[:, t % 2, part, :]), by_row(PS[:, uses[(name, t)][0], :]), ACT.Copy)\
                            .then_inc(emptied((name, t)), 1)
                        act.wait_ge(*emptying((name, t)))
                else:
                    act.wait_ge(*emptying(("O2", p - 1)))
                    for n in range(2):
                        merging_gate(n)
                if p >= 0:
                    near_turned(2 * p)
                    near_exps(2 * p + 1)
                    for d in range(2):
                        act.wait_ge(to_act.sem, to_act.seen_by("act"))
                        A(rg[:, 4 + d, :], rg[:, 4 + d, :], ACT.Sqrt, scale=2.0).then_inc(to_dve.sem, 1)
                        act.wait_ge(to_dve.sem, to_dve.raised())
                if t < KT:
                    if t >= 2:
                        act.wait_ge(*emptying(("O2", t - 2)))
                    act.wait_ge(*filling(("z", t)))
                    A(zs[:, t % 2, :], PS[:, uses[("z", t)][0], :], ACT.Silu)\
                        .then_inc(emptied(("z", t)), 1)
                    act.wait_ge(*emptying(("z", t)))
                if p >= 0:
                    near_turned(2 * p + 1)
                    act.wait_ge(to_act.sem, to_act.seen_by("act"))
                    A(y_hi[:, p, :], tmp[:, :], ACT.Copy).then_inc(h_hi.sem, 1)
                    act.wait_ge(h_hi.sem, h_hi.raised())
                if t < KT:
                    act.wait_ge(*filling(("za", t)))
                    A(sq[:, t % 2, :], PS[:, uses[("za", t)][0], :], ACT.Silu)\
                        .then_inc(emptied(("za", t)), 1)
                    act.wait_ge(*emptying(("za", t)))
                    for m in range(4):
                        col = VEC["b_gate"][0] + m * KT + t
                        act.wait_ge(*filling(("rg", t, m)))
                        A(rg[:, m, :], PS[:, uses[("rg", t, m)][0], :], ACT.Sigmoid, bias=vec[:, col:col + 1])\
                            .then_inc(emptied(("rg", t, m)), 1)
                        act.wait_ge(*emptying(("rg", t, m)))
                    if t + 1 < KT:
                        act.dma_start(rgw[:, :, :], a_rgw[t + 1]).then_inc(rgw_in, 16)
                    for d in range(2):
                        lc = d * KT + t
                        A(rg[:, 4 + d, :], rg[:, 2 * d, :], ACT.Tanh, scale=lam_p[:, lc:lc + 1])\
                            .then_inc(act_chain.sem, 1)
                        act.wait_ge(act_chain.sem, act_chain.raised())
                    for d in range(2):
                        lc = d * KT + t
                        A(rg[:, 2 * d, :], rg[:, 2 * d, :], ACT.Exp, scale=lam_n[:, lc:lc + 1])\
                            .then_inc(to_dve.sem, 1)
                        act.wait_ge(to_dve.sem, to_dve.raised())
            act.wait_ge(*emptying(("O2", KT - 1)))
            for n in range(2, 2 * KT):
                merging_gate(n)
                if n == KT + AHEAD - 2:
                    act.wait_ge(*filling(("prod", KT - 1)))
                    for k in range(KT):
                        A(y_hi[:, k, :], xc[:, k, :], ACT.Copy).then_inc(h_hi.sem, 1)
                        act.wait_ge(h_hi.sem, h_hi.raised())
            for m in range(KT):
                act.wait_ge(to_act.sem, to_act.seen_by("act"))
                A(a_hi[:, m, :], merged[:, m, :], ACT.Copy).then_inc(h_hi.sem, 1)
                act.wait_ge(h_hi.sem, h_hi.raised())
            for k in range(KT):
                act.wait_ge(*emptying(("wo", k)))
                square(k)
            inverse_rms(("n3",), D)
            A(rstd[:, :], rstd[:, :], ACT.Exp, scale=-0.5).then_inc(rstd_ok.sem, 1)
            act.wait_ge(rstd_ok.sem, rstd_ok.raised())

        @block.vector
        def _(dve):
            V = nc.vector
            TT, TS, STT, CP = V.tensor_tensor, V.tensor_scalar, V.scalar_tensor_tensor, V.tensor_copy

            V.memset(epst[:, :], EPS).then_inc(eps_ok.sem, 1)
            dve.wait_ge(eps_ok.sem, eps_ok.raised())
            dve.wait_ge(vec_in, 16)

            def windows(r, b, h):
                ap = PS[r, b, h:h + 1].unsqueeze(2).to_broadcast([HD, 16, NC])
                return bass.AP(ap.tensor, ap.offset, [list(ap.ap[0]), [2, 16], [CMP_STRIDE, NC]])

            def add_squares(k):
                dve.wait_ge(squares.sem, squares.seen_by("dve"))
                if k:
                    ins = TT(sums2[0], sq[:, 0, :] if k == 1 else sums2[0], sq[:, k % 2, :], ALU.add)
                    if k == KT - 1:
                        ins.then_inc(sum_ok.sem, 1)
                        dve.wait_ge(sum_ok.sem, sum_ok.raised())
                    else:
                        ins.then_inc(sq_used.sem, 1)
                        dve.wait_ge(sq_used.sem, sq_used.raised())

            def add_twin_squares(k):
                for which in range(2):
                    dve.wait_ge(squares.sem, squares.seen_by("dve"))
                    first, second = (sq[:, 0, :], sq[:, 1, :]) if which == 0 else (work[:, 0, :], work[:, 1, :])
                    if k:
                        ins = TT(sums2[which], first if k == 1 else sums2[which], second if k % 2 else first, ALU.add)
                        if k == KT - 1:
                            ins.then_inc(sum_ok.sem, 1)
                            dve.wait_ge(sum_ok.sem, sum_ok.raised())
                        elif which:
                            ins.then_inc(sq_used.sem, 1)
                            dve.wait_ge(sq_used.sem, sq_used.raised())
                        else:
                            ins.then_inc(dve_chain.sem, 1)
                            dve.wait_ge(dve_chain.sem, dve_chain.raised())

            def low_normed(k, gain):
                dve.wait_ge(h_hi.sem, h_hi.seen_by("dve"))
                STT(a_lo[:, k, :], x[:, k, :], gain[:, k:k + 1], a_hi[:, k, :].bitcast(F32),
                    ALU.mult, ALU.subtract).then_inc(h_lo.sem, 1)
                dve.wait_ge(h_lo.sem, h_lo.raised())

            for l in range(DEPTH):
                if l == 0:
                    for k in range(KT):
                        low_normed(k, v_("g_attn"))
                        add_squares(k)
                dve.wait_ge(rstd_ok.sem, rstd_ok.seen_by("dve"))
                dve.wait_ge(const_in, 16)
                dve.wait_ge(misc_in, 16 * (l + 1))

                def further(name):
                    t = T.get(name)
                    if name in ("kc", "vc"):
                        pos = m_("pos_k" if name == "kc" else "pos_v")
                        for g in range(GROUPS):
                            key = (l, name, "dup", g)
                            dve.wait_ge(*filling(key))
                            b = uses[key][0]
                            for h in range(2):
                                r = slice(HD * h, HD * h + HD)
                                src = windows(r, b, h)
                                ins = TT(X[int(name == "vc")][r, :, g * NC:(g + 1) * NC], src,
                                         pos[r, :].unsqueeze(2).to_broadcast([HD, 16, NC]), ALU.add)
                                if h == 0:
                                    ins.then_inc(dve_chain.sem, 1)
                                    dve.wait_ge(dve_chain.sem, dve_chain.raised())
                                else:
                                    ins.then_inc(emptied(key), 1)
                                    dve.wait_ge(*emptying(key))
                    elif name in ("ksl", "kwn"):
                        for g in range(GROUPS):
                            kd, kr = (l, name, "dup", g), (l, name, "rot", g)
                            dst = keys[:, int(name == "kwn"), g, :]
                            dve.wait_ge(*filling(kd))
                            TT(dst, PS[:, uses[kd][0], :], c_("cos"), ALU.mult).then_inc(emptied(kd), 1)
                            dve.wait_ge(*emptying(kd))
                            dve.wait_ge(*filling(kr))
                            TT(tmp[:, :], PS[:, uses[kr][0], :], c_("sin"), ALU.mult).then_inc(emptied(kr), 1)
                            dve.wait_ge(*emptying(kr))
                            TT(dst, dst, tmp[:, :], ALU.add).then_inc(roped.sem, 1)
                            dve.wait_ge(roped.sem, roped.raised())
                    elif name[0] == "q":
                        key = (l, name, "rot")
                        dve.wait_ge(*filling(key))
                        q = proj[:, t, :]
                        STT(tmp[:, :], PS[:, uses[key][0], :], HD ** -0.5, c_("sin"), ALU.mult, ALU.mult)\
                            .then_inc(emptied(key), 1)
                        dve.wait_ge(*emptying(key))
                        STT(q, q, HD ** -0.5, c_("cos"), ALU.mult, ALU.mult).then_inc(dve_chain.sem, 1)
                        dve.wait_ge(dve_chain.sem, dve_chain.raised())
                        TT(q, q, tmp[:, :], ALU.add).then_inc(roped.sem, 1)
                        dve.wait_ge(roped.sem, roped.raised())
                    elif name == "gate":
                        dve.wait_ge(*emptying((l, "gate", "T")))
                        g = gN[:, 0, 2:24:3]
                        TS(g, g, c_("rowok"), None, ALU.mult).then_inc(dve_chain.sem, 1)
                        dve.wait_ge(dve_chain.sem, dve_chain.raised())
                    elif name == "CK1":
                        dve.wait_ge(*filling((l, "kc2")))
                        CP(kc0[:, :], PS[:, uses[(l, "kc2")][0], 0:2 * NC]).then_inc(emptied((l, "kc2")), 1)
                        dve.wait_ge(*emptying((l, "kc2")))
                        dve.wait_ge(*filling((l, "kc2rot")))
                        TT(kcr[:, :], PS[:, uses[(l, "kc2rot")][0], 0:2 * NC], c_("sinc"), ALU.mult)\
                            .then_inc(emptied((l, "kc2rot")), 1)
                        dve.wait_ge(*emptying((l, "kc2rot")))
                        TT(tmp[:, 0:2 * NC], kc0[:, :], c_("cosc"), ALU.mult).then_inc(dve_chain.sem, 1)
                        dve.wait_ge(dve_chain.sem, dve_chain.raised())
                        TT(kcr[:, :], kcr[:, :], tmp[:, 0:2 * NC], ALU.add).then_inc(roped.sem, 1)
                        dve.wait_ge(roped.sem, roped.raised())

                for idx, name in enumerate(ORDER):
                    if name[0] != "C":
                        dve.wait_ge(*filling((l, name)))
                        TT(proj[:, T[name], :], PS[:, uses[(l, name)][0], :], rstd[:, :], ALU.mult)\
                            .then_inc(emptied((l, name)), 1)
                        dve.wait_ge(*emptying((l, name)))
                    if idx >= LAG:
                        further(ORDER[idx - LAG])
                for name in ORDER[-LAG:]:
                    further(name)

                U = HEADS * NT
                cm = c_("cmask").rearrange("p (n c) -> p n c", c=NC)

                def maxima(u):
                    i, par = u % NT, u % 2
                    w = (i + 1) * P
                    for br in range(2):
                        dve.wait_ge(*filling((l, "S", br, u)))
                    s2 = PS[:, 2 * par:2 * par + 2, :]
                    TT(s2[:, :, i * P:w], s2[:, :, i * P:w], c_("causal").unsqueeze(1).to_broadcast([P, 2, P]), ALU.add)\
                        .then_inc(dve_chain.sem, 1)
                    dve.wait_ge(dve_chain.sem, dve_chain.raised())
                    V.tensor_reduce(nmax[:, par, 0:2], s2[:, :, 0:w], AX.X, ALU.max, negate=True)\
                        .then_inc(max_ok.sem, 1)
                    dve.wait_ge(max_ok.sem, max_ok.raised())

                def compressed_maxima(h):
                    dve.wait_ge(*filling((l, "Sc", h)))
                    sc = PS[:, 7, 0:NT * 32].rearrange("p (n c) -> p n c", c=32)[:, :, 0:NC]
                    TT(sc, sc, cm, ALU.add).then_inc(dve_chain.sem, 1)
                    dve.wait_ge(dve_chain.sem, dve_chain.raised())
                    V.tensor_reduce(nmaxc[:, h % 2, :], sc, AX.X, ALU.max, negate=True).then_inc(maxc_ok.sem, 1)
                    dve.wait_ge(maxc_ok.sem, maxc_ok.raised())

                def scale_compressed(h):
                    dve.wait_ge(*emptying((l, "Sc", h)))
                    V.reciprocal(r3[:, 0:NT], sumsc[:, h % 2, :]).then_inc(dve_chain.sem, 1)
                    dve.wait_ge(dve_chain.sem, dve_chain.raised())
                    TT(r3[:, 0:NT], r3[:, 0:NT], gN[:, :, h * BR + 2], ALU.mult).then_inc(dve_chain.sem, 1)
                    dve.wait_ge(dve_chain.sem, dve_chain.raised())
                    pc = Pc[:, h % 2, :, 0:NC]
                    TT(pc, pc, r3[:, 0:NT].unsqueeze(2).to_broadcast([P, NT, NC]), ALU.mult).then_inc(scaledc.sem, 1)
                    dve.wait_ge(scaledc.sem, scaledc.raised())

                def compressed_turned(h):
                    dve.wait_ge(*filling((l, "PTc", h)))
                    CP(PTc[0:NC, h % 2, :], PS[0:NC, 7, :]).then_inc(emptied((l, "PTc", h)), 1)
                    dve.wait_ge(*emptying((l, "PTc", h)))

                def scale(u):
                    h, i, par = u // NT, u % NT, u % 2
                    for br in range(2):
                        dve.wait_ge(*emptying((l, "S", br, u)))
                    V.reciprocal(r3[:, 0:2], sums[:, par, 0:2]).then_inc(dve_chain.sem, 1)
                    dve.wait_ge(dve_chain.sem, dve_chain.raised())
                    TT(r3[:, 0:2], r3[:, 0:2], gN[:, i, h * BR:h * BR + 2], ALU.mult).then_inc(dve_chain.sem, 1)
                    dve.wait_ge(dve_chain.sem, dve_chain.raised())
                    w = (i + 1) * P
                    pr = work[:, 2 * par:2 * par + 2, 0:w]
                    TT(pr, pr, r3[:, 0:2].unsqueeze(2).to_broadcast([P, 2, w]), ALU.mult).then_inc(scaled.sem, 1)
                    dve.wait_ge(scaled.sem, scaled.raised())

                if l == 0:
                    dve.wait_ge(to_dve.sem, to_dve.seen_by("dve"))
                B = rstd[:, :]
                sv = proj[:, T["sv0"]:T["sv0"] + 2, :].rearrange("p t (n c) -> p t n c", c=P)

                def gating_norm(u):
                    if u == 12:
                        dve.wait_ge(*emptying((l, "sv1", "T")))
                        for n in range(NT):
                            V.bn_stats(small[:, 8 + 6 * n:14 + 6 * n], sv[:, :, n, :]).then_inc(dve_chain.sem, 1)
                            dve.wait_ge(dve_chain.sem, dve_chain.raised())
                        for n in range(NT):
                            ins = V.bn_aggr(small[:, 32 + 2 * n:34 + 2 * n], small[:, 8 + 6 * n:14 + 6 * n])
                            if n < NT - 1:
                                ins.then_inc(dve_chain.sem, 1)
                                dve.wait_ge(dve_chain.sem, dve_chain.raised())
                            else:
                                ins.then_inc(to_act.sem, 1)
                                dve.wait_ge(to_act.sem, to_act.raised())
                    elif u == 14:
                        dve.wait_ge(to_dve.sem, to_dve.seen_by("dve"))
                        for n in range(NT):
                            TS(sv[:, :, n, :], sv[:, :, n, :], small[:, 32 + 2 * n:33 + 2 * n], small[:, 48 + n:49 + n],
                               ALU.subtract, ALU.mult).then_inc(dve_chain.sem, 1)
                            dve.wait_ge(dve_chain.sem, dve_chain.raised())
                    elif u in (16, 17):
                        name, op = (("lng", ALU.mult), ("lnb", ALU.add))[u - 16]
                        tab = m_(name).rearrange("p (t c) -> p t c", c=P).unsqueeze(2).to_broadcast([P, 2, NT, P])
                        TT(sv, sv, tab, op).then_inc(dve_chain.sem, 1)
                        dve.wait_ge(dve_chain.sem, dve_chain.raised())
                    elif u == 18:
                        sw = m_("swt").rearrange("p (g c) -> p g c", c=P)
                        TT(sw, sw, c_("triu").unsqueeze(1).to_broadcast([P, 4, P]), ALU.mult).then_inc(to_pe.sem, 1)
                        dve.wait_ge(to_pe.sem, to_pe.raised())
                    elif u == 19:
                        dve.wait_ge(to_dve.sem, to_dve.seen_by("dve", 2))

                def before(name, bank):
                    dve.wait_ge(*filling((l, name)))
                    TT(proj[:, T[name], :], PS[:, bank, :], rstd[:, :], ALU.mult).then_inc(emptied((l, name)), 1)
                    dve.wait_ge(*emptying((l, name)))

                before(*BEFORE[0])
                compressed_maxima(0)
                maxima(0)
                maxima(1)
                scale_compressed(0)
                compressed_turned(0)
                scale(0)
                before(*BEFORE[1])
                for u in range(U):
                    i, par = u % NT, u % 2
                    if u >= 2:
                        pv_finished(dve, l, u - 2)
                    dve.wait_ge(*filling((l, "PT", 1, u)))
                    CP(work[:, 5 + 2 * par, 0:(i + 1) * P], PS[:, 5, 0:(i + 1) * P])\
                        .then_inc(emptied((l, "PT", 1, u)), 1)
                    dve.wait_ge(*emptying((l, "PT", 1, u)))
                    if u + 1 < U:
                        scale(u + 1)
                    if u + 2 < U:
                        maxima(u + 2)
                    h = u // NT
                    if i == 0 and h + 1 < HEADS:
                        compressed_maxima(h + 1)
                    if i == 1 and h + 1 < HEADS:
                        scale_compressed(h + 1)
                    if i in (1, 2) and 2 * h + i - 1 < len(BESIDE):
                        name, step = BESIDE[2 * h + i - 1]
                        if not step:
                            dve.wait_ge(*filling((l, name)))
                            TT(proj[:, T[name], :], PS[:, 7, :], rstd[:, :], ALU.mult).then_inc(emptied((l, name)), 1)
                            dve.wait_ge(*emptying((l, name)))
                    if 12 <= u < 20:
                        gating_norm(u)
                    if u == U - NT:
                        dve.wait_ge(to_dve.sem, to_dve.seen_by("dve", 2))
                        dve.wait_ge(*filling((l, "z")))
                        TS(B, PS[:, 7, :], m_("b_up"), None, ALU.add).then_inc(emptied((l, "z")), 1)
                        dve.wait_ge(*emptying((l, "z")))
                        CP(small[:, 62:63], epst[:, :]).then_inc(to_act.sem, 1)
                        dve.wait_ge(to_act.sem, to_act.raised())
                    if u == U - NT + 1:
                        dve.wait_ge(to_dve.sem, to_dve.seen_by("dve"))
                        STT(tmp[:, :], B, 0.0, tmp[:, :], ALU.min, ALU.subtract).then_inc(dve_chain.sem, 1)
                        dve.wait_ge(dve_chain.sem, dve_chain.raised())
                        V.tensor_tensor_scan(B, c_("ones")[:, 0:1].to_broadcast([P, S]), tmp[:, :], 0.0, ALU.mult, ALU.add)\
                            .then_inc(dve_chain.sem, 1)
                        dve.wait_ge(dve_chain.sem, dve_chain.raised())
                    if U - NT + 1 <= u < U - 1:
                        t = u - (U - NT + 1)
                        key = (l, "sg", t)
                        dve.wait_ge(*filling(key))
                        TT(sq[:, t, :].rearrange("p (n c) -> p n c", c=P), PS[:, 7, :].rearrange("p (n c) -> p n c", c=P),
                           m_("sgb")[:, t * P:(t + 1) * P].unsqueeze(1).to_broadcast([P, NT, P]), ALU.add)\
                            .then_inc(emptied(key), 1)
                        dve.wait_ge(*emptying(key))
                        TT(proj[:, T["su0"] + t, :], proj[:, T["su0"] + t, :], sq[:, t, :], ALU.mult).then_inc(to_act.sem, 1)
                        dve.wait_ge(to_act.sem, to_act.raised())
                    if i == 3 and h + 1 < HEADS:
                        compressed_turned(h + 1)
                    if u == U - 2:
                        TS(proj[:, T["gq"], :], proj[:, T["gq"], :], GDK_SCALE, None, ALU.mult).then_inc(to_pe.sem, 1)
                        dve.wait_ge(to_pe.sem, to_pe.raised())
                    if u >= U - NT + 1:
                        dve.wait_ge(h_hi.sem, h_hi.seen_by("dve"))
                        TT(a_lo[:, i - 1, :], proj[:, i - 1, :], a_hi[:, i - 1, :].bitcast(F32), ALU.subtract)\
                            .then_inc(h_lo.sem, 1)
                        dve.wait_ge(h_lo.sem, h_lo.raised())
                gq, gk = proj[:, T["gq"], :], proj[:, T["gk"], :]

                def distances(lv):
                    s = 64 >> lv
                    bb = B.rearrange("p (n c) -> p n c", c=2 * s)
                    out = work[:, 2 + lv % 2, :].rearrange("p (n c) -> p n c", c=2 * s)
                    n = S // (2 * s)
                    TT(out, bb, bb[:, :, s - 1:s].to_broadcast([P, n, 2 * s]), ALU.subtract).then_inc(to_act.sem, 1)
                    dve.wait_ge(to_act.sem, to_act.raised())

                def later_halves(ap, half):
                    return ap.rearrange("p (n b c) -> p n b c", n=NT, c=2 * half)[:, :, :, half:2 * half]

                def gather(lv):
                    for n in range(4):
                        dve.wait_ge(*filling((l, "lv", lv, n)))
                        if lv < 7:
                            half = 64 >> lv
                            dst = Ad[:, :, n, :].rearrange("p h (b c) -> p h b c", c=2 * half)[:, :, :, half:2 * half]
                            mask = c_("levels")[:, lv * P // 2:(lv + 1) * P // 2].bitcast(U32)\
                                .rearrange("p (b c) -> p b c", c=half).unsqueeze(1)\
                                .to_broadcast([P, GH, P // (2 * half), half])
                            src = PS[:, n, 0:S // 2].rearrange("p (h b c) -> p h b c", h=GH, c=half)
                        else:
                            b = uses[(l, "lv", 7, n)][0]
                            dst, src = Ad[:, n, :, :], PS[:, b, :].rearrange("p (n c) -> p n c", c=P)
                            mask = ident.bitcast(U32).unsqueeze(1).to_broadcast([P, NT, P])
                        V.copy_predicated(dst, mask, src).then_inc(emptied((l, "lv", lv, n)), 1)
                        dve.wait_ge(*emptying((l, "lv", lv, n)))

                TS(small[:, 0:4], B[:, P - 1:S:P], -1.0 / TAU, None, ALU.mult).then_inc(dve_chain.sem, 1)
                dve.wait_ge(dve_chain.sem, dve_chain.raised())
                TS(small[:, 4:8], B[:, P - 1:S:P], 1.0 / TAU, None, ALU.mult).then_inc(to_act.sem, 1)
                dve.wait_ge(to_act.sem, to_act.raised())
                distances(0)
                t = HEADS // 2 - 1
                dve.wait_ge(h_hi.sem, h_hi.seen_by("dve"))
                TT(tmp[:, :], PS[:, 6, :], a_hi[:, t, :].bitcast(F32), ALU.subtract)\
                    .then_inc(emptied((l, "O", t)), 1)
                dve.wait_ge(*emptying((l, "O", t)))
                CP(a_lo[:, t, :], tmp[:, :]).then_inc(h_lo.sem, 1)
                dve.wait_ge(h_lo.sem, h_lo.raised())

                for t in range(2):
                    dve.wait_ge(h_hi.sem, h_hi.seen_by("dve"))
                    TT(a_lo[:, 4 + t, :], proj[:, T["su0"] + t, :], a_hi[:, 4 + t, :].bitcast(F32), ALU.subtract)\
                        .then_inc(h_lo.sem, 1)
                    dve.wait_ge(h_lo.sem, h_lo.raised())
                for lv in range(7):
                    if lv + 1 < 7:
                        distances(lv + 1)
                    kd, e = work[:, 6 + lv % 2, :], work[:, 2 + lv % 2, :]
                    dve.wait_ge(to_dve.sem, to_dve.seen_by("dve"))
                    half = 64 >> lv
                    for h in range(GH):
                        r = slice(GDK * h, GDK * h + GDK)
                        own = spread[lv % 2][r, :, h, :].rearrange("p n (b c) -> p n b c", c=half)
                        TT(own, later_halves(gq[r, :], half), later_halves(e[r, :], half), ALU.mult)\
                            .then_inc(dve_chain.sem, 1)
                        dve.wait_ge(dve_chain.sem, dve_chain.raised())
                    TT(kd, gk, e, ALU.mult).then_inc(to_pe.sem, 1)
                    dve.wait_ge(to_pe.sem, to_pe.raised())
                    if lv == 0:
                        dve.wait_ge(to_dve.sem, to_dve.seen_by("dve"))
                        gather(7)
                    if lv in (1, 3, 5):
                        j = lv // 2
                        w = (NT - 1 - j) * P
                        fq, fk = factors[j][:, 0:w], factors[j][:, 3 * P:4 * P]
                        dve.wait_ge(to_dve.sem, to_dve.seen_by("dve"))
                        TT(fq, gq[:, (j + 1) * P:S], fq, ALU.mult).then_inc(dve_chain.sem, 1)
                        dve.wait_ge(dve_chain.sem, dve_chain.raised())
                        TT(fk, gk[:, j * P:(j + 1) * P], fk, ALU.mult).then_inc(to_pe.sem, 1)
                        dve.wait_ge(to_pe.sem, to_pe.raised())
                    if lv >= 1:
                        gather(lv - 1)
                gather(6)
                dve.wait_ge(to_dve.sem, to_dve.seen_by("dve", 2))
                for t in range(2):
                    key = (l, "og", t)
                    dve.wait_ge(*filling(key))
                    STT(work[:, 4 + t, :], PS[:, 4 + t, :], m_("gnorm"), work[:, 2 + t, :], ALU.mult, ALU.mult)\
                        .then_inc(emptied(key), 1)
                    dve.wait_ge(*emptying(key))
                for t in range(2):
                    TT(work[:, 4 + t, :], work[:, 4 + t, :], proj[:, T["gr0"] + t, :], ALU.mult)\
                        .then_inc(to_act.sem, 1)
                    dve.wait_ge(to_act.sem, to_act.raised())
                for t in range(2):
                    dve.wait_ge(h_hi.sem, h_hi.seen_by("dve"))
                    TT(a_lo[:, 6 + t, :], work[:, 4 + t, :], a_hi[:, 6 + t, :].bitcast(F32), ALU.subtract)\
                        .then_inc(h_lo.sem, 1)
                    dve.wait_ge(h_lo.sem, h_lo.raised())

                for m in range(KT):
                    key = (l, "out", m)
                    dve.wait_ge(*filling(key))
                    TT(x[:, m, :], PS[:, uses[key][0], :], x[:, m, :], ALU.add).then_inc(emptied(key), 1)
                    dve.wait_ge(*emptying(key))
                    if m:
                        add_squares(m - 1)

                for k in range(KT):
                    if k == KT - 1:
                        add_squares(k)
                    low_normed(k, m_("g_ffn"))
                dve.wait_ge(rstd_ok.sem, rstd_ok.seen_by("dve"))
                if l + 1 < DEPTH:
                    CP(small[:, 61:62], epst[:, :]).then_inc(misc_free.sem, 1)
                    dve.wait_ge(misc_free.sem, misc_free.raised())
                for c in range(FCH):
                    for f in range(FT + 1):
                        if f < FT:
                            for kind, b0, w0 in (("g", 0, 0), ("u", 2, 2)):
                                key = (l, kind, c, f)
                                dve.wait_ge(*filling(key))
                                TT(work[:, w0 + f % 2, :], PS[:, b0 + f % 2, :], rstd[:, :], ALU.mult)\
                                    .then_inc(emptied(key), 1)
                                dve.wait_ge(*emptying(key))
                                if kind == "g":
                                    CP(small[:, 60:61], epst[:, :]).then_inc(to_act.sem, 1)
                                    dve.wait_ge(to_act.sem, to_act.raised())
                        if f > 0:
                            k = f - 1
                            dve.wait_ge(to_dve.sem, to_dve.seen_by("dve"))
                            TT(work[:, 4 + k % 2, :], work[:, k % 2, :], work[:, 2 + k % 2, :], ALU.mult)\
                                .then_inc(to_act.sem, 1)
                            dve.wait_ge(to_act.sem, to_act.raised())
                            dve.wait_ge(h_hi.sem, h_hi.seen_by("dve"))
                            TT(f_lo[:, k, :], work[:, 4 + k % 2, :], f_hi[:, k, :].bitcast(F32), ALU.subtract)\
                                .then_inc(h_lo.sem, 1)
                            dve.wait_ge(h_lo.sem, h_lo.raised())
                        if MOD_FROM <= f < MOD_FROM + MOD_EACH:
                            m = mod_tile(l, c, f)
                            dve.wait_ge(c_ready.sem, l + 1)
                            dve.wait_ge(mod_in, 16 * (m + 1))
                            TT(mod_w, mod_w, csil, ALU.mult).then_inc(dve_chain.sem, 1)
                            dve.wait_ge(dve_chain.sem, dve_chain.raised())
                            V.tensor_reduce(modv[:, m:m + 1], mod_w, AX.X, ALU.add).then_inc(mod_used.sem, 1)
                            dve.wait_ge(mod_used.sem, mod_used.raised())
                    if l == 0 and c == 0:
                        TS(lam_s[:, :], lam_z[:, :], 2.0, None, ALU.add).then_inc(dve_chain.sem, 1)
                        dve.wait_ge(dve_chain.sem, dve_chain.raised())
                        V.reciprocal(lam_s[:, :], lam_s[:, :]).then_inc(dve_chain.sem, 1)
                        dve.wait_ge(dve_chain.sem, dve_chain.raised())
                        TT(lam_s[:, :], lam_s[:, :], lam_z[:, :], ALU.mult).then_inc(dve_chain.sem, 1)
                        dve.wait_ge(dve_chain.sem, dve_chain.raised())
                        TT(lam_q[:, :], lam_s[:, :], lam_s[:, :], ALU.mult).then_inc(dve_chain.sem, 1)
                        dve.wait_ge(dve_chain.sem, dve_chain.raised())
                        TS(lam_p[:, :], lam_q[:, :], 1.0 / 15, 1.0 / 13, ALU.mult, ALU.add).then_inc(dve_chain.sem, 1)
                        dve.wait_ge(dve_chain.sem, dve_chain.raised())
                        for k in (11, 9, 7, 5, 3, 1):
                            TT(lam_p[:, :], lam_p[:, :], lam_q[:, :], ALU.mult).then_inc(dve_chain.sem, 1)
                            dve.wait_ge(dve_chain.sem, dve_chain.raised())
                            TS(lam_p[:, :], lam_p[:, :], 1.0 / k, None, ALU.add).then_inc(dve_chain.sem, 1)
                            dve.wait_ge(dve_chain.sem, dve_chain.raised())
                        TT(lam_p[:, :], lam_p[:, :], lam_s[:, :], ALU.mult).then_inc(dve_chain.sem, 1)
                        dve.wait_ge(dve_chain.sem, dve_chain.raised())
                        TS(lam_n[:, :], v_("lam"), -1.0, 0.0, ALU.mult, ALU.max).then_inc(dve_chain.sem, 1)
                        dve.wait_ge(dve_chain.sem, dve_chain.raised())
                        STT(lam_p[:, :], lam_p[:, :], 2.0, lam_n[:, :], ALU.mult, ALU.add).then_inc(dve_chain.sem, 1)
                        dve.wait_ge(dve_chain.sem, dve_chain.raised())
                        TS(lam_p[:, :], lam_p[:, :], RG_C, None, ALU.mult).then_inc(dve_chain.sem, 1)
                        dve.wait_ge(dve_chain.sem, dve_chain.raised())
                        TS(lam_n[:, :], lam_p[:, :], -1.0, None, ALU.mult).then_inc(dve_chain.sem, 1)
                        dve.wait_ge(dve_chain.sem, dve_chain.raised())
                    last = c == FCH - 1
                    gain = v_("g_attn")[:, (l + 1) % DEPTH * KT:]
                    for m in range(KT):
                        key = (l, "d", c, m)
                        dve.wait_ge(*filling(key))
                        TT(x[:, m, :], PS[:, uses[key][0], :], x[:, m, :], ALU.add).then_inc(emptied(key), 1)
                        dve.wait_ge(*emptying(key))
                        if last and l + 1 < DEPTH:
                            if m:
                                low_normed(m - 1, gain)
                                add_squares(m - 1)
                            if m == KT - 1:
                                low_normed(m, gain)
                                add_squares(m)
                        elif last and m:
                            for k in (m - 1, m) if m == KT - 1 else (m - 1,):
                                add_twin_squares(k)

            TT(modv[:, :], modv[:, :], v_("b_c"), ALU.add).then_inc(dve_chain.sem, 1)
            dve.wait_ge(dve_chain.sem, dve_chain.raised())
            STT(gainm[:, :], modv[:, KT:2 * KT], 1.0, v_("g_pre"), ALU.add, ALU.mult).then_inc(dve_chain.sem, 1)
            dve.wait_ge(dve_chain.sem, dve_chain.raised())
            TT(gainm[:, :], gainm[:, :], v_("g_fin1"), ALU.mult).then_inc(dve_chain.sem, 1)
            dve.wait_ge(dve_chain.sem, dve_chain.raised())
            dve.wait_ge(rstd_ok.sem, rstd_ok.seen_by("dve"))
            dve.wait_ge(*filling(("n2",)))
            TT(tmp[:, :], PS[:, 0, :], rstd[:, :], ALU.mult).then_inc(emptied(("n2",)), 1)
            dve.wait_ge(*emptying(("n2",)))
            TT(tmp[:, :], tmp[:, :], rstd[:, :], ALU.mult).then_inc(to_act.sem, 1)
            dve.wait_ge(to_act.sem, to_act.raised())
            dve.wait_ge(to_dve.sem, to_dve.seen_by("dve"))
            TT(tmp[:, :], tmp[:, :], rstd[:, :], ALU.mult).then_inc(dve_chain.sem, 1)
            dve.wait_ge(dve_chain.sem, dve_chain.raised())
            for k in range(KT + 1):
                if k < KT:
                    STT(xc[:, k, :], x[:, k, :], gainm[:, k:k + 1], tmp[:, :], ALU.mult, ALU.mult)\
                        .then_inc(to_act.sem, 1)
                    dve.wait_ge(to_act.sem, to_act.raised())
                if k:
                    j = k - 1
                    dve.wait_ge(h_hi.sem, h_hi.seen_by("dve"))
                    STT(a_lo[:, j, :], xc[:, j, :], modv[:, j:j + 1], a_hi[:, j, :].bitcast(F32),
                        ALU.add, ALU.subtract).then_inc(h_lo.sem, 1)
                    dve.wait_ge(h_lo.sem, h_lo.raised())
            for k in range(KT):
                STT(x[:, k, :], x[:, k, :], v_("g_fin1")[:, k:k + 1], rstd[:, :], ALU.mult, ALU.mult)\
                    .then_inc(dve_chain.sem, 1)
                dve.wait_ge(dve_chain.sem, dve_chain.raised())
            V.memset(xpad[:, 0:2], 0.0).then_inc(dve_chain.sem, 1)
            dve.wait_ge(dve_chain.sem, dve_chain.raised())
            V.memset(xpad[:, S + 2:S + 3], 0.0).then_inc(dve_chain.sem, 1)
            dve.wait_ge(dve_chain.sem, dve_chain.raised())
            cw = v_("conv_w")
            for m in range(KT):
                dve.wait_ge(*filling(("xa", m)))
                CP(xpad[:, 2:S + 2], PS[:, m % 4, :]).then_inc(emptied(("xa", m)), 1)
                dve.wait_ge(*emptying(("xa", m)))
                TS(xc[:, m, :], xpad[:, 0:S], cw[:, m:m + 1], v_("conv_b")[:, m:m + 1], ALU.mult, ALU.add)\
                    .then_inc(dve_chain.sem, 1)
                dve.wait_ge(dve_chain.sem, dve_chain.raised())
                for j in range(1, 4):
                    ins = STT(xc[:, m, :], xpad[:, j:j + S], cw[:, j * KT + m:j * KT + m + 1], xc[:, m, :], ALU.mult, ALU.add)
                    if j == 3 and m == KT - 1:
                        ins.then_inc(to_pe.sem, 1)
                        dve.wait_ge(to_pe.sem, to_pe.raised())
                    else:
                        ins.then_inc(dve_chain.sem, 1)
                        dve.wait_ge(dve_chain.sem, dve_chain.raised())
            nm = c_("nmask").rearrange("p (n c) -> p n c", c=KC)

            def near_maxima(h):
                for half in range(2):
                    dve.wait_ge(*filling(("S2", h, half)))
                for i in range(4):
                    off = LOW[i] - QC * i + QC
                    s = PS[:, 2 + i // 2, i % 2 * 256:(i % 2 + 1) * 256].rearrange("p (c r) -> p r c", r=ROWS)
                    TT(s, s, bias[:, h % 4, ::-1, off:off + KC], ALU.add).then_inc(dve_chain.sem, 1)
                    dve.wait_ge(dve_chain.sem, dve_chain.raised())
                s4 = PS[:, 2:4, :].rearrange("p b (n c r) -> p (b n) c r", c=KC, r=ROWS)
                TT(s4, s4, nm.unsqueeze(3).to_broadcast([P, 4, KC, ROWS]), ALU.add).then_inc(dve_chain.sem, 1)
                dve.wait_ge(dve_chain.sem, dve_chain.raised())
                V.tensor_reduce(sm2[:, 0:4], PS[:, 2:4, :].rearrange("p b (n c) -> p (b n) c", c=256), AX.X, ALU.max,
                                negate=True).then_inc(max_ok.sem, 1)
                dve.wait_ge(max_ok.sem, max_ok.raised())

            def near_scale(h):
                for half in range(2):
                    dve.wait_ge(*emptying(("S2", h, half)))
                V.reciprocal(sm2[:, 8:12], sm2[:, 4:8]).then_inc(dve_chain.sem, 1)
                dve.wait_ge(dve_chain.sem, dve_chain.raised())
                TT(P2[:, :, :], P2[:, :, :], sm2[:, 8:12].unsqueeze(2).to_broadcast([P, 4, 256]), ALU.mult)\
                    .then_inc(scaled.sem, 1)
                dve.wait_ge(scaled.sem, scaled.raised())

            def near_turned(h):
                if h % 2:
                    dve.wait_ge(pv_done.sem, PV_FIRST + h // 2 + 1)
                dve.wait_ge(*filling(("PT2", h, 1)))
                CP(PT2[:, 2:4, :], PS[:, 5, :].rearrange("p (n c) -> p n c", c=256))\
                    .then_inc(emptied(("PT2", h, 1)), 1)
                dve.wait_ge(*emptying(("PT2", h, 1)))

            def decay_factor(d):
                e = rg[:, 4 + d, :]
                TS(tmp[:, :], e, 1.0, None, ALU.add).then_inc(dve_chain.sem, 1)
                dve.wait_ge(dve_chain.sem, dve_chain.raised())
                V.reciprocal(tmp[:, :], tmp[:, :]).then_inc(dve_chain.sem, 1)
                dve.wait_ge(dve_chain.sem, dve_chain.raised())
                TT(e, e, tmp[:, :], ALU.mult).then_inc(to_act.sem, 1)
                dve.wait_ge(to_act.sem, to_act.raised())

            def recurrence(p, d):
                a, i_, e = rg[:, 2 * d, :], rg[:, 2 * d + 1, :], rg[:, 4 + d, :]
                TT(i_, i_, xc[:, p, :], ALU.mult).then_inc(dve_chain.sem, 1)
                dve.wait_ge(dve_chain.sem, dve_chain.raised())
                dve.wait_ge(to_dve.sem, to_dve.seen_by("dve"))
                TT(i_, i_, e, ALU.mult).then_inc(dve_chain.sem, 1)
                dve.wait_ge(dve_chain.sem, dve_chain.raised())
                if d == 0:
                    V.tensor_tensor_scan(e, a, i_, 0.0, ALU.mult, ALU.add).then_inc(dve_chain.sem, 1)
                    dve.wait_ge(dve_chain.sem, dve_chain.raised())
                else:
                    V.tensor_tensor_scan(e[:, ::-1], a[:, ::-1], i_[:, ::-1], 0.0, ALU.mult, ALU.add)\
                        .then_inc(dve_chain.sem, 1)
                    dve.wait_ge(dve_chain.sem, dve_chain.raised())

            for t in range(KT + 1):
                p = t - 1
                if t < KT:
                    dve.wait_ge(*filling(("q", t)))
                    TS(by_column(qkv[:, t % 2, 0, :]), by_row(PS[:, uses[("q", t)][0], :]), HD ** -0.5, None, ALU.mult)\
                        .then_inc(emptied(("q", t)), 1)
                    dve.wait_ge(*emptying(("q", t)))
                if p >= 0:
                    dve.wait_ge(bias_in[p % 2], 16 * 2 * QC * (p // 2 + 1))
                    near_maxima(2 * p)
                    dve.wait_ge(*filling(("vT", p, 1)))
                    CP(vW[:, 4:8, :], PS[:, 7, :].rearrange("p (n c) -> p n c", c=P))\
                        .then_inc(emptied(("vT", p, 1)), 1)
                    dve.wait_ge(*emptying(("vT", p, 1)))
                    near_scale(2 * p)
                    near_maxima(2 * p + 1)
                    dve.wait_ge(to_dve.sem, to_dve.seen_by("dve", 2))
                    decay_factor(0)
                    near_turned(2 * p)
                    near_scale(2 * p + 1)
                    decay_factor(1)
                    recurrence(p, 0)
                    near_turned(2 * p + 1)
                    recurrence(p, 1)
                    TT(tmp[:, :], rg[:, 4, :], rg[:, 5, :], ALU.add).then_inc(dve_chain.sem, 1)
                    dve.wait_ge(dve_chain.sem, dve_chain.raised())
                    TT(tmp[:, :], tmp[:, :], sq[:, p % 2, :], ALU.mult).then_inc(to_act.sem, 1)
                    dve.wait_ge(to_act.sem, to_act.raised())
                    dve.wait_ge(*filling(("O2", p)))
                    dve.wait_ge(*emptying(("z", p)))
                    TT(by_row(xc[:, p, :]), by_column(PS[:, 6, :]), by_row(zs[:, p % 2, :]), ALU.mult)\
                        .then_inc(emptied(("O2", p)), 1)
                    dve.wait_ge(*emptying(("O2", p)))
                    dve.wait_ge(h_hi.sem, h_hi.seen_by("dve"))
                    TT(y_lo[:, p, :], tmp[:, :], y_hi[:, p, :].bitcast(F32), ALU.subtract)\
                        .then_inc(h_lo.sem, 1)
                    dve.wait_ge(h_lo.sem, h_lo.raised())

            def low_merged(m):
                dve.wait_ge(h_hi.sem, h_hi.seen_by("dve"))
                TT(a_lo[:, m, :], merged[:, m, :], a_hi[:, m, :].bitcast(F32), ALU.subtract)\
                    .then_inc(h_lo.sem, 1)
                dve.wait_ge(h_lo.sem, h_lo.raised())

            for n in range(2 * KT):
                dve.wait_ge(*emptying(("gate", n)))
                dve.wait_ge(*filling(("prod", n)))
                if n < KT:
                    TT(merged[:, n, :], PS[:, 2 + n % 2, :], gate_tile(n), ALU.mult).then_inc(emptied(("prod", n)), 1)
                    dve.wait_ge(*emptying(("prod", n)))
                else:
                    m = n - KT
                    TT(tmp[:, :], PS[:, 2 + n % 2, :], gate_tile(n), ALU.mult).then_inc(emptied(("prod", n)), 1)
                    dve.wait_ge(*emptying(("prod", n)))
                    TT(merged[:, m, :], merged[:, m, :], tmp[:, :], ALU.add).then_inc(to_act.sem, 1)
                    dve.wait_ge(to_act.sem, to_act.raised())
                if n == KT - 1:
                    for t in range(KT):
                        dve.wait_ge(h_hi.sem, h_hi.seen_by("dve"))
                        TT(y_lo[:, t, :], xc[:, t, :], y_hi[:, t, :].bitcast(F32), ALU.subtract)\
                            .then_inc(h_lo.sem, 1)
                        dve.wait_ge(h_lo.sem, h_lo.raised())
                if n == 2 * KT - AHEAD:
                    for m in range(KT - AHEAD):
                        low_merged(m)
                elif n > 2 * KT - AHEAD:
                    low_merged(n - KT - 1)
            low_merged(KT - 1)
            gate = modv[:, 2 * KT:3 * KT]
            for m in range(KT):
                key = ("wo", m)
                dve.wait_ge(*filling(key))
                STT(x[:, m, :], PS[:, m % 4, :], gate[:, m:m + 1], x[:, m, :], ALU.mult, ALU.add)\
                    .then_inc(emptied(key), 1)
                dve.wait_ge(*emptying(key))
                if m:
                    add_squares(m - 1)
            add_squares(KT - 1)
            dve.wait_ge(rstd_ok.sem, rstd_ok.seen_by("dve"))
            for k in range(KT):
                STT(xc[:, k, :], x[:, k, :], v_("g_fin2")[:, k:k + 1], rstd[:, :], ALU.mult, ALU.mult)\
                    .then_inc(out_ok.sem, 1)
                dve.wait_ge(out_ok.sem, out_ok.raised())

        @block.gpsimd
        def _(pool):
            G = nc.gpsimd

            def split(r, arrival, used, chain):
                pool.wait_ge(raw_in[r], arrival)
                if used is not None:
                    pool.wait_ge(slot_used, used)
                G.tensor_tensor(w_hi[:, r, :, :], raw[:, r, :, :], ones, ALU.mult).then_inc(pool_chain, 1)
                pool.wait_ge(pool_chain, chain)
                G.tensor_tensor(w_lo[:, r, :, :], raw[:, r, :, :], w_hi[:, r, :, :].bitcast(F32), ALU.subtract)\
                    .then_inc(split_done, 1)

            ones = c_("ones")[:, 0:1].unsqueeze(2).to_broadcast([P, 8, P])
            pool.wait_ge(head_in, 16)
            for r in range(RING):
                split(r, 16, None, r + 1)
            with pool.Fori(1, SLOTS // RING) as i:
                for r in range(RING):
                    split(r, i * 16 + 16, i * RING + (r - RING + 1), i * RING + (r + 1))
            last = SLOTS // RING
            for r in range(SLOTS % RING):
                split(r, 16 * (last + 1), last * RING + r - RING + 1, last * RING + r + 1)

        @block.sync
        def _(sp):
            for r in range(RING):
                sp.dma_start(x[:, 2 * r, :], a_x[:, 2 * r, :]).then_inc(x_in[2 * r], 16)
                sp.dma_start(raw[:, r, :, :], w_sl[r]).then_inc(raw_in[r], 16)
            sp.dma_start(misc[:, :], a_misc[0]).then_inc(misc_in, 16)
            sp.dma_start(const[:, HEAD:], a_const[:, HEAD:]).then_inc(const_in, 16)

            def weight_slots(first, last):
                with sp.Fori(first // RING, last // RING) as i:
                    for r in range(RING):
                        sp.wait_ge(split_done, i * RING + (r - RING + 1))
                        sp.dma_start(raw[:, r, :, :], w_rows[bass.ds((i * RING + r) * P, P), :]).then_inc(raw_in[r], 16)

            tile0 = PLAN.index(("in2", 2 * KT))
            PARTS = 5
            part_of = {}
            for t in range(KT):
                start = tile0 - 4 * PARTS + PARTS * t if t < 2 else tile0 + 5 * (t + 1) + 1
                for j in range(PARTS):
                    part_of[start + j] = (t, j)
            mixed = min(part_of) // RING * RING
            mixed_end = -(-(max(part_of) + 1) // RING) * RING
            weight_slots(RING, mixed)
            sp.wait_ge(rstd_ok.sem, 2 * DEPTH)
            for n in range(mixed, mixed_end):
                sp.wait_ge(split_done, n - RING + 1)
                sp.dma_start(raw[:, n % RING, :, :], w_sl[n]).then_inc(raw_in[n % RING], 16)
                if n in part_of:
                    t, j = part_of[n]
                    if j == 0 and t >= 2:
                        sp.wait_ge(max_ok.sem, DEPTH * HEADS * NT + 2 * (t - 1))
                    each = -(-BIAS_DMAS // PARTS)
                    load_bias(sp, t, range(j * each, min(BIAS_DMAS, (j + 1) * each)))
            last = SLOTS // RING * RING
            weight_slots(mixed_end, last)
            for r in range(SLOTS - last):
                sp.wait_ge(split_done, last + r - RING + 1)
                sp.dma_start(raw[:, r, :, :], w_sl[last + r]).then_inc(raw_in[r], 16)
            for k in range(KT):
                sp.wait_ge(out_ok.sem, k + 1)
                sp.dma_start(a_out[:, k, :], xc[:, k, :]).then_inc(out_done, 16)
            sp.wait_ge(out_done, 16 * KT)


def kernel(**inputs):
    import numpy as np
    import concourse.bacc as bacc
    from concourse.bass_utils import run_bass_kernel_spmd

    f32 = np.float32
    a = {k: np.asarray(v) for k, v in inputs.items()}

    const = np.zeros((P, CONST_N), f32)

    def put(name, v):
        const[:, CONST[name][0]:CONST[name][1]] = np.asarray(v, f32).reshape(P, -1)

    p = np.arange(P)
    tok = np.arange(S)
    inv = 1.0 / (10000.0 ** ((p % (HD // 2)).astype(f32) / (HD // 2)))
    put("ident", np.eye(P))
    put("ones", np.ones((P, P)))
    ang = inv[:, None].astype(f32) * tok[None, :].astype(f32)
    put("cos", np.cos(ang))
    put("sin", np.sin(ang))
    ends = np.tile(np.arange(NC) * CMP_STRIDE + CMP_LEN - 1, 2)
    angc = inv[:, None].astype(f32) * ends[None, :].astype(f32)
    put("cosc", np.cos(angc))
    put("sinc", np.sin(angc))
    NEG = -1e30
    put("causal", np.where(p[None, :] <= p[:, None], 0.0, NEG))
    t_of = p[:, None] + P * np.arange(NT)[None, :]
    put("cmask", np.where(ends[None, None, :NC] <= t_of[:, :, None], 0.0, NEG))
    put("rowok", (p >= CMP_LEN - 1).astype(f32))
    rot = np.zeros((P, P))
    for m in range(P):
        if m % HD < HD // 2:
            rot[m + HD // 2, m] = -1.0
        else:
            rot[m - HD // 2, m] = 1.0
    put("rot", rot)
    dup = np.zeros((P, GROUPS, P))
    for g in range(GROUPS):
        dup[g * HD + p % HD, g, p] = 1.0
    put("dup", dup)
    put("rotdup", np.stack([dup_g @ rot for dup_g in dup.transpose(1, 0, 2)], 1))
    put("headones", (p[:, None] // HD == p[None, :] // HD))
    put("triu", p[:, None] <= p[None, :])
    levels = np.zeros((P, 7, P // 2))
    for lv in range(7):
        half = 64 >> lv
        q = p.reshape(-1, 2 * half)[:, half:].reshape(-1)
        levels[:, lv, :] = (p[:, None] // (2 * half) == q[None, :] // (2 * half)) & (p[:, None] % (2 * half) < half)
    put("levels", levels)
    nmask = np.zeros((P, NT, KC))
    for i in range(NT):
        c = QC * i + p // ROWS
        c0 = np.clip(c - QC // 2, 0, GRID - QC)
        kc = LOW[i] + np.arange(KC)
        nmask[:, i, :] = np.where((kc[None, :] >= c0[:, None]) & (kc[None, :] < c0[:, None] + QC), 0.0, NEG)
    put("nmask", nmask)

    def vecs(v):
        return np.ascontiguousarray(v.reshape(-1, P).T)

    misc = np.zeros((DEPTH, P, MISC_N), f32)
    for l in range(DEPTH):
        def mput(name, v):
            misc[l, :, MISC[name][0]:MISC[name][1]] = v.reshape(P, -1)

        mput("g_ffn", vecs(a["ffn_norm"][l]))
        mput("pos_k", vecs(a["cmp_pos_k"][l].reshape(-1)))
        mput("pos_v", vecs(a["cmp_pos_v"][l].reshape(-1)))
        mput("b_up", a["gla_b_up"][l])
        mput("gnorm", np.tile(a["gla_norm"][l], 2))
        w2k = a["cmp_w2_k"][l].reshape(2, P, HD).transpose(1, 0, 2)
        mput("w2k", np.concatenate([w2k, w2k], 2))
        mput("w2v", a["cmp_w2_v"][l].reshape(2, P, HD).transpose(1, 0, 2))
        misc[l, 32:48, MISC["w_up"][0]:MISC["w_up"][1]] = a["gla_w_up"][l]
        mput("swt", a["sg_w"][l].transpose(2, 0, 1))
        mput("lng", np.broadcast_to(a["sg_ln_g"][l], (P, 2 * P)))
        mput("lnb", np.broadcast_to(a["sg_ln_b"][l], (P, 2 * P)))
        mput("sgb", np.repeat(a["sg_b"][l].reshape(2, 2, P), HD, 1).transpose(1, 0, 2))
    vec = np.zeros((P, VEC_N), f32)

    def vput(name, v):
        vec[:, VEC[name][0]:VEC[name][1]] = v.reshape(P, -1)

    vput("g_fin1", vecs(a["final_norm"]))
    vput("g_attn", np.concatenate([vecs(a["attn_norm"][l]) for l in range(DEPTH)], 1))
    vput("b_c", vecs(a["b_c_2"][0]))
    vput("g_pre", vecs(a["g_pre_2"][0]))
    vput("conv_w", vecs(a["conv_w_2"][0].reshape(-1)))
    vput("conv_b", vecs(a["conv_b_2"][0]))
    vput("b_gate", np.concatenate([vecs(a[k][0]) for k in ("b_r_f_2", "b_i_f_2", "b_r_b_2", "b_i_b_2")], 1))
    vput("lam", np.concatenate([vecs(a["lam_f_2"][0]), vecs(a["lam_b_2"][0])], 1))
    vput("g_fin2", vecs(a["g_final_2"]))
    rgw = np.zeros((KT, P, 4, P), f32)
    for m, k in enumerate(("w_r_f_2", "w_i_f_2", "w_r_b_2", "w_i_b_2")):
        w = a[k][0].reshape(KT, 2, HD, HD)
        for hh in range(2):
            rgw[:, HD * hh:HD * hh + HD, m, HD * hh:HD * hh + HD] = w[:, hh]
    rpb = np.zeros(RPB_LEN + 2 * RPB_PAD, f32)
    rpb[RPB_PAD:RPB_PAD + RPB_LEN] = a["rpb_2"][0][:, ::-1].reshape(-1)

    cols = {}
    at = 0
    for name, n in (("q", 512), ("kc", P), ("vc", P), ("ksl", P), ("vsl", P), ("kwn", P), ("vwn", P), ("gts", 24),
                    ("gq", P), ("gk", P), ("gv", 2 * P), ("ga", 16), ("gr", 2 * P), ("su", 2 * P), ("sv", 2 * P)):
        cols[name] = at
        at += n

    def tile(w, c):
        return w[:, c:c + P].reshape(-1, P, P).transpose(1, 0, 2)

    stream = []
    for item in stream_plan():
        kind = item[0]
        if kind == "in":
            w, name = a["w_in"][item[1]], item[2]
            if name == "gate":
                g = w[:, cols["gts"]:cols["gts"] + 24].reshape(D, HEADS, BR)[:, :, [1, 2, 0]].reshape(D, 24)
                wide = np.zeros((D, P), f32)
                wide[:, 0:24] = g
                wide[:, 32:48] = w[:, cols["ga"]:cols["ga"] + 16]
                stream.append(tile(wide, 0))
            else:
                base = name if name in cols else name[:-1]
                n = 0 if name in cols else int(name[-1])
                stream.append(tile(w, cols[base] + n * P))
        elif kind == "out":
            w = a["w_out"][item[1]]
            rows = [(OUT_ROWS[k] * P, m * P) for m, k in OUT_TILES[8 * item[2]:8 * item[2] + 8]]
            stream.append(np.stack([w[r:r + P, c:c + P] for r, c in rows], 1))
        elif kind in ("gate", "up"):
            stream.append(tile(a["w_gate" if kind == "gate" else "w_up"][item[1]], item[2] * P))
        elif kind == "down":
            l, c, i = item[1:]
            w = a["w_down"][l][c * FT * P:(c + 1) * FT * P].reshape(FT, P, KT, P).transpose(2, 0, 1, 3)
            stream.append(w.reshape(KT * FT, P, P)[8 * i:8 * i + 8].transpose(1, 0, 2))
        elif kind == "in2":
            stream.append(tile(a["w_in_2"][0], item[1] * P))
        else:
            w = a[{"pa": "w_pa_2", "pb": "w_pb_2", "wo": "w_o_2"}[kind]][0]
            stream.append(tile(w, item[1] * P))
    stream = np.stack(stream).reshape(-1, P, 8 * P)
    cmp_w = np.stack([a[k][l][:, m * P:(m + 1) * P].reshape(CMP_K, P, P).transpose(1, 0, 2)
                      for l in range(DEPTH) for k in ("cmp_w1_k", "cmp_w1_v") for m in range(2)])
    mod_w = a["w_c_2"][0].T.reshape(MOD_SLOTS, P, D)
    c_rows = np.broadcast_to(a["c_2"][0].reshape(1, D), (P, D))

    arrays = {
        "x_t": np.ascontiguousarray(a["x"][0].T.reshape(KT, P, S).transpose(1, 0, 2)),
        "weights": stream, "cmp_w": cmp_w, "mod_w": np.ascontiguousarray(mod_w),
        "c_rows": np.ascontiguousarray(c_rows), "const": const, "misc": misc, "vec": vec, "rgw": rgw, "rpb": rpb,
    }
    nc = bacc.Bacc("TRN2", target_bir_lowering=False, num_devices=1)
    F32 = mybir.dt.float32
    args = [nc.dram_tensor(k, v.shape, F32, kind="ExternalInput").ap() for k, v in arrays.items()]
    out = nc.dram_tensor("out", (P, KT, S), F32, kind="ExternalOutput").ap()
    build(nc, *args, out)
    r = run_bass_kernel_spmd(nc, [arrays], core_ids=[0])
    y = np.asarray(r.results[0]["out"])
    return np.ascontiguousarray(y.transpose(1, 0, 2).reshape(D, S).T).reshape(1, S, D)
```
